# Optimizing a Trainium2 kernel written in Bass

```python
import math
import jax, jax.numpy as jnp
from jax import lax
import numpy as np

D_MODEL = 1024
BATCH = 1
SEQ = 2048
DEPTH = 1

CHUNK = 64
Q_BLOCK = 128
EPS = 1e-6

MLA_HEADS = 8
MLA_NOPE = 64
MLA_ROPE = 32
MLA_V = 64
MLA_QK = MLA_NOPE + MLA_ROPE
Q_LORA = 768
KV_LORA = 256
ROPE_THETA = 10000.0
MLA_WIDTH = MLA_HEADS * MLA_V

HG_HEADS = 8
HG_DK = 64
HG_DV = 64
HG_KEY_WIDTH = HG_HEADS * HG_DK
HG_WIDTH = HG_HEADS * HG_DV
HG_BLOCK = 32

N_BRANCH = 2
IN_SPLITS = (Q_LORA, KV_LORA, MLA_ROPE, MLA_WIDTH,
             HG_KEY_WIDTH, HG_KEY_WIDTH, HG_WIDTH, HG_WIDTH,
             N_BRANCH * D_MODEL)
D_IN = sum(IN_SPLITS)

kernel_name = "hybrid_mla_hgrn2_gated_merge"

def rmsnorm(x, g):
    xf = x.astype(jnp.float32)
    y = xf * lax.rsqrt(jnp.mean(xf * xf, axis=-1, keepdims=True) + EPS)
    return (y * g.astype(jnp.float32)).astype(x.dtype)

def rope_tables(seq):
    inv = ROPE_THETA ** (-jnp.arange(0, MLA_ROPE, 2, dtype=jnp.float32) / MLA_ROPE)
    ang = jnp.arange(seq, dtype=jnp.float32)[:, None] * inv[None, :]
    return jnp.cos(ang), jnp.sin(ang)

def apply_rope(x, cos, sin):
    half = MLA_ROPE // 2
    xf = x.astype(jnp.float32)
    x1, x2 = xf[..., :half], xf[..., half:]
    c = cos[None, :, None, :]
    s = sin[None, :, None, :]
    return jnp.concatenate([x1 * c - x2 * s, x1 * s + x2 * c], axis=-1).astype(x.dtype)

def chunk_causal_attention(q, k, v):
    b, h, s, dq = q.shape
    nqb = s // Q_BLOCK
    qb = q.reshape(b, h, nqb, Q_BLOCK, dq).transpose(2, 0, 1, 3, 4)
    key_chunk = jnp.arange(s) // CHUNK
    q_chunk = (jnp.arange(s) // CHUNK).reshape(nqb, Q_BLOCK)
    scale = 1.0 / math.sqrt(dq)

    def one_block(args):
        qi, qc = args
        sc = jnp.einsum('bhqd,bhkd->bhqk', qi, k).astype(jnp.float32) * scale
        mask = key_chunk[None, :] <= qc[:, None]
        sc = jnp.where(mask, sc, -jnp.inf)
        p = jax.nn.softmax(sc, axis=-1).astype(v.dtype)
        return jnp.einsum('bhqk,bhkd->bhqd', p, v)

    out = lax.map(one_block, (qb, q_chunk))
    return out.transpose(1, 2, 0, 3, 4).reshape(b, h, s, -1)

def hgrn2_chunkwise(q, k, v, log_f):
    b, s, h, dk = q.shape
    dv = v.shape[-1]
    n = s // HG_BLOCK

    def blocks(t):
        return t.astype(jnp.float32).reshape(b, n, HG_BLOCK, h, -1).transpose(0, 3, 1, 2, 4)

    qc, kc, vc, gc = blocks(q), blocks(k), blocks(v), blocks(log_f)
    cum = jnp.cumsum(gc, axis=3)
    last = cum[..., -1:, :]
    q_dec = qc * jnp.exp(cum)
    k_inv = kc * jnp.exp(-cum)
    k_end = kc * jnp.exp(last - cum)
    causal = jnp.tril(jnp.ones((HG_BLOCK, HG_BLOCK), dtype=bool))
    a = jnp.where(causal, jnp.einsum('bhntk,bhnsk->bhnts', q_dec, k_inv), 0.0)
    o_intra = jnp.einsum('bhnts,bhnsv->bhntv', a, vc)
    upd = jnp.einsum('bhnsk,bhnsv->bhnkv', k_end, vc)
    decay = jnp.exp(last[..., 0, :])

    def step(state, xs):
        d, u = xs
        return d[..., None] * state + u, state

    init = jnp.zeros((b, h, dk, dv), jnp.float32)
    _, s_prev = lax.scan(step, init, (jnp.moveaxis(decay, 2, 0), jnp.moveaxis(upd, 2, 0)))
    s_prev = jnp.moveaxis(s_prev, 0, 2)
    o_inter = jnp.einsum('bhntk,bhnkv->bhntv', q_dec, s_prev)
    return (o_intra + o_inter).transpose(0, 2, 3, 1, 4).reshape(b, s, h, dv)

def setup_inputs(seed: int = 0) -> dict:
    key = jax.random.key(seed)
    ks = jax.random.split(key, 14)

    def nrm(k, shape, fan_in):
        return jax.random.normal(k, shape, jnp.float32) * (fan_in ** -0.5)

    def gain(k, shape):
        return 1.0 + 0.02 * jax.random.normal(k, shape, jnp.float32)

    return {
        "x": jax.random.normal(ks[0], (BATCH, SEQ, D_MODEL), jnp.float32),
        "g_pre": gain(ks[1], (DEPTH, D_MODEL)),
        "w_in": nrm(ks[2], (DEPTH, D_MODEL, D_IN), D_MODEL),
        "b_gate": 0.01 * jax.random.normal(ks[3], (DEPTH, N_BRANCH * D_MODEL), jnp.float32),
        "g_q": gain(ks[4], (DEPTH, Q_LORA)),
        "w_uq": nrm(ks[5], (DEPTH, Q_LORA, MLA_HEADS * MLA_QK), Q_LORA),
        "g_kv": gain(ks[6], (DEPTH, KV_LORA)),
        "w_ukv": nrm(ks[7], (DEPTH, KV_LORA, MLA_HEADS * (MLA_NOPE + MLA_V)), KV_LORA),
        "lb_logits": 0.1 * jax.random.normal(ks[8], (DEPTH + 1, HG_KEY_WIDTH), jnp.float32),
        "g_hgrn": gain(ks[9], (DEPTH, HG_DV)),
        "w_branch_a": nrm(ks[10], (DEPTH, MLA_WIDTH, D_MODEL), MLA_WIDTH),
        "w_branch_b": nrm(ks[11], (DEPTH, HG_WIDTH, D_MODEL), HG_WIDTH),
        "w_out": nrm(ks[12], (DEPTH, D_MODEL, D_MODEL), D_MODEL),
        "g_post": gain(ks[13], (DEPTH, D_MODEL)),
    }

def reference(x, g_pre, w_in, b_gate, g_q, w_uq, g_kv, w_ukv, lb_logits,
              g_hgrn, w_branch_a, w_branch_b, w_out, g_post):
    b, s, _ = x.shape
    cos, sin = rope_tables(s)
    split_at = [int(o) for o in np.cumsum(IN_SPLITS)[:-1]]
    lower_bounds = jnp.cumsum(jax.nn.softmax(lb_logits.astype(jnp.float32), axis=0), axis=0)

    for l in range(DEPTH):
        h = rmsnorm(x, g_pre[l])
        proj = h @ w_in[l]
        (c_q, c_kv, k_pe, gate_a, hq, hf, hi, gate_b, merge_logits) = jnp.split(proj, split_at, axis=-1)

        q = (rmsnorm(c_q, g_q[l]) @ w_uq[l]).reshape(b, s, MLA_HEADS, MLA_QK)
        q_nope, q_pe = q[..., :MLA_NOPE], apply_rope(q[..., MLA_NOPE:], cos, sin)
        kv = (rmsnorm(c_kv, g_kv[l]) @ w_ukv[l]).reshape(b, s, MLA_HEADS, MLA_NOPE + MLA_V)
        k_nope, v = kv[..., :MLA_NOPE], kv[..., MLA_NOPE:]
        k_pe = jnp.broadcast_to(apply_rope(k_pe[:, :, None, :], cos, sin), (b, s, MLA_HEADS, MLA_ROPE))
        qf = jnp.concatenate([q_nope, q_pe], axis=-1).transpose(0, 2, 1, 3)
        kf = jnp.concatenate([k_nope, k_pe], axis=-1).transpose(0, 2, 1, 3)
        vf = v.transpose(0, 2, 1, 3)
        attn = chunk_causal_attention(qf, kf, vf).transpose(0, 2, 1, 3).reshape(b, s, MLA_WIDTH)
        y_a = (attn * jax.nn.silu(gate_a)) @ w_branch_a[l]

        lb = lower_bounds[l]
        f = lb + (1.0 - lb) * jax.nn.sigmoid(hf.astype(jnp.float32))
        log_f = jnp.log(f).reshape(b, s, HG_HEADS, HG_DK)
        k_in = (1.0 - f).reshape(b, s, HG_HEADS, HG_DK)
        o = hgrn2_chunkwise(hq.reshape(b, s, HG_HEADS, HG_DK), k_in,
                            hi.reshape(b, s, HG_HEADS, HG_DV), log_f)
        o = rmsnorm(o, g_hgrn[l]).astype(x.dtype).reshape(b, s, HG_WIDTH)
        y_b = (o * jax.nn.silu(gate_b)) @ w_branch_b[l]

        gates = jax.nn.sigmoid((merge_logits + b_gate[l]).astype(jnp.float32)).astype(x.dtype)
        m = gates[..., :D_MODEL] * y_a + gates[..., D_MODEL:] * y_b
        y = m @ w_out[l]
        x = x + rmsnorm(y, g_post[l])
    return x


_drawn_inputs = setup_inputs


def setup_inputs(seed=0):
    import zlib

    import numpy as np

    out = dict(_drawn_inputs(seed))
    spreads = {}
    factors = {'b_gate': 8.0, 'g_q': 8.0, 'g_kv': 8.0, 'g_hgrn': 3.768, 'g_post': 3.88}
    for name, (base, spread) in spreads.items():
        noise = np.random.default_rng([zlib.crc32(name.encode()), seed]).standard_normal(out[name].shape)
        drawn = base * np.exp(spread * noise) if base else spread * noise
        out[name] = __import__('jax').numpy.asarray(drawn.astype(out[name].dtype))
    for name, factor in factors.items():
        out[name] = (out[name] * factor).astype(out[name].dtype)
    return out
```

```python
import numpy as np
import concourse.bass as bass
from concourse import mybir
from contextlib import ExitStack

F32 = mybir.dt.float32
F32R = mybir.dt.float32r
ALU = mybir.AluOpType
ACT = mybir.ActivationFunctionType
AX = mybir.AxisListType
ds = bass.ds

P = 128
S = 2048
D = 1024
KD = D // P
TT = S // P
BLK = 512
NB = S // BLK
TPB = BLK // P
EPS = 1e-6

HEADS = 8
NOPE, ROPE, VD = 64, 32, 64
QK = NOPE + ROPE
Q_LORA, KV_LORA = 768, 256
KQ, KKV = Q_LORA // P, KV_LORA // P
ROPE_THETA = 10000.0
CHUNK = 64
SCALE = 1.0 / float(np.sqrt(QK))
MASKED = -1.0e30

HG_BLOCK = 32
PAIRS = HEADS // 2
NCH = S // HG_BLOCK
W = HEADS * VD
KW = W // P

C_CQ = 0
C_PE = Q_LORA + KV_LORA
C_GA = C_PE + ROPE
C_HQ = C_GA + W
C_HF = C_HQ + W
C_HI = C_HF + W
C_GB = C_HI + W
C_ML = C_GB + W

N_LORA = KQ + KKV
T_HQ = N_LORA
T_HF = T_HQ + KW
T_PE = T_HF + KW
T_ML = T_PE + 1
N_FM = T_ML + 2 * KD

SEG_COLS = (C_HI, C_GA, C_GB)


def three_products(pe, out, a, b, first, last):
    (a_hi, a_lo), (b_hi, b_lo) = a, b
    pe.matmul(out, a_hi, b_hi, start=first, stop=False)
    pe.matmul(out, a_hi, b_lo, start=False, stop=False)
    return pe.matmul(out, a_lo, b_hi, start=False, stop=last)


def clear_semaphores(nc, sems):
    nc.all_engine_barrier()
    nc.clear_and_free_semaphores(sems)
    nc.all_engine_barrier()


def input_projection(nc, hT_hi, hT_lo, x, g_pre, w_in, ident_d, projT, gateTok, hgTok):
    sems = []
    with ExitStack() as ctx:
        def sb(name, shape, dt=F32):
            return ctx.enter_context(nc.sbuf_tensor(name, shape, dt))

        def sem(name):
            sems.append(nc.alloc_semaphore(name))
            return sems[-1]

        x_tile = sb("x_tile", [P, 2, D])
        w_raw = sb("w_raw", [P, 2, KD, P])
        w_hi = sb("w_hi", [P, 2, KD, P], F32R)
        w_lo = sb("w_lo", [P, 2, KD, P], F32R)
        wt_raw = sb("wt_raw", [P, 2, W])
        wt_hi = sb("wt_hi", [P, KD, W], F32R)
        wt_lo = sb("wt_lo", [P, KD, W], F32R)
        stage = sb("stage", [P, 4, BLK])
        ident = sb("ident", [P, P])
        gain = sb("gain", [P, KD])
        eps = sb("eps", [P, 1])
        ss = sb("ss", [P, TT])
        std = sb("std", [P, TT])
        rstd = sb("rstd", [P, TT])
        bank = ctx.enter_context(nc.psum_tensor("bankA", [P, 8, BLK], F32))

        const_in = sem("const_in")
        const_set = sem("const_set")
        waited_pool = sem("waited_pool")
        waited_act = sem("waited_act")
        x_in = [sem("x_in0"), sem("x_in1")]
        sq_done = sem("sq_done")
        std_ready = sem("std_ready")
        rstd_ready = sem("rstd_ready")
        xn_ready = sem("xn_ready")
        xT_done = sem("xT_done")
        hT_hi_ready = sem("hT_hi_ready")
        hT_lo_ready = sem("hT_lo_ready")
        w_in_s = [sem("w_in0"), sem("w_in1")]
        w_hi_ready = sem("w_hi_ready")
        w_ready = sem("w_ready")
        raw_free = sem("raw_free")
        fm_done = sem("fm_done")
        bank_free = sem("bank_free")
        stored = [sem(f"stored{i}") for i in range(4)]
        wt_in = [sem("wt_in0"), sem("wt_in1")]
        wt_raw_free = sem("wt_raw_free")
        wt_hi_ready = sem("wt_hi_ready")
        wt_ready = sem("wt_ready")
        wt_used = sem("wt_used")
        tm_done = sem("tm_done")
        tm_free = sem("tm_free")
        v_hi = sem("v_hi")
        v_stored = [sem("v_stored0"), sem("v_stored1")]

        N_TILES = T_PE + 1
        v_out = x_tile[:].bitcast(F32R).rearrange("p u (h c n) -> p u h c n", c=2, n=VD)

        w_v = w_in.rearrange("(k p) n -> p k n", p=P)

        with nc.Block() as block:

            @block.sync
            def _(sp):
                sp.dma_start(ident[:], ident_d).then_inc(const_in, 16)
                sp.dma_start(gain[:], g_pre.rearrange("o (k p) -> p (o k)", p=P),
                             allow_slow_non_contiguous=True).then_inc(const_in, 16)
                sp.sem_inc(raw_free, 2)
                for j in range(2):
                    sp.dma_start(x_tile[:, j, :], x[j * P:(j + 1) * P, :]).then_inc(x_in[j], 16)
                with sp.Fori(0, TT // 2 - 1) as i:
                    for j in range(2):
                        sp.wait_ge(xT_done, i * 2 + (j + 1))
                        sp.dma_start(x_tile[:, j, :], x[ds(i * (2 * P) + (2 + j) * P, P), :]).then_inc(x_in[j], 16)

                def load_tiles(n0, count, col0):
                    with sp.Fori(0, count // 2) as i:
                        for u in range(2):
                            sp.wait_ge(raw_free, i * 2 + (n0 + u + 1))
                            sp.dma_start(w_raw[:, u], w_v[:, :, ds(i * (2 * P) + (col0 + u * P), P)])\
                              .then_inc(w_in_s[u], 16)

                load_tiles(0, N_LORA, C_CQ)
                load_tiles(T_HQ, 2 * KW, C_HQ)
                sp.wait_ge(raw_free, T_PE + 1)
                sp.dma_start(w_raw[:, 0, :, 0:QK], w_v[:, :, C_PE - NOPE:C_PE + ROPE]).then_inc(w_in_s[0], 16)
                sp.dma_start(w_raw[:, 0, :, QK:QK + 16], w_v[:, :, C_PE + 16:C_PE + 32]).then_inc(w_in_s[0], 16)
                sp.dma_start(w_raw[:, 0, :, QK + 16:P], w_v[:, :, C_PE:C_PE + 16]).then_inc(w_in_s[0], 16)
                sp.sem_inc(wt_raw_free, 2)
                for v in v_stored:
                    sp.sem_inc(v, 16)

                def load_segment(s):
                    with sp.Fori(0, KD // 2) as i:
                        for u in range(2):
                            sp.wait_ge(wt_raw_free, i * 2 + (s * KD + u + 1))
                            sp.dma_start(wt_raw[:, u], w_in[ds(i * (2 * P) + u * P, P), SEG_COLS[s]:SEG_COLS[s] + W])\
                              .then_inc(wt_in[u], 16)

                def store_values(first, end):
                    for t in range(first, end):
                        sp.wait_ge(tm_free, 8 + t + 1)
                        sp.dma_start(hgTok[t], x_tile[:, t % 2]).then_inc(v_stored[t % 2], 16)

                load_segment(0)
                store_values(0, TT // 2)
                load_segment(1)
                store_values(TT // 2, TT)
                load_segment(2)
                for v in v_stored:
                    sp.wait_ge(v, 16 + 16 * TT // 2)

            @block.gpsimd
            def _(pool):
                pool.memset(eps[:], EPS).then_inc(const_set, 1)

                def split_tile(u, n, arrived):
                    pool.wait_ge(w_in_s[u], arrived)
                    pool.wait_ge(fm_done, n * NB + NB)
                    pool.sem_inc(waited_pool, 1)
                    pool.tensor_scalar(w_hi[:, u], w_raw[:, u], 1.0, None, ALU.mult).then_inc(w_hi_ready, 1)
                    pool.wait_ge(w_hi_ready, n + 1)
                    pool.tensor_tensor(w_lo[:, u], w_raw[:, u], w_hi[:, u].bitcast(F32), ALU.subtract)\
                        .then_inc(w_ready, 1)
                    pool.wait_ge(w_ready, n + 1)
                    pool.sem_inc(raw_free, 1)

                with pool.Fori(0, T_PE // 2) as i:
                    for u in range(2):
                        split_tile(u, i * 2 + u, i * 16 + 16)
                split_tile(0, T_PE, T_PE // 2 * 16 + 48)

                pool.sem_inc(wt_used, KD - 1)
                with pool.Fori(0, len(SEG_COLS)) as s:
                    for k in range(KD):
                        u = k % 2
                        pool.wait_ge(wt_in[u], s * (KD // 2 * 16) + (k // 2 + 1) * 16)
                        if k < KD - 1:
                            pool.wait_ge(wt_used, s * (KD - 1) + (k + 1))
                        else:
                            pool.wait_ge(tm_done, s * TT + TT)
                        pool.sem_inc(waited_pool, 1)
                        pool.tensor_scalar(wt_hi[:, k], wt_raw[:, u], 1.0, None, ALU.mult).then_inc(wt_hi_ready, 1)
                        pool.wait_ge(wt_hi_ready, s * KD + (k + 1))
                        pool.tensor_tensor(wt_lo[:, k], wt_raw[:, u], wt_hi[:, k].bitcast(F32), ALU.subtract)\
                            .then_inc(wt_ready, 1)
                        pool.wait_ge(wt_ready, s * KD + (k + 1))
                        pool.sem_inc(wt_raw_free, 1)

            @block.scalar
            def _(act):
                act.wait_ge(const_in, 32)
                act.wait_ge(const_set, 1)
                with act.Fori(0, NB) as g:
                    for j in range(TPB):
                        act.wait_ge(x_in[j % 2], g * (TPB // 2 * 16) + (j // 2 + 1) * 16)
                        act.activation(stage[:, 0:2].rearrange("p a n -> p (a n)"), x_tile[:, j % 2], ACT.Square,
                                       accum_out=ss[:, ds(g * TPB + j, 1)]).then_inc(sq_done, 1)
                        act.wait_ge(sq_done, g * TPB + (j + 1))
                        act.sem_inc(waited_act, 1)
                        act.activation(std[:, ds(g * TPB + j, 1)], ss[:, ds(g * TPB + j, 1)], ACT.Sqrt,
                                       bias=eps[:, 0:1], scale=1.0 / D).then_inc(std_ready, 1)
                    act.wait_ge(xT_done, g * TPB + TPB)
                    for k in range(KD):
                        act.sem_inc(waited_act, 1)
                        act.activation(hT_hi[:, k, ds(g * BLK, BLK)], bank[:, k], ACT.Copy, scale=gain[:, k:k + 1])\
                           .then_inc(hT_hi_ready, 1)


                def tile_out(n, u, func):
                    for blk in range(NB):
                        act.wait_ge(fm_done, n * NB + (8 + blk + 1))
                        act.wait_ge(stored[blk], n * 16 + 16)
                        src = bank[:, u * NB + blk]
                        act.activation(stage[:, blk], src, func).then_inc(bank_free, 1)
                        act.wait_ge(bank_free, n * NB + (8 + blk + 1))
                        act.dma_start(projT[ds(n, 1), :, blk * BLK:(blk + 1) * BLK].rearrange("o p n -> (o p) n"),
                                      stage[:, blk]).then_inc(stored[blk], 16)

                for s in stored:
                    act.sem_inc(s, 16)
                with act.Fori(0, T_HF // 2) as i:
                    for u in range(2):
                        tile_out(i * 2 + u, u, ACT.Copy)
                with act.Fori(0, (T_PE - T_HF) // 2) as i:
                    for u in range(2):
                        tile_out(i * 2 + (T_HF + u), u, ACT.Sigmoid)
                tile_out(T_PE, 0, ACT.Copy)

                for t in range(TT):
                    act.wait_ge(tm_done, TT + t + 1)
                    act.wait_ge(v_stored[t % 2], 16 * (t // 2 + 1))
                    act.activation(v_out[:, t % 2, :, 0], bank[:, t % 8].rearrange("p (h n) -> p h n", n=VD), ACT.Copy)\
                       .then_inc(v_hi, 1)
                with act.Fori(1, len(SEG_COLS)) as s:
                    for t in range(TT):
                        act.wait_ge(tm_done, s * TT + (TT + t + 1))
                        act.wait_ge(stored[t % 4], s * (TT // 4 * 16) + (N_TILES + t // 4 + 1 - TT // 4) * 16)
                        act.activation(stage[:, t % 4], bank[:, t % 8], ACT.Copy).then_inc(tm_free, 1)
                        act.wait_ge(tm_free, s * TT + (8 + t + 1))
                        act.dma_start(gateTok[ds(s - 1, 1), t].rearrange("o p n -> (o p) n"), stage[:, t % 4])\
                           .then_inc(stored[t % 4], 16)
                for s in stored:
                    act.wait_ge(s, 16 * (1 + N_TILES + (len(SEG_COLS) - 1) * TT // 4))

            @block.vector
            def _(dve):
                dve.wait_ge(const_in, 32)
                with dve.Fori(0, NB) as g:
                    for j in range(TPB):
                        dve.wait_ge(std_ready, g * TPB + (j + 1))
                        dve.reciprocal(rstd[:, ds(g * TPB + j, 1)], std[:, ds(g * TPB + j, 1)]).then_inc(rstd_ready, 1)
                        dve.wait_ge(rstd_ready, g * TPB + (j + 1))
                        dve.tensor_scalar(x_tile[:, j % 2], x_tile[:, j % 2], rstd[:, ds(g * TPB + j, 1)], None,
                                          ALU.mult).then_inc(xn_ready, 1)
                    for k in range(KD):
                        dve.wait_ge(hT_hi_ready, g * KD + (k + 1))
                        dve.scalar_tensor_tensor(hT_lo[:, k, ds(g * BLK, BLK)], bank[:, k], gain[:, k:k + 1],
                                                 hT_hi[:, k, ds(g * BLK, BLK)].bitcast(F32), ALU.mult, ALU.subtract)\
                           .then_inc(hT_lo_ready, 1)

                for t in range(TT):
                    dve.wait_ge(v_hi, t + 1)
                    dve.tensor_tensor(v_out[:, t % 2, :, 1], bank[:, t % 8].rearrange("p (h n) -> p h n", n=VD),
                                      v_out[:, t % 2, :, 0].bitcast(F32), ALU.subtract).then_inc(tm_free, 1)

            @block.tensor
            def _(pe):
                pe.wait_ge(const_in, 32)
                pe.sem_inc(hT_lo_ready, KD)
                with pe.Fori(0, NB) as g:
                    for j in range(TPB):
                        pe.wait_ge(xn_ready, g * TPB + (j + 1))
                        if j == 0:
                            pe.wait_ge(hT_lo_ready, g * KD + KD)
                        for k in range(KD):
                            last = pe.transpose(bank[:, k, j * P:(j + 1) * P], x_tile[:, j % 2, k * P:(k + 1) * P],
                                                ident[:])
                        last.then_inc(xT_done, 1)
                pe.wait_ge(hT_lo_ready, KD + NB * KD)

                def tile_products(u, n):
                    pe.wait_ge(w_ready, n + 1)
                    for blk in range(NB):
                        pe.wait_ge(bank_free, n * NB + (blk + 1))
                        cols = slice(blk * BLK, (blk + 1) * BLK)
                        for k in range(KD):
                            last = three_products(pe, bank[:, u * NB + blk], (w_hi[:, u, k], w_lo[:, u, k]),
                                                  (hT_hi[:, k, cols], hT_lo[:, k, cols]), k == 0, k == KD - 1)
                        last.then_inc(fm_done, 1)

                pe.sem_inc(bank_free, 8)
                pe.sem_inc(fm_done, 8)
                with pe.Fori(0, T_PE // 2) as i:
                    for u in range(2):
                        tile_products(u, i * 2 + u)
                tile_products(0, T_PE)

                pe.wait_ge(bank_free, 8 + N_TILES * NB)
                pe.sem_inc(tm_free, 8)
                pe.sem_inc(tm_done, TT)
                with pe.Fori(0, len(SEG_COLS)) as s:
                    for half in range(2):
                        for k in range(KD):
                            if half == 0:
                                pe.wait_ge(wt_ready, s * KD + (k + 1))
                            for b in range(8):
                                t = half * 8 + b
                                if k == 0:
                                    pe.wait_ge(tm_free, s * TT + (t + 1))
                                rows = slice(t * P, (t + 1) * P)
                                last = three_products(pe, bank[:, b], (hT_hi[:, k, rows], hT_lo[:, k, rows]),
                                                      (wt_hi[:, k], wt_lo[:, k]), k == 0, k == KD - 1)
                                if k == KD - 1:
                                    last.then_inc(tm_done, 1)
                                elif half == 1 and b == 7:
                                    last.then_inc(wt_used, 1)
    clear_semaphores(nc, sems)


def merge_logits_and_recurrence(nc, hT_hi, hT_lo, w_in, b_gate, lb_logits, g_hgrn, ident_d, causal_d, projT, hgTok, oB):
    UNITS = PAIRS * NB
    CPB = BLK // HG_BLOCK
    CPT = P // HG_BLOCK
    AT_SCORES, AT_TURN_K, AT_UPDATES, AT_OUTPUTS, AT_TURN = 0, 4, 8, 17, (22, 26)
    HALVES = (slice(0, 64), slice(64, P))

    sems = []
    with ExitStack() as ctx:
        def sb(name, shape, dt=F32):
            return ctx.enter_context(nc.sbuf_tensor("d_" + name, shape, dt))

        def sem(name):
            sems.append(nc.alloc_semaphore("d_" + name))
            return sems[-1]

        w_raw = sb("w_raw", [P, KD, P])
        w_hi = sb("w_hi", [P, KD, P], F32R)
        w_lo = sb("w_lo", [P, KD, P], F32R)
        stage = sb("stage", [P, 2, BLK])
        q_in = sb("q_in", [P, BLK])
        f_in = sb("f_in", [P, BLK])
        e = sb("e", [P, BLK])
        cum = sb("cum", [P, BLK])
        k_end = sb("k_end", [P, BLK])
        qd = sb("qd", [P, 2, BLK], F32R)
        ki = sb("ki", [P, 2, BLK], F32R)
        ket = sb("ket", [P, 2, BLK], F32R)
        v = sb("v", [P, TPB, 2, 2 * VD], F32R)
        masked = sb("masked", [P, BLK])
        a_hl = sb("a_hl", [P, 2, 2, BLK], F32R)
        states = sb("states", [P, VD, CPB + 1])
        decay = sb("decay", [P, VD, CPB + 1])
        s_hl = sb("s_hl", [P, CPB, 2, VD], F32R)
        o_fm = sb("o_fm", [P, BLK])
        o_lo = sb("o_lo", [P, 2, TPB, VD])
        o_sum = sb("o_sum", [P, 2, TPB, VD])
        o_out = sb("o_out", [P, TPB, 2, VD])
        mean = sb("mean", [P, 2 * TPB])
        logm = sb("logm", [P, 2 * TPB])
        rms = sb("rms", [P, 2 * TPB])
        ident = sb("ident", [P, P])
        causal = sb("causal", [P, P], mybir.dt.int32)
        inside = sb("inside", [P, BLK], mybir.dt.bfloat16)
        bias = sb("bias", [P, 2 * KD])
        gain = sb("gain", [P, VD])
        eps = sb("eps", [P, 1])
        lb_in = sb("lb_in", [P, 2, PAIRS])
        lb_tmp = sb("lb_tmp", [P, 3, PAIRS])
        lb = sb("lb", [P, PAIRS])
        span = sb("span", [P, PAIRS])
        bank = ctx.enter_context(nc.psum_tensor("bankD", [P, 8, BLK], F32))
        B_SCORE, B_TURN, B_UPD = 2, (4, 7), 4

        const_in = sem("const_in")
        const_set = sem("const_set")
        waited_act = sem("waited_act")
        waited_dve = sem("waited_dve")
        lb_step = sem("lb_step")
        lb_exp = sem("lb_exp")
        w_arrived = sem("w_arrived")
        w_hi_done = sem("w_hi_done")
        w_split = sem("w_split")
        half_used = sem("half_used")
        prod_done = sem("prod_done")
        logits_out = sem("logits_out")
        stored = [sem("stored0"), sem("stored1")]
        qf_in = sem("qf_in")
        v_in = sem("v_in")
        f_ready = sem("f_ready")
        ln_ready = sem("ln_ready")
        k_ready = sem("k_ready")
        cum_ready = sem("cum_ready")
        up_ready = sem("up_ready")
        decay_ready = sem("decay_ready")
        q_ready = sem("q_ready")
        diff_ready = sem("diff_ready")
        qd_hi = sem("qd_hi")
        qd_lo = sem("qd_lo")
        down_ready = sem("down_ready")
        kd_ready = sem("kd_ready")
        ki_hi = sem("ki_hi")
        ki_lo = sem("ki_lo")
        to_end_ready = sem("to_end_ready")
        k_end_ready = sem("k_end_ready")
        scores_done = sem("scores_done")
        ket_turned = sem("ket_turned")
        ket_hi = sem("ket_hi")
        ket_lo = sem("ket_lo")
        masked_ready = sem("masked_ready")
        a_hi = sem("a_hi")
        a_lo = sem("a_lo")
        carried = sem("carried")
        updated = sem("updated")
        upd_act = sem("upd_act")
        upd_dve = sem("upd_dve")
        states_ready = sem("states_ready")
        s_hi = sem("s_hi")
        s_lo = sem("s_lo")
        o_done = sem("o_done")
        o_fm_ready = sem("o_fm_ready")
        o_turned = sem("o_turned")
        o_lo_ready = sem("o_lo_ready")
        o_sum_ready = sem("o_sum_ready")
        sq_ready = sem("sq_ready")
        mean_ready = sem("mean_ready")
        log_ready = sem("log_ready")
        rms_ready = sem("rms_ready")
        normed = sem("normed")
        o_ready = sem("o_ready")
        o_stored = sem("o_stored")

        w_v = w_in.rearrange("(k p) n -> p k n", p=P)

        def chunk_c(rows, c):
            return states[rows, :, 1:].rearrange("p v (t c) -> p c t v", c=CPT)[:, c]

        def by_chunk(ap):
            return ap.rearrange("p (c n) -> p c n", n=HG_BLOCK)

        def is_first(n):
            return isinstance(n, int) and n == 0

        with nc.Block() as block:

            @block.sync
            def _(sp):
                sp.dma_start(ident[:], ident_d).then_inc(const_in, 16)
                sp.dma_start(causal[:], causal_d).then_inc(const_in, 16)
                sp.dma_start(bias[:], b_gate.rearrange("o (k p) -> p (o k)", p=P),
                             allow_slow_non_contiguous=True).then_inc(const_in, 16)
                for row in range(2):
                    sp.dma_start(lb_in[:, row], lb_logits[row:row + 1].rearrange("o (h p) -> p (o h)", p=P),
                                 allow_slow_non_contiguous=True).then_inc(const_in, 16)
                sp.dma_start(gain[:], g_hgrn[0:1, :].to_broadcast([P, VD])).then_inc(const_in, 16)

                def load_weights(n):
                    sp.dma_start(w_raw[:], w_v[:, :, ds(n * P + C_ML, P)]).then_inc(w_arrived, 16)

                def load_qf(pair, blk):
                    cols = slice(blk * BLK, (blk + 1) * BLK)
                    for dst, t in ((q_in, T_HQ), (f_in, T_HF)):
                        sp.dma_start(dst[:], projT[ds(pair + t, 1), :, cols].rearrange("o p n -> (o p) n")).then_inc(qf_in, 16)

                def load_v(pair, blk):
                    sp.dma_start(v[:].rearrange("p t h n -> p t (h n)").bitcast(F32),
                                 hgTok[blk * TPB:(blk + 1) * TPB, :, ds(pair * (4 * VD), 4 * VD)].rearrange("t p n -> p t n"))\
                      .then_inc(v_in, 16)

                def store_o(pair, blk, n):
                    sp.wait_ge(o_ready, n + 1)
                    sp.dma_start(oB[blk * TPB:(blk + 1) * TPB, :, ds(pair * P, P)].rearrange("t p n -> p t n"),
                                 o_out[:].rearrange("p t h n -> p t (h n)")).then_inc(o_stored, 16)

                def unit(pair, blk, after_pair, after_blk, n):
                    sp.wait_ge(w_split, n * 2 + 2)
                    load_weights(n + 1)
                    sp.wait_ge(qd_lo, n + 1)
                    sp.wait_ge(k_end_ready, n + 1)
                    load_qf(after_pair, after_blk)
                    sp.wait_ge(o_done, n * 2 + 2)
                    load_v(after_pair, after_blk)
                    store_o(pair, blk, n)

                sp.sem_inc(o_stored, 16)
                load_weights(0)
                load_qf(0, 0)
                load_v(0, 0)
                with sp.Fori(0, PAIRS - 1) as pair:
                    for blk in range(NB):
                        unit(pair, blk, pair + (blk + 1) // NB, (blk + 1) % NB, pair * NB + blk)
                for blk in range(NB - 1):
                    unit(PAIRS - 1, blk, PAIRS - 1, blk + 1, (PAIRS - 1) * NB + blk)
                store_o(PAIRS - 1, NB - 1, UNITS - 1)
                sp.wait_ge(o_stored, 16 + 16 * UNITS)

            @block.gpsimd
            def _(pool):
                pool.memset(eps[:], EPS).then_inc(const_set, 1)
                pool.memset(masked[:], 0.0).then_inc(const_set, 1)
                pool.memset(decay[:], 0.0).then_inc(const_set, 1)
                pool.memset(inside[:], 1.0).then_inc(const_set, 1)
                pool.wait_ge(const_set, 4)
                pool.memset(by_chunk(inside[:])[:, :, 0:1], 0.0).then_inc(const_set, 1)

                def split_weights(n):
                    for half in range(2):
                        ks = slice(half * KD // 2, (half + 1) * KD // 2)
                        pool.wait_ge(w_hi_done, n * 2 + (half + 1))
                        pool.tensor_tensor(w_lo[:, ks], w_raw[:, ks], w_hi[:, ks].bitcast(F32), ALU.subtract)\
                            .then_inc(w_split, 1)

                def split_unit(n):
                    pool.wait_ge(ki_hi, n + 1)
                    pool.tensor_tensor(ki[:, 1], e[:], ki[:, 0].bitcast(F32), ALU.subtract).then_inc(ki_lo, 1)
                    pool.wait_ge(qd_hi, n + 1)
                    pool.tensor_tensor(qd[:, 1], q_in[:], qd[:, 0].bitcast(F32), ALU.subtract).then_inc(qd_lo, 1)

                split_weights(0)
                split_unit(0)
                with pool.Fori(0, UNITS - 1) as n:
                    split_unit(n + 1)
                    split_weights(n + 1)

            @block.scalar
            def _(act):
                act.wait_ge(const_in, 96)
                act.wait_ge(const_set, 5)
                act.wait_ge(lb_step, 2)
                act.activation(lb_in[:], lb_in[:], ACT.Exp).then_inc(lb_exp, 1)

                def logits(n, j):
                    act.wait_ge(prod_done, n * NB + (4 + j + 1))
                    act.wait_ge(stored[j % 2], n * 32 + (j // 2 + 1) * 16)
                    act.sem_inc(waited_act, 1)
                    act.activation(stage[:, j % 2], bank[:, j % 2], ACT.Identity, bias=bias[:, ds(n, 1)]).then_inc(logits_out, 1)
                    act.wait_ge(logits_out, n * NB + (2 + j + 1))
                    act.dma_start(projT[ds(n + T_ML, 1), :, j * BLK:(j + 1) * BLK].rearrange("o p n -> (o p) n"), stage[:, j % 2])\
                       .then_inc(stored[j % 2], 16)

                for s in stored:
                    act.sem_inc(s, 16)

                def log_f(n):
                    act.wait_ge(f_ready, n + 1)
                    act.wait_ge(ki_lo, n + 1)
                    act.activation(e[:], f_in[:], ACT.Ln).then_inc(ln_ready, 1)

                def exp_up(n):
                    act.wait_ge(cum_ready, n + 1)
                    act.activation(e[:], cum[:], ACT.Exp).then_inc(up_ready, 1)

                def factors(n):
                    act.wait_ge(up_ready, n + 1)
                    if not is_first(n):
                        act.wait_ge(states_ready, n)
                    act.activation(decay[:, :, 1:], by_chunk(e[:])[:, :, HG_BLOCK - 1].unsqueeze(1).to_broadcast([P, VD, CPB]),
                                   ACT.Copy).then_inc(decay_ready, 1)
                    act.wait_ge(q_ready, n + 1)
                    act.wait_ge(decay_ready, n + 1)
                    act.activation(e[:], cum[:], ACT.Exp, scale=-1.0).then_inc(down_ready, 1)
                    act.wait_ge(diff_ready, n + 1)
                    act.activation(k_end[:], k_end[:], ACT.Exp).then_inc(to_end_ready, 1)

                def round_unit(n):
                    act.wait_ge(kd_ready, n + 1)
                    if not is_first(n):
                        act.wait_ge(scores_done, n * 2)
                    act.activation(ki[:, 0], e[:], ACT.Copy).then_inc(ki_hi, 1)
                    act.wait_ge(q_ready, n + 1)
                    if not is_first(n):
                        act.wait_ge(o_done, n * 2)
                    act.activation(qd[:, 0], q_in[:], ACT.Copy).then_inc(qd_hi, 1)

                def unit(n, more):
                    for hh in range(2):
                        act.wait_ge(masked_ready, n * 2 + (hh + 1))
                        act.activation(a_hl[:, hh, 0], masked[:], ACT.Copy).then_inc(a_hi, 1)
                        if hh == 0:
                            act.wait_ge(ket_turned, n + 1)
                            act.activation(ket[:, 0], bank[:, B_TURN[0]], ACT.Copy).then_inc(ket_hi, 1)
                    if more:
                        log_f(n + 1)
                    logits(n, 0)
                    act.wait_ge(carried, n + 1)
                    for c in range(CPT):
                        act.wait_ge(updated, n * CPT + (c + 1))
                        act.activation(chunk_c(HALVES[1], c),
                                       bank[HALVES[1], B_UPD + c].rearrange("p (t h v) -> p t h v", h=2, v=VD)[:, :, 1],
                                       ACT.Copy).then_inc(upd_act, 1)
                    act.wait_ge(states_ready, n + 1)
                    act.activation(s_hl[:, :, 0], states[:, :, 0:CPB].rearrange("p v c -> p c v"), ACT.Copy).then_inc(s_hi, 1)
                    if more:
                        exp_up(n + 1)
                    logits(n, 1)
                    if more:
                        factors(n + 1)
                    for hh in range(2):
                        act.wait_ge(o_done, n * 2 + (hh + 1))
                        act.wait_ge(o_turned, n * 2 + (hh + 1))
                        act.activation(o_fm[:], bank[:, B_SCORE + hh], ACT.Copy).then_inc(o_fm_ready, 1)
                    if more:
                        round_unit(n + 1)
                    logits(n, 2)
                    for hh in range(2):
                        act.wait_ge(o_turned, n * 2 + (hh + 2))
                        act.activation(o_lo[:, hh], bank[:, B_TURN[hh]].rearrange("p (t n) -> p t n", n=P)[:, :, VD:], ACT.Copy)\
                           .then_inc(o_lo_ready, 1)
                    act.wait_ge(mean_ready, n + 1)
                    act.activation(logm[:], mean[:], ACT.Ln, bias=eps[:, 0:1], scale=1.0 / VD).then_inc(log_ready, 1)
                    act.wait_ge(log_ready, n + 1)
                    act.activation(rms[:], logm[:], ACT.Exp, scale=-0.5).then_inc(rms_ready, 1)
                    logits(n, 3)

                log_f(0)
                exp_up(0)
                factors(0)
                round_unit(0)
                with act.Fori(0, UNITS - 1) as n:
                    unit(n, True)
                unit(UNITS - 1, False)
                for s in stored:
                    act.wait_ge(s, 16 + 16 * UNITS * NB // 2)

            @block.vector
            def _(dve):
                dve.wait_ge(const_in, 96)
                dve.tensor_tensor(lb_tmp[:, 0], lb_in[:, 0], lb_in[:, 1], ALU.max).then_inc(lb_step, 1)
                dve.wait_ge(lb_step, 1)
                dve.tensor_tensor(lb_in[:], lb_in[:], lb_tmp[:, 0:1].to_broadcast([P, 2, PAIRS]), ALU.subtract).then_inc(lb_step, 1)
                dve.wait_ge(lb_exp, 1)
                dve.tensor_tensor(lb_tmp[:, 1], lb_in[:, 0], lb_in[:, 1], ALU.add).then_inc(lb_step, 1)
                dve.wait_ge(lb_step, 3)
                dve.reciprocal(lb_tmp[:, 2], lb_tmp[:, 1]).then_inc(lb_step, 1)
                dve.wait_ge(lb_step, 4)
                dve.tensor_tensor(lb[:], lb_in[:, 0], lb_tmp[:, 2], ALU.mult).then_inc(lb_step, 1)
                dve.wait_ge(lb_step, 5)
                dve.tensor_scalar(span[:], lb[:], -1.0, 1.0, ALU.mult, ALU.add).then_inc(lb_step, 1)
                dve.wait_ge(lb_step, 6)
                dve.wait_ge(const_set, 5)

                dve.sem_inc(ki_lo, 1)

                def round_weights(n, half):
                    if half == 0:
                        dve.wait_ge(w_arrived, n * 16 + 16)
                        dve.wait_ge(half_used, n + 1)
                    else:
                        dve.wait_ge(prod_done, n * NB + NB)
                    ks = slice(half * KD // 2, (half + 1) * KD // 2)
                    dve.tensor_copy(w_hi[:, ks], w_raw[:, ks]).then_inc(w_hi_done, 1)

                def lower_bounded(pair, n):
                    dve.wait_ge(qf_in, n * 32 + 32)
                    dve.tensor_scalar(f_in[:], f_in[:], span[:, ds(pair, 1)], lb[:, ds(pair, 1)], ALU.mult, ALU.add)\
                       .then_inc(f_ready, 1)

                def accumulated(n):
                    dve.wait_ge(ln_ready, n + 1)
                    dve.tensor_tensor_scan(cum[:], inside[:], e[:], 0.0, ALU.mult, ALU.add).then_inc(cum_ready, 1)
                    dve.tensor_scalar(f_in[:], f_in[:], -1.0, 1.0, ALU.mult, ALU.add).then_inc(k_ready, 1)
                    dve.wait_ge(cum_ready, n + 1)
                    if not is_first(n):
                        dve.wait_ge(ket_turned, n)
                    dve.tensor_tensor(by_chunk(k_end[:]), by_chunk(cum[:])[:, :, HG_BLOCK - 1:].to_broadcast([P, CPB, HG_BLOCK]),
                                      by_chunk(cum[:]), ALU.subtract).then_inc(diff_ready, 1)

                def decayed_q(n):
                    dve.wait_ge(up_ready, n + 1)
                    dve.tensor_tensor(q_in[:], q_in[:], e[:], ALU.mult).then_inc(q_ready, 1)

                def decayed_k(n):
                    dve.wait_ge(k_ready, n + 1)
                    dve.wait_ge(down_ready, n + 1)
                    dve.tensor_tensor(e[:], f_in[:], e[:], ALU.mult).then_inc(kd_ready, 1)
                    dve.wait_ge(to_end_ready, n + 1)
                    dve.tensor_tensor(k_end[:], f_in[:], k_end[:], ALU.mult).then_inc(k_end_ready, 1)

                def unit(blk, n, after_pair, more):
                    for hh in range(2):
                        dve.wait_ge(scores_done, n * 2 + (hh + 1))
                        if hh == 1:
                            dve.wait_ge(a_lo, n * 2 + 1)
                        dve.sem_inc(waited_dve, 1)
                        dve.copy_predicated(masked[:].rearrange("p (t n) -> p t n", n=P),
                                            causal[:].unsqueeze(1).to_broadcast([P, TPB, P]),
                                            bank[:, B_SCORE + hh].rearrange("p (t n) -> p t n", n=P)).then_inc(masked_ready, 1)
                        if hh == 1:
                            dve.wait_ge(ket_hi, n + 1)
                            dve.tensor_tensor(ket[:, 1], bank[:, B_TURN[0]], ket[:, 0].bitcast(F32), ALU.subtract).then_inc(ket_lo, 1)
                        dve.wait_ge(a_hi, n * 2 + (hh + 1))
                        dve.tensor_tensor(a_hl[:, hh, 1], masked[:], a_hl[:, hh, 0].bitcast(F32), ALU.subtract).then_inc(a_lo, 1)
                    if more:
                        lower_bounded(after_pair, n + 1)
                    if blk == 0:
                        dve.memset(states[:, :, 0:1], 0.0).then_inc(carried, 1)
                    else:
                        dve.tensor_copy(states[:, :, 0:1], states[:, :, CPB:]).then_inc(carried, 1)
                    dve.wait_ge(carried, n + 1)
                    for c in range(CPT):
                        dve.wait_ge(updated, n * CPT + (c + 1))
                        dve.tensor_copy(chunk_c(HALVES[0], c),
                                        bank[HALVES[0], B_UPD + c].rearrange("p (t h v) -> p t h v", h=2, v=VD)[:, :, 0])\
                           .then_inc(upd_dve, 1)
                    dve.wait_ge(decay_ready, n + 1)
                    dve.wait_ge(upd_act, n * CPT + CPT)
                    dve.wait_ge(upd_dve, n * CPT + CPT)
                    flat = states[:].rearrange("p v c -> p (v c)")
                    dve.tensor_tensor_scan(flat, decay[:].rearrange("p v c -> p (v c)"), flat, 0.0, ALU.mult, ALU.add)\
                       .then_inc(states_ready, 1)
                    if more:
                        accumulated(n + 1)
                    dve.wait_ge(s_hi, n + 1)
                    dve.tensor_tensor(s_hl[:, :, 1], states[:, :, 0:CPB].rearrange("p v c -> p c v"), s_hl[:, :, 0].bitcast(F32),
                                      ALU.subtract).then_inc(s_lo, 1)
                    if more:
                        decayed_q(n + 1)
                        decayed_k(n + 1)
                    for hh in range(2):
                        dve.wait_ge(o_lo_ready, n * 2 + (hh + 1))
                        dve.tensor_tensor(o_sum[:, hh], bank[:, B_TURN[hh]].rearrange("p (t n) -> p t n", n=P)[:, :, 0:VD],
                                          o_lo[:, hh], ALU.add).then_inc(o_sum_ready, 1)
                    dve.wait_ge(o_sum_ready, n * 2 + 4)
                    dve.tensor_tensor(o_lo[:], o_sum[:], o_sum[:], ALU.mult).then_inc(sq_ready, 1)
                    dve.wait_ge(sq_ready, n + 1)
                    dve.reduce_sum(mean[:].rearrange("p (h t) -> p h t", h=2), o_lo[:], AX.X).then_inc(mean_ready, 1)
                    if more:
                        round_weights(n + 1, 0)
                    dve.wait_ge(rms_ready, n + 1)
                    dve.tensor_tensor(o_sum[:].rearrange("p h t n -> p (h t) n"), o_sum[:].rearrange("p h t n -> p (h t) n"),
                                      rms[:].unsqueeze(2).to_broadcast([P, 2 * TPB, VD]), ALU.mult).then_inc(normed, 1)
                    dve.wait_ge(normed, n + 1)
                    dve.wait_ge(o_stored, n * 16 + 16)
                    dve.tensor_tensor(o_out[:].rearrange("p t h n -> p h t n"), o_sum[:],
                                      gain[:].unsqueeze(1).unsqueeze(1).to_broadcast([P, 2, TPB, VD]), ALU.mult).then_inc(o_ready, 1)
                    if more:
                        round_weights(n + 1, 1)

                round_weights(0, 0)
                round_weights(0, 1)
                lower_bounded(0, 0)
                accumulated(0)
                decayed_q(0)
                decayed_k(0)
                with dve.Fori(0, PAIRS - 1) as pair:
                    for blk in range(NB):
                        unit(blk, pair * NB + blk, pair + (blk + 1) // NB, True)
                for blk in range(NB):
                    unit(blk, (PAIRS - 1) * NB + blk, PAIRS - 1, blk < NB - 1)

            @block.tensor
            def _(pe):
                pe.wait_ge(const_in, 96)

                def scores(n, part):
                    hh, rows = part // 2, HALVES[part // 2]
                    if part == 0:
                        pe.wait_ge(qd_lo, n + 1)
                        pe.wait_ge(ki_lo, n + 2)
                    for t in range(part % 2 * 2, part % 2 * 2 + 2):
                        cols = slice(t * P, (t + 1) * P)
                        last = three_products(pe, bank[:, B_SCORE + hh, cols], (ki[rows, 0, cols], ki[rows, 1, cols]),
                                              (qd[rows, 0, cols], qd[rows, 1, cols]), True, True)
                    if part % 2:
                        last.then_inc(scores_done, 1)

                def turn_k(n):
                    pe.wait_ge(k_end_ready, n + 1)
                    pe.wait_ge(o_sum_ready, n * 2 + 2)
                    for t in range(TPB):
                        cols = slice(t * P, (t + 1) * P)
                        last = pe.transpose(bank[:, B_TURN[0], cols], k_end[:, cols], ident[:])
                    last.then_inc(ket_turned, 1)

                def updates(n, t):
                    if t == 0:
                        pe.wait_ge(ket_lo, n + 1)
                        pe.wait_ge(v_in, n * 16 + 16)
                    for c in range(CPT):
                        rows = slice(c * HG_BLOCK, (c + 1) * HG_BLOCK)
                        last = three_products(pe, bank[:, B_UPD + c, t * P:(t + 1) * P],
                                              (ket[rows, 0, t * P:(t + 1) * P], ket[rows, 1, t * P:(t + 1) * P]),
                                              (v[rows, t, :, 0:VD], v[rows, t, :, VD:]), True, True)
                        if t == TPB - 1:
                            last.then_inc(updated, 1)

                def outputs(n, part):
                    hh, t = part // TPB, part % TPB
                    if part == 0:
                        pe.wait_ge(a_lo, n * 2 + 2)
                        pe.wait_ge(s_lo, n + 1)
                    cols = slice(t * P, (t + 1) * P)
                    dst = bank[:, B_SCORE + hh]
                    for half in range(2):
                        pe.matmul(dst[:, cols], v[:, t, hh], a_hl[:, hh, half, cols], start=half == 0, stop=False)
                    for c in range(t * CPT, (t + 1) * CPT):
                        own = slice(c * HG_BLOCK, (c + 1) * HG_BLOCK)
                        for half in range(2):
                            last = pe.matmul(dst[:, own], s_hl[HALVES[hh], c].rearrange("p a n -> p (a n)"),
                                             qd[HALVES[hh], half, own], start=False, stop=half == 1 and c == (t + 1) * CPT - 1)
                    if t == TPB - 1:
                        last.then_inc(o_done, 1)

                def turn_outputs(n, hh):
                    pe.wait_ge(o_fm_ready, n * 2 + (hh + 1))
                    for t in range(TPB):
                        cols = slice(t * P, (t + 1) * P)
                        last = pe.transpose(bank[:, B_TURN[hh], cols], o_fm[:, cols], ident[:])
                    last.then_inc(o_turned, 1)

                pe.sem_inc(prod_done, 4)
                pe.sem_inc(logits_out, 2)
                pe.sem_inc(half_used, 1)
                pe.sem_inc(o_turned, 1)
                pe.sem_inc(o_sum_ready, 2)
                with pe.Fori(0, UNITS) as n:
                    for g in range(NB * KD):
                        j, k = g // KD, g % KD
                        if 0 <= g - AT_SCORES < 4:
                            scores(n, g - AT_SCORES)
                        if g == AT_TURN_K:
                            turn_k(n)
                        if 0 <= g - AT_UPDATES < TPB:
                            updates(n, g - AT_UPDATES)
                        if 0 <= g - AT_OUTPUTS < 2 * TPB:
                            outputs(n, g - AT_OUTPUTS)
                        if g in AT_TURN:
                            turn_outputs(n, AT_TURN.index(g))
                        if j == 0 and k in (0, KD // 2):
                            pe.wait_ge(w_split, n * 2 + (k // (KD // 2) + 1))
                        if k == 0:
                            pe.wait_ge(logits_out, n * NB + (j + 1))
                        cols = slice(j * BLK, (j + 1) * BLK)
                        last = three_products(pe, bank[:, j % 2], (w_hi[:, k], w_lo[:, k]),
                                              (hT_hi[:, k, cols], hT_lo[:, k, cols]), k == 0, k == KD - 1)
                        if k == KD - 1:
                            last.then_inc(prod_done, 1)
                        elif j == NB - 1 and k == KD // 2 - 1:
                            last.then_inc(half_used, 1)
    clear_semaphores(nc, sems)


PE_ROWS, ROT_ROWS = slice(NOPE, QK), slice(QK, P)


def latent_projections(nc, projT, g_q, g_kv, w_uq, w_ukv, rope_d, ident_d, qT, knT, kpT, vTok):
    sems = []
    with ExitStack() as ctx:
        def sb(name, shape, dt=F32):
            return ctx.enter_context(nc.sbuf_tensor(name, shape, dt))

        def sem(name):
            sems.append(nc.alloc_semaphore("b_" + name))
            return sems[-1]

        HALF, QTR = S // 2, S // 4
        c_hi = sb("c_hi", [P, N_LORA, S], F32R)
        c_lo = sb("c_lo", [P, N_LORA, S], F32R)
        rope = sb("rope_b", [P, S])
        acc_rs = sb("acc_rs", [P, S])
        sq = sb("sq", [P, 2, QTR])
        scaled = sb("scaled", [P, 2, HALF])
        wq_raw = sb("wq_raw", [P, 2, KQ, P])
        wq_hi = sb("wq_hi", [P, 2, KQ, P], F32R)
        wq_lo = sb("wq_lo", [P, 2, KQ, P], F32R)
        wk_hi = sb("wk_hi", [P, KKV, W], F32R)
        wk_lo = sb("wk_lo", [P, KKV, W], F32R)
        wv_hi = sb("wv_hi", [P, KKV, W], F32R)
        wv_lo = sb("wv_lo", [P, KKV, W], F32R)
        out = sb("out_b", [P, 2, 2, BLK], F32R)
        turned = sb("turned", [P, 2, BLK])
        rot = sb("rot", [P, BLK])
        ident = sb("ident_b", [P, P])
        ones = sb("ones_b", [P, 1])
        gain = sb("gain_b", [P, N_LORA])
        eps = sb("eps_b", [P, 1])
        std = sb("std_b", [P, 2, TT])
        rstd = sb("rstd_b", [P, 2, TT])
        bank = ctx.enter_context(nc.psum_tensor("bankB", [P, 8, BLK], F32))
        SUMS, SPREAD = 4, 4

        const_in = sem("const_in")
        const_set = sem("const_set")
        waited_pool = sem("waited_pool")
        c_in = [sem(f"c_in{k}") for k in range(N_LORA)]
        wkv_in = sem("wkv_in")
        wkv_hi = sem("wkv_hi")
        wkv_ready = sem("wkv_ready")
        wq_in = [sem("wq_in0"), sem("wq_in1")]
        wq_raw_free = sem("wq_raw_free")
        wq_hi_ready = sem("wq_hi_ready")
        wq_ready = sem("wq_ready")
        kpe_in = sem("kpe_in")
        sq_ready = sem("sq_ready")
        sq_added = sem("sq_added")
        sums_done = sem("sums_done")
        std_ready = sem("std_ready")
        rstd_ready = sem("rstd_ready")
        spread_done = sem("spread_done")
        rs_ready = sem("rs_ready")
        scaled_ready = sem("scaled_ready")
        c_hi_ready = sem("c_hi_ready")
        c_ready = sem("c_ready")
        prod_done = sem("prod_done")
        bank_free = sem("bank_free")
        turned_ready = sem("turned_ready")
        rot_ready = sem("rot_ready")
        out_hi = sem("out_hi")
        out_lo = sem("out_lo")
        stored = [sem("stored0"), sem("stored1")]

        E_V, E_Q, E_PE, E_END = PAIRS * NB, PAIRS * NB + TT, PAIRS * NB + TT + HEADS * NB, 68
        SQ_KV = KKV * 4
        kv_tiles, q_tiles = range(KQ, N_LORA), range(KQ)

        wkv_v = w_ukv.rearrange("(k p) (h n) -> p k h n", p=P, n=P)
        wq_v = w_uq.rearrange("(k p) n -> p k n", p=P)

        with nc.Block() as block:

            @block.sync
            def _(sp):
                sp.dma_start(ident[:], ident_d).then_inc(const_in, 16)
                sp.dma_start(rope[:], rope_d).then_inc(const_in, 16)
                sp.dma_start(gain[:, 0:KQ], g_q.rearrange("o (k p) -> p (o k)", p=P),
                             allow_slow_non_contiguous=True).then_inc(const_in, 16)
                sp.dma_start(gain[:, KQ:], g_kv.rearrange("o (k p) -> p (o k)", p=P),
                             allow_slow_non_contiguous=True).then_inc(const_in, 16)
                for k in kv_tiles:
                    sp.dma_start(c_lo[:, k].bitcast(F32), projT[k]).then_inc(c_in[k], 16)
                for k in range(KKV):
                    sp.dma_start(scaled[:, 0, k * W:(k + 1) * W].rearrange("p (h n) -> p h n", n=NOPE),
                                 wkv_v[:, k, :, 0:NOPE]).then_inc(wkv_in, 16)
                    sp.dma_start(scaled[:, 1, k * W:(k + 1) * W].rearrange("p (h n) -> p h n", n=VD),
                                 wkv_v[:, k, :, NOPE:P]).then_inc(wkv_in, 16)
                for k in q_tiles:
                    sp.dma_start(c_lo[:, k].bitcast(F32), projT[k]).then_inc(c_in[k], 16)
                def load_wq(u, h):
                    for to, of, n in ((0, 0, QK), (QK, NOPE + 16, 16), (QK + 16, NOPE, 16)):
                        sp.dma_start(wq_raw[:, u, :, to:to + n], wq_v[:, :, ds(h * QK + of, n)]).then_inc(wq_in[u], 16)

                load_wq(0, 0)
                load_wq(1, 1)
                for s in stored:
                    sp.sem_inc(s, 32)
                for e in range(E_V):
                    p, blk = e // NB, e % NB
                    sp.wait_ge(bank_free, 4 + e + 1)
                    for part in range(2):
                        sp.dma_start(knT[p, part, :, blk * BLK:(blk + 1) * BLK], out[:, e % 2, part].bitcast(F32))\
                          .then_inc(stored[e % 2], 16)
                for t in range(TT):
                    e = E_V + t
                    sp.wait_ge(bank_free, 4 + e + 1)
                    for part in range(2):
                        sp.dma_start(vTok[part * 4:(part + 1) * 4, :, t, :].rearrange("h p n -> p h n"),
                                     out[:, e % 2, part].bitcast(F32).rearrange("p (h n) -> p h n", n=2 * VD))\
                          .then_inc(stored[e % 2], 16)
                sp.wait_ge(c_ready, 2 * N_LORA)
                sp.dma_start(scaled[NOPE:P].rearrange("p a n -> p (a n)"), projT[T_PE, NOPE:P, :]).then_inc(kpe_in, 16)

                def store_q(h, n0):
                    for blk in range(NB):
                        sp.wait_ge(out_lo, n0 + (blk + 3))
                        for part in range(2):
                            sp.dma_start(qT[ds(h, 1), part, :, blk * BLK:(blk + 1) * BLK].rearrange("o p n -> (o p) n"),
                                         out[0:QK, blk % 2, part].bitcast(F32)).then_inc(stored[blk % 2], 16)

                with sp.Fori(0, HEADS // 2 - 1) as i:
                    for u in range(2):
                        sp.wait_ge(wq_raw_free, i * 2 + (u + 1))
                        load_wq(u, i * 2 + (2 + u))
                        store_q(i * 2 + u, i * (2 * NB) + u * NB)
                for h in range(HEADS - 2, HEADS):
                    store_q(h, h * NB)
                for blk in range(NB):
                    sp.wait_ge(out_lo, HEADS * NB + blk + 3)
                    for part in range(2):
                        sp.dma_start(kpT[part, :, blk * BLK:(blk + 1) * BLK], out[PE_ROWS, blk % 2, part].bitcast(F32))\
                          .then_inc(stored[blk % 2], 16)
                for s in stored:
                    sp.wait_ge(s, 32 + 32 * (E_END // 2))

            @block.gpsimd
            def _(pool):
                pool.memset(eps[:], EPS).then_inc(const_set, 1)
                pool.memset(ones[:], 1.0).then_inc(const_set, 1)
                pool.wait_ge(wkv_in, 2 * KKV * 16)
                for n, (hi, lo) in enumerate(((wk_hi, wk_lo), (wv_hi, wv_lo))):
                    flat = scaled[:, n]
                    hi, lo = (w[:].rearrange("p k n -> p (k n)") for w in (hi, lo))
                    pool.sem_inc(waited_pool, 1)
                    pool.tensor_scalar(hi, flat, 1.0, None, ALU.mult).then_inc(wkv_hi, 1)
                    pool.wait_ge(wkv_hi, n + 1)
                    pool.tensor_tensor(lo, flat, hi.bitcast(F32), ALU.subtract).then_inc(wkv_ready, 1)

                def split_c(m):
                    k, half = m // 2, m % 2
                    tile = (*kv_tiles, *q_tiles)[k]
                    cols = slice(half * HALF, (half + 1) * HALF)
                    pool.wait_ge(c_hi_ready, m + 1)
                    pool.tensor_tensor(c_lo[:, tile, cols], scaled[:, m % 2], c_hi[:, tile, cols].bitcast(F32),
                                       ALU.subtract).then_inc(c_ready, 1)

                def split_wq(u, i):
                    pool.wait_ge(wq_in[u], i * 48 + 48)
                    pool.wait_ge(prod_done, (i * 2 + u) * NB + (E_Q + 4))
                    pool.sem_inc(waited_pool, 1)
                    pool.tensor_scalar(wq_hi[:, u], wq_raw[:, u], 1.0, None, ALU.mult).then_inc(wq_hi_ready, 1)
                    pool.wait_ge(wq_hi_ready, i * 2 + (u + 1))
                    pool.tensor_tensor(wq_lo[:, u], wq_raw[:, u], wq_hi[:, u].bitcast(F32), ALU.subtract)\
                        .then_inc(wq_ready, 1)
                    pool.wait_ge(wq_ready, i * 2 + (u + 1))
                    pool.sem_inc(wq_raw_free, 1)

                for m in range(2 * N_LORA):
                    split_c(m)
                with pool.Fori(0, HEADS // 2) as i:
                    for u in range(2):
                        split_wq(u, i)

            @block.scalar
            def _(act):
                act.wait_ge(const_in, 64)
                act.wait_ge(const_set, 2)

                def square(m):
                    n = m if m < SQ_KV else m - SQ_KV
                    tile, quarter = (kv_tiles if m < SQ_KV else q_tiles)[n // 4], n % 4
                    cols = slice(quarter * QTR, (quarter + 1) * QTR)
                    act.wait_ge(c_in[tile], 16)
                    if n < 4:
                        if m >= SQ_KV:
                            act.wait_ge(scaled_ready, 2 * KKV)
                        dst = acc_rs[:, cols]
                    else:
                        if m >= 2:
                            act.wait_ge(sq_added, m - 1)
                        dst = sq[:, m % 2]
                    act.activation(dst, c_lo[:, tile, cols].bitcast(F32), ACT.Square).then_inc(sq_ready, 1)

                def root(g, width):
                    act.wait_ge(sums_done, g + 1)
                    act.activation(std[:, g], bank[:, SUMS, 0:TT], ACT.Sqrt, bias=eps[:, 0:1], scale=1.0 / width)\
                       .then_inc(std_ready, 1)

                def take_spread(g):
                    act.wait_ge(spread_done, g + 1)
                    act.activation(acc_rs[:].rearrange("p (b n) -> p b n", n=BLK), bank[:, SPREAD:SPREAD + NB], ACT.Copy)\
                       .then_inc(rs_ready, 1)

                def round_c(m):
                    k, half = m // 2, m % 2
                    tile = (*kv_tiles, *q_tiles)[k]
                    act.wait_ge(scaled_ready, m + 1)
                    act.activation(c_hi[:, tile, half * HALF:(half + 1) * HALF], scaled[:, m % 2], ACT.Copy)\
                       .then_inc(c_hi_ready, 1)

                for m in range(SQ_KV):
                    square(m)
                root(0, KV_LORA)
                take_spread(0)
                for m in range(2 * KKV):
                    round_c(m)
                for e in range(E_V):
                    act.wait_ge(prod_done, 8 + e + 1)
                    act.wait_ge(stored[e % 2], e // 2 * 32 + 32)
                    act.activation(out[:, e % 2, 0], bank[:, e % 4], ACT.Copy).then_inc(out_hi, 1)
                    for m in range(2 * e, 2 * e + 2):
                        if m < 4 * KQ:
                            square(SQ_KV + m)
                root(1, Q_LORA)
                take_spread(1)
                for t in range(TT):
                    e = E_V + t
                    if t < 2 * KQ:
                        round_c(2 * KKV + t)
                    act.wait_ge(prod_done, 8 + e + 1)
                    act.wait_ge(stored[e % 2], e // 2 * 32 + 32)
                    act.activation(out[:, e % 2].rearrange("p a (h c n) -> p (a h) c n", c=2, n=VD)[:, :, 0],
                                   bank[:, e % 4].rearrange("p (h n) -> p h n", n=VD), ACT.Copy).then_inc(out_hi, 1)

                def round_turned(e, slot, rows):
                    act.wait_ge(turned_ready, e + (1 - E_Q))
                    act.wait_ge(stored[slot], (e - slot) * 16 + 32)
                    act.activation(out[rows, slot, 0], turned[rows, slot], ACT.Copy).then_inc(out_hi, 1)

                with act.Fori(0, HEADS) as h:
                    for blk in range(NB):
                        round_turned(h * NB + (E_Q + blk), blk % 2, slice(0, QK))
                for blk in range(NB):
                    round_turned(E_PE + blk, blk % 2, PE_ROWS)

            @block.vector
            def _(dve):
                dve.wait_ge(const_in, 64)

                def add_square(m):
                    n = m if m < SQ_KV else m - SQ_KV
                    dve.wait_ge(sq_ready, m + 1)
                    if n < 4:
                        dve.sem_inc(sq_added, 1)
                        return
                    cols = slice(n % 4 * QTR, (n % 4 + 1) * QTR)
                    if n >= 8:
                        dve.wait_ge(sq_added, m - 3)
                    dve.tensor_tensor(acc_rs[:, cols], acc_rs[:, cols], sq[:, m % 2], ALU.add).then_inc(sq_added, 1)

                def inverse(g):
                    dve.wait_ge(std_ready, g + 1)
                    dve.reciprocal(rstd[:, g], std[:, g]).then_inc(rstd_ready, 1)

                def scale(m):
                    k, half = m // 2, m % 2
                    tile = (*kv_tiles, *q_tiles)[k]
                    cols = slice(half * HALF, (half + 1) * HALF)
                    if m < 2:
                        dve.wait_ge(wkv_ready, m + 1)
                    else:
                        dve.wait_ge(c_ready, m - 1)
                    dve.scalar_tensor_tensor(scaled[:, m % 2], c_lo[:, tile, cols].bitcast(F32), gain[:, tile:tile + 1],
                                             acc_rs[:, cols], ALU.mult, ALU.mult).then_inc(scaled_ready, 1)

                for m in range(SQ_KV):
                    add_square(m)
                inverse(0)
                dve.wait_ge(rs_ready, 1)
                for m in range(2 * KKV):
                    scale(m)
                for e in range(E_V):
                    dve.wait_ge(out_hi, e + 1)
                    dve.tensor_tensor(out[:, e % 2, 1], bank[:, e % 4], out[:, e % 2, 0].bitcast(F32), ALU.subtract)\
                       .then_inc(bank_free, 1)
                    for m in range(2 * e, 2 * e + 2):
                        if m < 4 * KQ:
                            add_square(SQ_KV + m)
                inverse(1)
                dve.wait_ge(rs_ready, 2)
                for t in range(TT):
                    e = E_V + t
                    if t < 2 * KQ:
                        scale(2 * KKV + t)
                    dve.wait_ge(out_hi, e + 1)
                    o = out[:, e % 2].rearrange("p a (h c n) -> p (a h) c n", c=2, n=VD)
                    dve.tensor_tensor(o[:, :, 1], bank[:, e % 4].rearrange("p (h n) -> p h n", n=VD),
                                      o[:, :, 0].bitcast(F32), ALU.subtract).then_inc(bank_free, 1)

                def turn(e, slot, rows, src, rot_src, cols):
                    dve.wait_ge(out_lo, e + (1 - E_Q))
                    dve.tensor_tensor(rot[PE_ROWS], rot_src, rope[ROT_ROWS, cols], ALU.mult).then_inc(rot_ready, 1)
                    last = dve.tensor_tensor(turned[rows, slot], src, rope[rows, cols], ALU.mult)
                    last.then_inc(bank_free, 1)
                    dve.wait_ge(rot_ready, e + (1 - E_Q))
                    dve.wait_ge(bank_free, e + 5)
                    dve.tensor_tensor(turned[PE_ROWS, slot], turned[PE_ROWS, slot], rot[PE_ROWS], ALU.add)\
                       .then_inc(turned_ready, 1)
                    dve.wait_ge(out_hi, e + 1)
                    dve.tensor_tensor(out[rows, slot, 1], turned[rows, slot], out[rows, slot, 0].bitcast(F32),
                                      ALU.subtract).then_inc(out_lo, 1)

                dve.sem_inc(out_lo, 2)
                with dve.Fori(0, HEADS) as h:
                    for blk in range(NB):
                        src = bank[:, blk]
                        dve.wait_ge(prod_done, h * NB + (8 + E_Q + blk + 1))
                        turn(h * NB + (E_Q + blk), blk % 2, slice(0, QK), src[0:QK], src[ROT_ROWS],
                             slice(blk * BLK, (blk + 1) * BLK))
                dve.wait_ge(kpe_in, 16)
                flat = scaled[:].rearrange("p a n -> p (a n)")
                for blk in range(NB):
                    cols = slice(blk * BLK, (blk + 1) * BLK)
                    turn(E_PE + blk, blk % 2, PE_ROWS, flat[PE_ROWS, cols], flat[ROT_ROWS, cols], cols)

            @block.tensor
            def _(pe):
                pe.wait_ge(const_in, 64)
                pe.wait_ge(const_set, 2)

                def norm(g, added):
                    pe.wait_ge(sq_added, added)
                    for t in range(TT):
                        last = pe.matmul(bank[:, SUMS, t:t + 1], acc_rs[:, t * P:(t + 1) * P], ones[:], start=True, stop=True)
                    last.then_inc(sums_done, 1)
                    pe.wait_ge(rstd_ready, g + 1)
                    for t in range(TT):
                        last = pe.matmul(bank[:, SPREAD + t // TPB, t % TPB * P:(t % TPB + 1) * P],
                                         rstd[:, g, t:t + 1].to_broadcast([P, P]), ident[:], start=True, stop=True)
                    last.then_inc(spread_done, 1)

                norm(0, SQ_KV)
                pe.wait_ge(wkv_ready, 2)
                pe.sem_inc(bank_free, 4)
                pe.sem_inc(prod_done, 8)
                pe.wait_ge(c_ready, 2 * KKV)
                for p in range(PAIRS):
                    for blk in range(NB):
                        e = p * NB + blk
                        pe.wait_ge(bank_free, e + 1)
                        cols, of = slice(blk * BLK, (blk + 1) * BLK), slice(p * P, (p + 1) * P)
                        for k in range(KKV):
                            last = three_products(pe, bank[:, e % 4], (wk_hi[:, k, of], wk_lo[:, k, of]),
                                                  (c_hi[:, KQ + k, cols], c_lo[:, KQ + k, cols]), k == 0, k == KKV - 1)
                        last.then_inc(prod_done, 1)
                norm(1, SQ_KV + 4 * KQ)
                for t in range(TT):
                    e = E_V + t
                    pe.wait_ge(bank_free, e + 1)
                    rows = slice(t * P, (t + 1) * P)
                    for k in range(KKV):
                        last = three_products(pe, bank[:, e % 4], (c_hi[:, KQ + k, rows], c_lo[:, KQ + k, rows]),
                                              (wv_hi[:, k], wv_lo[:, k]), k == 0, k == KKV - 1)
                    last.then_inc(prod_done, 1)
                pe.wait_ge(c_ready, 2 * N_LORA)
                with pe.Fori(0, HEADS // 2) as i:
                    for u in range(2):
                        pe.wait_ge(wq_ready, i * 2 + (u + 1))
                        for blk in range(NB):
                            pe.wait_ge(bank_free, i * (2 * NB) + (E_Q + u * NB + blk + 1))
                            cols = slice(blk * BLK, (blk + 1) * BLK)
                            for k in range(KQ):
                                last = three_products(pe, bank[:, blk], (wq_hi[:, u, k], wq_lo[:, u, k]),
                                                      (c_hi[:, k, cols], c_lo[:, k, cols]), k == 0, k == KQ - 1)
                            last.then_inc(prod_done, 1)
    clear_semaphores(nc, sems)


def attention_schedule():
    steps = []
    for b in range(NB):
        for r in range(TPB):
            steps.append([TPB * b + r, [(b - 1, j) for j in range(r * b, (r + 1) * b)], None, None])
    for j in range(0, TT, 2):
        steps.append([None, [(NB - 1, j), (NB - 1, j + 1)], None, None])
    steps += [[None, [], None, None], [None, [], None, None]]
    for s in range(len(steps) - 1):
        if steps[s][1] and steps[s][1][-1][1] == TPB * (steps[s][1][-1][0] + 1) - 1:
            steps[s + 1][2] = steps[s][1][-1][0]
            steps[s + 2][3] = steps[s][1][-1][0]
    return steps


def attention(nc, qT, knT, kpT, vTok, ident_d, oA):
    STEPS = attention_schedule()
    CHUNK_AT, CHUNKS = {}, 0
    PIECE_AT, PIECES = {}, 0
    TURN_AT, TURNS = {}, 0
    TILE_AT, TILES = {}, 0
    for i, tiles, _, o_block in STEPS:
        if i is not None:
            for c in range(i // TPB + 1):
                CHUNK_AT[i, c] = CHUNKS
                CHUNKS += 1
            for piece in range(i // (2 * TPB) + 1):
                PIECE_AT[i, piece] = PIECES
                PIECES += 1
        for tile in tiles:
            TURN_AT[tile], TILE_AT[tile] = TURNS, TILES
            TURNS += 1
            TILES += 1
        if o_block is not None:
            TURN_AT["o", o_block] = TURNS
            TURNS += 1

    def s_bank(i, c):
        b, r = i // TPB, i % TPB
        return c + (r if b == 0 else 2 * (r % 2) if b == 1 else 0)

    def pieces_before(i, c):
        need = 0
        for (t, piece), at in PIECE_AT.items():
            if t < i:
                b = t // TPB
                used = {s_bank(t, x) for x in range(2 * piece, min(2 * piece + 2, b + 1))}
                if s_bank(i, c) in used:
                    need = max(need, at + 1)
        return need

    def width(i, c):
        return BLK if c < i // TPB else (i % TPB + 1) * P

    sems = []
    with ExitStack() as ctx:
        def sb(name, shape, dt=F32):
            return ctx.enter_context(nc.sbuf_tensor(name, shape, dt))

        def sem(name):
            sems.append(nc.alloc_semaphore("c_" + name))
            return sems[-1]

        q_sb = sb("q_sb", [P, 2, 2, S], F32R)
        k_sb = sb("k_sb", [P, 2, 2, S], F32R)
        v_sb = sb("v_sb", [P, 2, TT, 2 * VD], F32R)
        probs = [sb("probs_even", [P, TPB, 3 * BLK]), sb("probs_odd", [P, TPB, 4 * BLK])]
        RING = 6
        pT = sb("pT", [P, RING, 2, BLK], F32R)
        oT = sb("oT", [P, BLK])
        o_lo = sb("o_lo", [P, TPB, VD])
        o_sum = sb("o_sum", [P, TPB, VD])
        o_out = sb("o_out", [P, 2, TPB, VD])
        ident = sb("ident_c", [P, P])
        early_q = sb("early_q", [1, P], F32R)
        late_k = sb("late_k", [1, P], F32R)
        mask_raw = sb("mask_raw", [1, 2, P])
        chunk_max = sb("chunk_max", [P, NB])
        row_max = sb("row_max", [P, 1])
        neg_max = sb("neg_max", [P, 2])
        sums = sb("sums", [P, NB, TPB, 2])
        total = sb("total", [P, TPB])
        inv = sb("inv", [P, TPB])
        scores = ctx.enter_context(nc.psum_tensor("scores", [P, 4, BLK], F32))
        turn = ctx.enter_context(nc.psum_tensor("turn", [P, 3, BLK], F32))
        o_acc = ctx.enter_context(nc.psum_tensor("o_acc", [P, BLK], F32))

        const_in = sem("const_in")
        const_set = sem("const_set")
        mask_set = sem("mask_set")
        kp_in = sem("kp_in")
        head_in = [sem("head_in0"), sem("head_in1")]
        head_done = sem("head_done")
        qk_done = sem("qk_done")
        chunk_max_done = sem("chunk_max_done")
        row_max_done = sem("row_max_done")
        max_ready = sem("max_ready")
        exp_done = sem("exp_done")
        turned = sem("turned")
        hi_ready = sem("hi_ready")
        turn_read = sem("turn_read")
        pv_done = sem("pv_done")
        o_copied = sem("o_copied")
        o_lo_ready = sem("o_lo_ready")
        total_ready = sem("total_ready")
        inv_ready = sem("inv_ready")
        o_sum_ready = sem("o_sum_ready")
        o_ready = sem("o_ready")
        o_stored = [sem("o_stored0"), sem("o_stored1")]

        with nc.Block() as block:

            @block.sync
            def _(sp):
                sp.dma_start(ident[:], ident_d).then_inc(const_in, 16)
                for u in range(2):
                    for part in range(2):
                        sp.dma_start(k_sb[PE_ROWS, u, part].bitcast(F32), kpT[part]).then_inc(kp_in, 16)
                def load_head(i, u):
                    for part in range(2):
                        sp.dma_start(q_sb[0:QK, u, part].bitcast(F32),
                                     qT[ds(i * 2 + u, 1), part].rearrange("o p n -> (o p) n")).then_inc(head_in[u], 16)
                        sp.dma_start(k_sb[0:NOPE, u, part].bitcast(F32),
                                     knT[ds(i, 1), part, u * NOPE:(u + 1) * NOPE].rearrange("o p n -> (o p) n"))\
                          .then_inc(head_in[u], 16)
                    sp.dma_start(v_sb[:, u].bitcast(F32),
                                 vTok[ds(i * 2 + u, 1)].rearrange("o p t n -> (o p) t n")).then_inc(head_in[u], 16)

                def store_head(i, u):
                    h = i * 2 + u
                    for b in range(NB):
                        sp.wait_ge(o_ready, h * NB + (b + 1))
                        sp.dma_start(oA[b * TPB:(b + 1) * TPB, :, ds(h * VD, VD)].rearrange("t p n -> p t n"),
                                     o_out[:, b % 2]).then_inc(o_stored[b % 2], 16)

                for u in range(2):
                    load_head(0, u)
                with sp.Fori(0, PAIRS - 1) as i:
                    for u in range(2):
                        store_head(i, u)
                        sp.wait_ge(head_done, i * 2 + (u + 1))
                        load_head(i + 1, u)
                for u in range(2):
                    store_head(PAIRS - 1, u)
                for s in o_stored:
                    sp.wait_ge(s, 16 + 16 * HEADS * NB // 2)

            @block.gpsimd
            def _(pool):
                pool.memset(mask_raw[:], 0.0).then_inc(mask_set, 1)
                pool.wait_ge(mask_set, 1)
                pool.memset(mask_raw[:, 0, 0:CHUNK], 1.0).then_inc(mask_set, 1)
                pool.memset(mask_raw[:, 1, CHUNK:P], MASKED).then_inc(mask_set, 1)
                pool.wait_ge(mask_set, 3)
                pool.tensor_scalar(early_q[:], mask_raw[:, 0], 1.0, None, ALU.mult).then_inc(const_set, 1)
                pool.tensor_scalar(late_k[:], mask_raw[:, 1], 1.0, None, ALU.mult).then_inc(const_set, 1)

            @block.scalar
            def _(act):
                def exponentials(h, i, piece):
                    b, r = i // TPB, i % TPB
                    first, end = 2 * piece, min(2 * piece + 2, b + 1)
                    n = min(end * BLK, (i + 1) * P) - first * BLK
                    bank = s_bank(i, 0)
                    src = scores[:].rearrange("p b n -> p (b n)")[:, (bank + first) * BLK:(bank + first) * BLK + n]
                    if piece == 0:
                        act.wait_ge(max_ready, h * TT + (i + 1))
                        if b >= 1 and r == 0:
                            last = (b - 2, TPB * (b - 1) - 1) if b >= 2 else None
                            if last:
                                act.wait_ge(turned, h * TURNS + (TURN_AT[last] + 1))
                    act.activation(probs[b % 2][:, r, first * BLK:first * BLK + n], src, ACT.Exp,
                                   bias=neg_max[:, i % 2:i % 2 + 1], scale=SCALE,
                                   accum_out=sums[:, b, r, piece:piece + 1]).then_inc(exp_done, 1)

                def hi_part(h, tile):
                    b, j = tile
                    r0 = max(0, j - TPB * b)
                    at = TILE_AT[tile]
                    act.wait_ge(turned, h * TURNS + (TURN_AT[tile] + 1))
                    act.wait_ge(pv_done, h * TILES + (at + 2))
                    act.activation(pT[:, at % RING, 0, r0 * P:], turn[:, TURN_AT[tile] % 3, r0 * P:], ACT.Copy)\
                       .then_inc(hi_ready, 1)

                act.sem_inc(exp_done, 1)
                act.sem_inc(o_copied, 1)
                with act.Fori(0, HEADS) as h:
                    for i, tiles, done, o_block in STEPS:
                        for tile in tiles[:1]:
                            hi_part(h, tile)
                        if i is not None:
                            exponentials(h, i, 0)
                        for tile in tiles[1:]:
                            hi_part(h, tile)
                        if i is not None and i >= 2 * TPB:
                            exponentials(h, i, 1)
                        if done is not None:
                            act.wait_ge(pv_done, h * TILES + (TILE_AT[done, TPB * (done + 1) - 1] + RING + 2))
                            if done > 0:
                                act.wait_ge(turned, h * TURNS + (TURN_AT["o", done - 1] + 1))
                            act.activation(oT[:], o_acc[:], ACT.Copy).then_inc(o_copied, 1)
                        if o_block is not None:
                            at = TURN_AT["o", o_block]
                            act.wait_ge(turned, h * TURNS + (at + 1))
                            if o_block > 0:
                                act.wait_ge(o_sum_ready, h * NB + o_block)
                            act.activation(o_lo[:], turn[:, at % 3].rearrange("p (t n) -> p t n", n=P)[:, :, VD:], ACT.Copy)\
                               .then_inc(o_lo_ready, 1)

            @block.vector
            def _(dve):
                def maxima(h, i):
                    b = i // TPB
                    for c in range(b + 1):
                        dve.wait_ge(qk_done, h * CHUNKS + (CHUNK_AT[i, c] + 1))
                        dve.reduce_max(chunk_max[:, c:c + 1], scores[:, s_bank(i, c), 0:width(i, c)], AX.X)\
                           .then_inc(chunk_max_done, 1)
                    dve.wait_ge(chunk_max_done, h * CHUNKS + (CHUNK_AT[i, b] + 1))
                    dve.reduce_max(row_max[:], chunk_max[:, 0:b + 1], AX.X).then_inc(row_max_done, 1)
                    dve.wait_ge(row_max_done, h * TT + (i + 1))
                    if i >= 2:
                        dve.wait_ge(exp_done, h * PIECES + (PIECE_AT[i - 2, (i - 2) // (2 * TPB)] + 2))
                    dve.tensor_scalar(neg_max[:, i % 2:i % 2 + 1], row_max[:], -SCALE, None, ALU.mult).then_inc(max_ready, 1)

                def lo_part(h, tile):
                    b, j = tile
                    r0 = max(0, j - TPB * b)
                    at = TILE_AT[tile]
                    dve.wait_ge(hi_ready, h * TILES + (at + 1))
                    dve.tensor_tensor(pT[:, at % RING, 1, r0 * P:], turn[:, TURN_AT[tile] % 3, r0 * P:],
                                      pT[:, at % RING, 0, r0 * P:].bitcast(F32), ALU.subtract).then_inc(turn_read, 1)

                def outputs(h, b):
                    at = TURN_AT["o", b]
                    n = h * NB + (b + 1)
                    if b >= 2:
                        dve.tensor_tensor(total[:], sums[:, b, :, 0], sums[:, b, :, 1], ALU.add).then_inc(total_ready, 1)
                    else:
                        dve.tensor_copy(total[:], sums[:, b, :, 0]).then_inc(total_ready, 1)
                    dve.wait_ge(total_ready, n)
                    dve.reciprocal(inv[:], total[:]).then_inc(inv_ready, 1)
                    dve.wait_ge(o_lo_ready, n)
                    dve.tensor_tensor(o_sum[:], turn[:, at % 3].rearrange("p (t n) -> p t n", n=P)[:, :, 0:VD], o_lo[:],
                                      ALU.add).then_inc(o_sum_ready, 1)
                    dve.wait_ge(o_sum_ready, n)
                    dve.wait_ge(inv_ready, n)
                    dve.sem_inc(turn_read, 1)
                    dve.wait_ge(o_stored[b % 2], h * 32 + (b // 2 * 16 + 16))
                    dve.tensor_tensor(o_out[:, b % 2], o_sum[:], inv[:].unsqueeze(2).to_broadcast([P, TPB, VD]), ALU.mult)\
                       .then_inc(o_ready, 1)

                dve.sem_inc(turn_read, 1)
                for s in o_stored:
                    dve.sem_inc(s, 16)
                with dve.Fori(0, HEADS) as h:
                    for i, tiles, _, o_block in STEPS:
                        if i is not None:
                            maxima(h, i)
                        for tile in tiles:
                            lo_part(h, tile)
                        if o_block is not None:
                            outputs(h, o_block)

            @block.tensor
            def _(pe):
                def queries(h, i, u):
                    b, r = i // TPB, i % TPB
                    rows = slice(i * P, (i + 1) * P)
                    q = q_sb[0:QK, u, 0, rows], q_sb[0:QK, u, 1, rows]
                    for c in range(b + 1):
                        n = width(i, c)
                        cols = slice(c * BLK, c * BLK + n)
                        dst = scores[:, s_bank(i, c), 0:n]
                        pe.wait_ge(exp_done, h * PIECES + (pieces_before(i, c) + 1))
                        diagonal = c == b
                        last = three_products(pe, dst, q, (k_sb[0:QK, u, 0, cols], k_sb[0:QK, u, 1, cols]), True, not diagonal)
                        if diagonal:
                            last = pe.matmul(dst[:, n - P:n], early_q[:], late_k[:], start=False, stop=True)
                        last.then_inc(qk_done, 1)

                def transposes(h, tile):
                    b, j = tile
                    at = TURN_AT[tile]
                    if at < 3:
                        pe.wait_ge(turn_read, h * TURNS + 1)
                    else:
                        pe.wait_ge(turn_read, h * TURNS + (at - 1))
                    if j == 0 or j >= TPB * b:
                        i = TPB * b + (TPB - 1 if j == 0 else j - TPB * b)
                        pe.wait_ge(exp_done, h * PIECES + (PIECE_AT[i, i // (2 * TPB)] + 2))
                    for r in range(max(0, j - TPB * b), TPB):
                        last = pe.transpose(turn[:, at % 3, r * P:(r + 1) * P], probs[b % 2][:, r, j * P:(j + 1) * P], ident[:])
                    last.then_inc(turned, 1)

                def values(h, tile, u):
                    b, j = tile
                    r0 = max(0, j - TPB * b)
                    at = TILE_AT[tile]
                    pe.wait_ge(turn_read, h * TURNS + (TURN_AT[tile] + 2))
                    if j == 0:
                        pe.wait_ge(o_copied, h * NB + (b + 1))
                    dst = o_acc[:, r0 * P:]
                    end = TPB * (b + 1) - 1
                    pe.matmul(dst, v_sb[:, u, j], pT[:, at % RING, 0, r0 * P:], start=j == 0, stop=False)
                    pe.matmul(dst, v_sb[:, u, j], pT[:, at % RING, 1, r0 * P:], start=False, stop=j == end)\
                      .then_inc(pv_done, 1)

                pe.wait_ge(const_in, 16)
                pe.wait_ge(const_set, 2)
                pe.wait_ge(kp_in, 64)
                pe.sem_inc(pv_done, 1 + RING)
                with pe.Fori(0, PAIRS) as pair:
                    for u in range(2):
                        h = pair * 2 + u
                        pe.wait_ge(head_in[u], pair * 80 + 80)
                        before = []
                        for i, tiles, _, o_block in STEPS:
                            if i is not None:
                                queries(h, i, u)
                            for tile in tiles:
                                transposes(h, tile)
                            for tile in before:
                                values(h, tile, u)
                            before = tiles
                            if o_block is not None:
                                at = TURN_AT["o", o_block]
                                pe.wait_ge(o_copied, h * NB + (o_block + 2))
                                pe.wait_ge(turn_read, h * TURNS + (at - 1))
                                for r in range(TPB):
                                    last = pe.transpose(turn[:, at % 3, r * P:(r + 1) * P], oT[:, r * P:(r + 1) * P], ident[:])
                                last.then_inc(turned, 1)
                                if o_block == NB - 1:
                                    pe.wait_ge(turned, h * TURNS + TURNS)
                                    pe.sem_inc(head_done, 1)
    clear_semaphores(nc, sems)


def merge_and_output(nc, x, oA, oB, gateTok, projT, w_branch_a, w_branch_b, w_out, g_post, ident_d, result):
    sems = []
    with ExitStack() as ctx:
        def sb(name, shape, dt=F32):
            return ctx.enter_context(nc.sbuf_tensor("e_" + name, shape, dt))

        def sem(name):
            sems.append(nc.alloc_semaphore("e_" + name))
            return sems[-1]

        wo_hi = sb("wo_hi", [P, KD, D], F32R)
        wo_lo = sb("wo_lo", [P, KD, D], F32R)
        wb_raw = sb("wb_raw", [P, 2, 2, KW, P])
        wb_hi = sb("wb_hi", [P, 2, 2, KW, P], F32R)
        wb_lo = sb("wb_lo", [P, 2, 2, KW, P], F32R)
        uT = sb("uT", [P, 2, KW, 2, BLK], F32R)
        mT = sb("mT", [P, KD, 2, BLK], F32R)
        o_in = sb("o_in", [P, 2, BLK])
        g_in = sb("g_in", [P, 2, BLK])
        sg = sb("sg", [P, 2, BLK])
        u = sb("u", [P, TPB, BLK])
        l_in = sb("l_in", [P, 2, BLK])
        part_a = sb("part_a", [P, BLK])
        part_b = sb("part_b", [P, BLK])
        x_in = sb("x_in", [P, D])
        y = sb("y", [P, 2, D])
        gain = sb("gain", [P, D])
        ident = sb("ident", [P, P])
        eps = sb("eps", [P, 1])
        ss = sb("ss", [P, 2])
        std = sb("std", [P, 1])
        rstd = sb("rstd", [P, 1])
        bank = ctx.enter_context(nc.psum_tensor("bankE", [P, 8, BLK], F32))
        B_TURN = 4

        const_in = sem("const_in")
        const_set = sem("const_set")
        wo_in = [sem("wo_in0"), sem("wo_in1")]
        wo_rounded = sem("wo_rounded")
        wo_ready = sem("wo_ready")
        wb_in = [sem("wb_in0"), sem("wb_in1")]
        wb_rounded = sem("wb_rounded")
        wb_ready = sem("wb_ready")
        og_in = [sem("og_in0"), sem("og_in1")]
        sg_ready = sem("sg_ready")
        gated = sem("gated")
        u_ready = sem("u_ready")
        turned = sem("turned")
        uT_hi = sem("uT_hi")
        uT_lo = sem("uT_lo")
        l_arrived = sem("l_arrived")
        l_ready = sem("l_ready")
        pair_done = sem("pair_done")
        pair_free = sem("pair_free")
        parts_ready = sem("parts_ready")
        m_ready = sem("m_ready")
        m_hi = sem("m_hi")
        m_lo = sem("m_lo")
        x_arrived = sem("x_arrived")
        ss_ready = sem("ss_ready")
        std_ready = sem("std_ready")
        rstd_ready = sem("rstd_ready")
        y_scaled = sem("y_scaled")
        y_ready = sem("y_ready")
        stored = [sem("stored0"), sem("stored1")]

        PAIRS_PB = KD + TPB
        Q = 2 * TPB
        EARLY = TPB + 2

        wa_v = w_branch_a.rearrange("(k p) n -> p k n", p=P)
        wb_v = w_branch_b.rearrange("(k p) n -> p k n", p=P)

        with nc.Block() as block:

            @block.sync
            def _(sp):
                sp.dma_start(ident[:], ident_d).then_inc(const_in, 16)
                sp.dma_start(gain[:], g_post[0:1, :].to_broadcast([P, D])).then_inc(const_in, 16)

                def load_gated(blk, q):
                    br, t = q // TPB, q % TPB
                    sp.dma_start(o_in[:, q % 2], (oA, oB)[br][ds(blk * TPB + t, 1)].rearrange("o p n -> (o p) n")).then_inc(og_in[q % 2], 16)
                    sp.dma_start(g_in[:, q % 2], gateTok[br, ds(blk * TPB + t, 1)].rearrange("o p n -> (o p) n")).then_inc(og_in[q % 2], 16)

                def next_gated(blk, q):
                    sp.wait_ge(u_ready, blk * Q + (q + 1))
                    load_gated(blk, q)

                def load_wb(m):
                    cols = slice(m * P, (m + 1) * P)
                    sp.dma_start(wb_raw[:, m % 2, 0], wa_v[:, :, cols]).then_inc(wb_in[m % 2], 16)
                    sp.dma_start(wb_raw[:, m % 2, 1], wb_v[:, :, cols]).then_inc(wb_in[m % 2], 16)

                def load_logits(blk, m):
                    for br in range(2):
                        sp.dma_start(l_in[:, br], projT[T_ML + br * KD + m, :, ds(blk * BLK, BLK)]).then_inc(l_arrived, 16)

                for s in stored:
                    sp.sem_inc(s, 16)
                load_wb(0)
                load_wb(1)
                load_logits(0, 0)
                for q in range(Q):
                    if q >= 2:
                        sp.wait_ge(u_ready, q + 1)
                        sp.wait_ge(wo_ready, q - 1)
                    load_gated(0, q)
                    sp.dma_start(y[:, q % 2], w_out[q * P:(q + 1) * P, :]).then_inc(wo_in[q % 2], 16)

                def block_io(blk, more):
                    for m in range(KD):
                        if more and m < EARLY:
                            next_gated(blk + 1, m)
                        if m < KD - 3 or more:
                            sp.wait_ge(wb_ready, blk * KD + (m + 2))
                            load_wb((m + 3) % KD)
                        if m < KD - 1 or more:
                            sp.wait_ge(parts_ready, blk * (2 * KD) + (2 * m + 2))
                            load_logits(blk + (m + 1) // KD, (m + 1) % KD)
                    for t in range(TPB):
                        sp.wait_ge(y_ready, blk * TPB + (t + 1))
                        sp.dma_start(result[ds(blk * BLK + t * P, P), :], y[:, t % 2]).then_inc(stored[t % 2], 16)
                        if t < TPB - 1 or more:
                            sp.dma_start(x_in[:], x[ds(blk * BLK + (t + 1) * P, P), :]).then_inc(x_arrived, 16)
                        if more and t == 0:
                            for q in range(EARLY, Q):
                                next_gated(blk + 1, q)

                sp.dma_start(x_in[:], x[0:P, :]).then_inc(x_arrived, 16)
                sp.wait_ge(wb_ready, 1)
                load_wb(2)
                with sp.Fori(0, NB - 1) as blk:
                    block_io(blk, True)
                block_io(NB - 1, False)
                for s in stored:
                    sp.wait_ge(s, 16 + 16 * TT // 2)

            @block.gpsimd
            def _(pool):
                pool.memset(eps[:], EPS).then_inc(const_set, 1)

                with pool.Fori(0, NB) as blk:
                    for m in range(KD):
                        pool.wait_ge(wb_rounded, blk * KD + (m + 1))
                        pool.tensor_tensor(wb_lo[:, m % 2], wb_raw[:, m % 2], wb_hi[:, m % 2].bitcast(F32), ALU.subtract)\
                            .then_inc(wb_ready, 1)

            @block.scalar
            def _(act):
                def sigmoid_of_gate(blk, q):
                    act.wait_ge(og_in[q % 2], blk * (16 * Q) + (q // 2 + 1) * 32)
                    act.wait_ge(u_ready, blk * Q + (q + 1))
                    act.activation(sg[:, q % 2], g_in[:, q % 2], ACT.Sigmoid).then_inc(sg_ready, 1)

                def round_weights(blk, m):
                    blk, m = blk + m // KD, m % KD
                    act.wait_ge(wb_in[m % 2], blk * (16 * KD) + (m // 2 + 1) * 32)
                    act.wait_ge(pair_done, blk * PAIRS_PB + (m + 5 if m >= 2 else m + 5 - TPB))
                    act.activation(wb_hi[:, m % 2], wb_raw[:, m % 2], ACT.Copy).then_inc(wb_rounded, 1)

                def round_uT(blk, br):
                    for k in range(KW):
                        act.wait_ge(turned, blk * (2 * KW) + (br * KW + k + 5))
                        if k == 0:
                            act.wait_ge(pair_done, blk * PAIRS_PB + (6 - TPB))
                        act.activation(uT[:, br, k, 0], bank[:, B_TURN + k], ACT.Copy).then_inc(uT_hi, 1)

                act.wait_ge(const_in, 32)
                act.wait_ge(const_set, 1)
                round_weights(0, 0)
                round_weights(0, 1)
                for q in range(Q):
                    sigmoid_of_gate(0, q)
                    act.wait_ge(wo_in[q % 2], 16 * (q // 2 + 1))
                    act.activation(wo_hi[:, q], y[:, q % 2], ACT.Copy).then_inc(wo_rounded, 1)
                    if q % TPB == TPB - 1:
                        round_uT(0, q // TPB)

                def block_work(blk, more):
                    for m in range(KD):
                        act.wait_ge(l_arrived, blk * (32 * KD) + (32 * m + 32))
                        act.activation(l_in[:], l_in[:], ACT.Sigmoid).then_inc(l_ready, 1)
                        if more and m < EARLY:
                            sigmoid_of_gate(blk + 1, m)
                        if m < KD - 2 or more:
                            round_weights(blk, m + 2)
                        act.wait_ge(m_ready, blk * KD + (m + 1))
                        if m == 0:
                            act.wait_ge(pair_done, blk * PAIRS_PB + 6)
                        act.activation(mT[:, m, 0], part_a[:], ACT.Copy).then_inc(m_hi, 1)
                    for t in range(TPB):
                        act.wait_ge(pair_done, blk * PAIRS_PB + (KD + t + 7))
                        slot = (KD + t) % 2
                        act.wait_ge(stored[t % 2], blk * 32 + (t // 2 + 1) * 16)
                        act.wait_ge(std_ready, blk * TPB + (t + 1))
                        act.activation(y[:, t % 2], bank[:, 2 * slot:2 * slot + 2].rearrange("p b n -> p (b n)"), ACT.Square,
                                       accum_out=ss[:, 0:1]).then_inc(ss_ready, 1)
                        act.wait_ge(ss_ready, blk * TPB + (t + 1))
                        act.wait_ge(rstd_ready, blk * TPB + (t + 1))
                        act.activation(std[:], ss[:, 0:1], ACT.Sqrt, bias=eps[:, 0:1], scale=1.0 / D).then_inc(std_ready, 1)
                        if more and t < 2:
                            round_uT(blk + 1, t)
                        if more and t == 0:
                            for q in range(EARLY, Q):
                                sigmoid_of_gate(blk + 1, q)

                with act.Fori(0, NB - 1) as blk:
                    block_work(blk, True)
                block_work(NB - 1, False)

            @block.vector
            def _(dve):
                def gate(blk, q):
                    dve.wait_ge(sg_ready, blk * Q + (q + 1))
                    dve.tensor_tensor(sg[:, q % 2], sg[:, q % 2], g_in[:, q % 2], ALU.mult).then_inc(gated, 1)
                    if q % TPB == 0:
                        dve.wait_ge(turned, blk * (2 * KW) + (q // TPB * KW + 4))
                    dve.wait_ge(gated, blk * Q + (q + 1))
                    dve.tensor_tensor(u[:, q % TPB], sg[:, q % 2], o_in[:, q % 2], ALU.mult).then_inc(u_ready, 1)

                def split_uT(blk, br):
                    for k in range(KW):
                        dve.wait_ge(uT_hi, blk * (2 * KW) + (br * KW + k + 1))
                        dve.tensor_tensor(uT[:, br, k, 1], bank[:, B_TURN + k], uT[:, br, k, 0].bitcast(F32), ALU.subtract)\
                           .then_inc(uT_lo, 1)

                dve.sem_inc(u_ready, 2)
                dve.sem_inc(rstd_ready, 1)
                dve.sem_inc(std_ready, 1)
                dve.wait_ge(const_in, 32)
                for q in range(Q):
                    gate(0, q)
                    dve.wait_ge(wo_rounded, q + 1)
                    dve.tensor_tensor(wo_lo[:, q], y[:, q % 2], wo_hi[:, q].bitcast(F32), ALU.subtract).then_inc(wo_ready, 1)
                    if q % TPB == TPB - 1:
                        split_uT(0, q // TPB)

                def block_work(blk, more):
                    for m in range(KD):
                        dve.wait_ge(pair_done, blk * PAIRS_PB + (m + 7))
                        dve.wait_ge(l_ready, blk * KD + (m + 1))
                        slot = m % 2
                        dve.wait_ge(m_lo, blk * KD + (m + 1))
                        dve.tensor_tensor(part_a[:], bank[:, 2 * slot], l_in[:, 0], ALU.mult).then_inc(parts_ready, 1)
                        dve.tensor_tensor(part_b[:], bank[:, 2 * slot + 1], l_in[:, 1], ALU.mult).then_inc(parts_ready, 1)
                        dve.wait_ge(parts_ready, blk * (2 * KD) + (2 * m + 2))
                        dve.sem_inc(pair_free, 1)
                        dve.tensor_tensor(part_a[:], part_a[:], part_b[:], ALU.add).then_inc(m_ready, 1)
                        if more and m < TPB:
                            gate(blk + 1, m)
                        dve.wait_ge(m_hi, blk * KD + (m + 1))
                        dve.tensor_tensor(mT[:, m, 1], part_a[:], mT[:, m, 0].bitcast(F32), ALU.subtract).then_inc(m_lo, 1)
                    for t in range(TPB):
                        slot = (KD + t) % 2
                        dve.wait_ge(std_ready, blk * TPB + (t + 2))
                        dve.reciprocal(rstd[:], std[:]).then_inc(rstd_ready, 1)
                        dve.wait_ge(rstd_ready, blk * TPB + (t + 2))
                        dve.scalar_tensor_tensor(y[:, t % 2], bank[:, 2 * slot:2 * slot + 2].rearrange("p b n -> p (b n)"), rstd[:, 0:1],
                                                 gain[:], ALU.mult, ALU.mult).then_inc(y_scaled, 1)
                        dve.wait_ge(y_scaled, blk * TPB + (t + 1))
                        dve.sem_inc(pair_free, 1)
                        dve.wait_ge(x_arrived, blk * (16 * TPB) + (16 * t + 16))
                        dve.tensor_tensor(y[:, t % 2], y[:, t % 2], x_in[:], ALU.add).then_inc(y_ready, 1)
                        if more and t < 2:
                            split_uT(blk + 1, t)
                        if more and t == 0:
                            for q in range(TPB, Q):
                                gate(blk + 1, q)

                dve.sem_inc(m_lo, 1)
                with dve.Fori(0, NB - 1) as blk:
                    block_work(blk, True)
                block_work(NB - 1, False)

            @block.tensor
            def _(pe):
                pe.wait_ge(const_in, 32)

                def turn_branch(blk, br):
                    pe.wait_ge(u_ready, blk * Q + (br * TPB + TPB + 2))
                    pe.wait_ge(uT_lo, blk * (2 * KW) + (br * KW + KW))
                    for k in range(KW):
                        for t in range(TPB):
                            last = pe.transpose(bank[:, B_TURN + k, t * P:(t + 1) * P], u[:, t, k * P:(k + 1) * P], ident[:])
                        last.then_inc(turned, 1)

                pe.sem_inc(turned, 4)
                pe.sem_inc(uT_lo, 4)
                pe.sem_inc(pair_done, 6)
                pe.sem_inc(pair_free, 2)
                turn_branch(0, 0)
                turn_branch(0, 1)

                def block_work(blk, more):
                    pe.wait_ge(uT_lo, blk * (2 * KW) + (2 * KW + 4))
                    for m in range(KD):
                        pe.wait_ge(wb_ready, blk * KD + (m + 1))
                        pe.wait_ge(pair_free, blk * PAIRS_PB + (m + 1))
                        slot = m % 2
                        for br in range(2):
                            for k in range(KW):
                                last = three_products(pe, bank[:, 2 * slot + br], (wb_hi[:, slot, br, k], wb_lo[:, slot, br, k]),
                                                      (uT[:, br, k, 0], uT[:, br, k, 1]), k == 0, k == KW - 1)
                        last.then_inc(pair_done, 1)
                    pe.wait_ge(m_lo, blk * KD + (KD + 1))
                    pe.wait_ge(wo_ready, KD)
                    for t in range(TPB):
                        slot = (KD + t) % 2
                        rows = slice(t * P, (t + 1) * P)
                        pe.wait_ge(pair_free, blk * PAIRS_PB + (KD + t + 1))
                        for half in range(2):
                            cols = slice(half * BLK, (half + 1) * BLK)
                            for k in range(KD):
                                last = three_products(pe, bank[:, 2 * slot + half], (mT[:, k, 0, rows], mT[:, k, 1, rows]),
                                                      (wo_hi[:, k, cols], wo_lo[:, k, cols]), k == 0, k == KD - 1)
                        last.then_inc(pair_done, 1)
                        if more and t < 2:
                            turn_branch(blk + 1, t)

                with pe.Fori(0, NB - 1) as blk:
                    block_work(blk, True)
                block_work(NB - 1, False)
    clear_semaphores(nc, sems)


def hybrid_mla_hgrn2_gated_merge(nc, x, g_pre, w_in, b_gate, g_q, w_uq, g_kv, w_ukv, lb_logits, g_hgrn,
                                 w_branch_a, w_branch_b, w_out, g_post, ident, rope, causal, result):
    def scratch(name, *shape):
        return nc.dram_tensor(name, shape, F32).ap()

    projT = scratch("projT", N_FM, P, S)
    gateTok = scratch("gateTok", 2, TT, P, W)
    hgTok = scratch("hgTok", TT, P, 2 * W)
    qT = scratch("qT", HEADS, 2, QK, S)
    knT = scratch("knT", PAIRS, 2, P, S)
    kpT = scratch("kpT", 2, ROPE, S)
    vTok = scratch("vTok", HEADS, P, TT, P)
    oA = scratch("oA", TT, P, W)
    oB = scratch("oB", TT, P, W)

    with nc.sbuf_tensor("hT_hi", [P, KD, S], F32R) as hT_hi, nc.sbuf_tensor("hT_lo", [P, KD, S], F32R) as hT_lo:
        input_projection(nc, hT_hi, hT_lo, x, g_pre, w_in, ident, projT, gateTok, hgTok)
        merge_logits_and_recurrence(nc, hT_hi, hT_lo, w_in, b_gate, lb_logits, g_hgrn, ident, causal, projT, hgTok, oB)
    latent_projections(nc, projT, g_q, g_kv, w_uq, w_ukv, rope, ident, qT, knT, kpT, vTok)
    attention(nc, qT, knT, kpT, vTok, ident, oA)
    merge_and_output(nc, x, oA, oB, gateTok, projT, w_branch_a, w_branch_b, w_out, g_post, ident, result)


_INS = ['x', 'g_pre', 'w_in', 'b_gate', 'g_q', 'w_uq', 'g_kv', 'w_ukv', 'lb_logits', 'g_hgrn',
        'w_branch_a', 'w_branch_b', 'w_out', 'g_post']


def _rope_table():
    half = ROPE // 2
    inv = np.float32(ROPE_THETA) ** (-np.arange(0, ROPE, 2, dtype=np.float32) / np.float32(ROPE))
    angle = (np.arange(S, dtype=np.float32)[:, None] * inv[None, :]).T
    return np.concatenate([np.ones((NOPE, S)), np.cos(angle), np.cos(angle), -np.sin(angle), np.sin(angle)]).astype(np.float32)


def _causal_mask():
    t = np.arange(P)
    return ((t[:, None] // HG_BLOCK == t[None, :] // HG_BLOCK) & (t[None, :] >= t[:, None])).astype(np.int32)


def kernel(**inputs):
    import concourse.bacc as bacc
    from concourse.bass_utils import run_bass_kernel_spmd

    nc = bacc.Bacc("TRN2", target_bir_lowering=False, num_devices=1)
    data = {name: inputs[name] for name in _INS}
    data = {name: a.reshape(a.shape[-2:]) for name, a in data.items()}
    data["ident"] = np.eye(P, dtype=np.float32)
    data["rope"] = _rope_table()
    data["causal"] = _causal_mask()
    arrays, args = {}, []
    for name, a in data.items():
        arrays[f"in_{name}_dram"] = np.ascontiguousarray(a)
        args.append(nc.dram_tensor(f"in_{name}_dram", a.shape, mybir.dt.from_np(a.dtype), kind="ExternalInput").ap())
    args.append(nc.dram_tensor("out_0_dram", (S, D), F32, kind="ExternalOutput").ap())
    hybrid_mla_hgrn2_gated_merge(nc, *args)
    r = run_bass_kernel_spmd(nc, [arrays], core_ids=[0])
    return r.results[0]["out_0_dram"].reshape(1, S, D)
```

```python
import numpy as np
import concourse.bass as bass
from concourse import mybir
from contextlib import ExitStack

F32 = mybir.dt.float32
F32R = mybir.dt.float32r
ALU = mybir.AluOpType
ACT = mybir.ActivationFunctionType
AX = mybir.AxisListType
ds = bass.ds

P = 128
S = 2048
D = 1024
KD = D // P
TT = S // P
BLK = 512
NB = S // BLK
TPB = BLK // P
EPS = 1e-6

HEADS = 8
NOPE, ROPE, VD = 64, 32, 64
QK = NOPE + ROPE
Q_LORA, KV_LORA = 768, 256
KQ, KKV = Q_LORA // P, KV_LORA // P
ROPE_THETA = 10000.0
CHUNK = 64
SCALE = 1.0 / float(np.sqrt(QK))
MASKED = -1.0e30

HG_BLOCK = 32
PAIRS = HEADS // 2
NCH = S // HG_BLOCK
W = HEADS * VD
KW = W // P

C_CQ = 0
C_PE = Q_LORA + KV_LORA
C_GA = C_PE + ROPE
C_HQ = C_GA + W
C_HF = C_HQ + W
C_HI = C_HF + W
C_GB = C_HI + W
C_ML = C_GB + W

N_LORA = KQ + KKV
T_HQ = N_LORA
T_HF = T_HQ + KW
T_PE = T_HF + KW
T_ML = T_PE + 1
N_FM = T_ML + 2 * KD

SEG_COLS = (C_HI, C_GA, C_GB)


def three_products(pe, out, a, b, first, last):
    (a_hi, a_lo), (b_hi, b_lo) = a, b
    pe.matmul(out, a_hi, b_hi, start=first, stop=False)
    pe.matmul(out, a_hi, b_lo, start=False, stop=False)
    return pe.matmul(out, a_lo, b_hi, start=False, stop=last)


def clear_semaphores(nc, sems):
    nc.all_engine_barrier()
    nc.clear_and_free_semaphores(sems)
    nc.all_engine_barrier()


def input_projection(nc, hT_hi, hT_lo, x, g_pre, w_in, ident_d, projT, gateTok, hgTok):
    sems = []
    with ExitStack() as ctx:
        def sb(name, shape, dt=F32):
            return ctx.enter_context(nc.sbuf_tensor(name, shape, dt))

        def sem(name):
            sems.append(nc.alloc_semaphore(name))
            return sems[-1]

        with nc.sbuf_tensor("x_even", [P, TPB, D], F32) as x_even, nc.sbuf_tensor("x_odd", [P, TPB, D], F32) as x_odd:
            x_tile = [x_even, x_odd]
        wt_hi = sb("wt_hi", [P, KD, W], F32R)
        wt_lo = sb("wt_lo", [P, KD, W], F32R)
        v_raw = sb("v_raw", [P, 2, D])
        w_raw = sb("w_raw", [P, 2, KD, P])
        w_hi = sb("w_hi", [P, 2, KD, P], F32R)
        w_lo = sb("w_lo", [P, 2, KD, P], F32R)
        wt_raw = sb("wt_raw", [P, 2, W])
        stage = sb("stage", [P, 4, BLK])
        ident = sb("ident", [P, P])
        gain = sb("gain", [P, KD])
        eps = sb("eps", [P, 1])
        ss = sb("ss", [P, TT])
        std = sb("std", [P, TT])
        rstd = sb("rstd", [P, TT])
        bank = ctx.enter_context(nc.psum_tensor("bankA", [P, 8, BLK], F32))

        const_in = sem("const_in")
        const_set = sem("const_set")
        waited_pool = sem("waited_pool")
        x_in = [[sem(f"x_in{g}{j}") for j in range(TPB)] for g in range(2)]
        sq_done = sem("sq_done")
        std_ready = sem("std_ready")
        rstd_ready = sem("rstd_ready")
        xn_ready = sem("xn_ready")
        xT_done = sem("xT_done")
        hT_hi_ready = sem("hT_hi_ready")
        hT_lo_ready = sem("hT_lo_ready")
        w_in_s = [sem("w_in0"), sem("w_in1")]
        w_hi_ready = sem("w_hi_ready")
        w_ready = sem("w_ready")
        raw_free = sem("raw_free")
        fm_done = sem("fm_done")
        bank_free = sem("bank_free")
        stored = [sem(f"stored{i}") for i in range(4)]
        wt_in = [sem("wt_in0"), sem("wt_in1")]
        wt_raw_free = sem("wt_raw_free")
        wt_hi_ready = sem("wt_hi_ready")
        wt_ready = sem("wt_ready")
        wt_used = sem("wt_used")
        tm_done = sem("tm_done")
        tm_free = sem("tm_free")
        v_hi = sem("v_hi")
        v_stored = [sem("v_stored0"), sem("v_stored1")]

        N_TILES = T_PE + 1
        B_XT = 4
        v_out = v_raw[:].bitcast(F32R).rearrange("p u (h c n) -> p u h c n", c=2, n=VD)

        w_v = w_in.rearrange("(k p) n -> p k n", p=P)

        with nc.Block() as block:

            @block.sync
            def _(sp):
                sp.dma_start(ident[:], ident_d).then_inc(const_in, 16)
                sp.dma_start(gain[:], g_pre.rearrange("o (k p) -> p (o k)", p=P),
                             allow_slow_non_contiguous=True).then_inc(const_in, 16)
                def load_tiles(n0, count, col0):
                    with sp.Fori(0, count // 2) as i:
                        for u in range(2):
                            sp.wait_ge(raw_free, i * 2 + (n0 + u + 1))
                            sp.dma_start(w_raw[:, u], w_v[:, :, ds(i * (2 * P) + (col0 + u * P), P)])\
                              .then_inc(w_in_s[u], 16)

                sp.sem_inc(raw_free, 2)
                for g in range(NB):
                    if g == 1:
                        load_tiles(0, 2, C_CQ)
                    if g >= 2:
                        sp.wait_ge(xT_done, 2 * g - 2)
                    for j in range(TPB):
                        t = g * TPB + j
                        sp.dma_start(x_tile[g % 2][:, j], x[t * P:(t + 1) * P, :]).then_inc(x_in[g % 2][j], 16)

                load_tiles(2, N_LORA - 2, C_CQ + 2 * P)
                load_tiles(T_HQ, 2 * KW, C_HQ)
                sp.wait_ge(raw_free, T_PE + 1)
                sp.dma_start(w_raw[:, 0, :, 0:QK], w_v[:, :, C_PE - NOPE:C_PE + ROPE]).then_inc(w_in_s[0], 16)
                sp.dma_start(w_raw[:, 0, :, QK:QK + 16], w_v[:, :, C_PE + 16:C_PE + 32]).then_inc(w_in_s[0], 16)
                sp.dma_start(w_raw[:, 0, :, QK + 16:P], w_v[:, :, C_PE:C_PE + 16]).then_inc(w_in_s[0], 16)
                sp.sem_inc(wt_raw_free, 2)
                for v in v_stored:
                    sp.sem_inc(v, 16)

                def load_segment(s):
                    with sp.Fori(0, KD // 2) as i:
                        for u in range(2):
                            sp.wait_ge(wt_raw_free, i * 2 + (s * KD + u + 1))
                            sp.dma_start(wt_raw[:, u], w_in[ds(i * (2 * P) + u * P, P), SEG_COLS[s]:SEG_COLS[s] + W])\
                              .then_inc(wt_in[u], 16)

                def store_values(first, end):
                    for t in range(first, end):
                        sp.wait_ge(tm_free, 8 + t + 1)
                        sp.dma_start(hgTok[t], v_raw[:, t % 2]).then_inc(v_stored[t % 2], 16)

                load_segment(0)
                store_values(0, TT // 2)
                load_segment(1)
                store_values(TT // 2, TT)
                load_segment(2)
                for v in v_stored:
                    sp.wait_ge(v, 16 + 16 * TT // 2)

            @block.gpsimd
            def _(pool):
                pool.memset(eps[:], EPS).then_inc(const_set, 1)

                def split_tile(u, n, arrived):
                    pool.wait_ge(w_in_s[u], arrived)
                    pool.wait_ge(fm_done, n * NB + NB)
                    pool.sem_inc(waited_pool, 1)
                    pool.tensor_scalar(w_hi[:, u], w_raw[:, u], 1.0, None, ALU.mult).then_inc(w_hi_ready, 1)
                    pool.wait_ge(w_hi_ready, n + 1)
                    pool.tensor_tensor(w_lo[:, u], w_raw[:, u], w_hi[:, u].bitcast(F32), ALU.subtract)\
                        .then_inc(w_ready, 1)
                    pool.wait_ge(w_ready, n + 1)
                    pool.sem_inc(raw_free, 1)

                with pool.Fori(0, T_PE // 2) as i:
                    for u in range(2):
                        split_tile(u, i * 2 + u, i * 16 + 16)
                split_tile(0, T_PE, T_PE // 2 * 16 + 48)

                pool.sem_inc(wt_used, KD - 1)
                with pool.Fori(0, len(SEG_COLS)) as s:
                    for k in range(KD):
                        u = k % 2
                        pool.wait_ge(wt_in[u], s * (KD // 2 * 16) + (k // 2 + 1) * 16)
                        if k < KD - 1:
                            pool.wait_ge(wt_used, s * (KD - 1) + (k + 1))
                        else:
                            pool.wait_ge(tm_done, s * TT + TT)
                        pool.sem_inc(waited_pool, 1)
                        pool.tensor_scalar(wt_hi[:, k], wt_raw[:, u], 1.0, None, ALU.mult).then_inc(wt_hi_ready, 1)
                        pool.wait_ge(wt_hi_ready, s * KD + (k + 1))
                        pool.tensor_tensor(wt_lo[:, k], wt_raw[:, u], wt_hi[:, k].bitcast(F32), ALU.subtract)\
                            .then_inc(wt_ready, 1)
                        pool.wait_ge(wt_ready, s * KD + (k + 1))
                        pool.sem_inc(wt_raw_free, 1)

            @block.scalar
            def _(act):
                act.wait_ge(const_in, 32)
                act.wait_ge(const_set, 1)

                def squares(g, j):
                    n = g * TPB + j
                    act.wait_ge(x_in[g % 2][j], g // 2 * 16 + 16)
                    act.activation(stage[:, 0:2].rearrange("p a n -> p (a n)"), x_tile[g % 2][:, j], ACT.Square,
                                   accum_out=ss[:, n:n + 1]).then_inc(sq_done, 1)
                    act.wait_ge(sq_done, n + 1)
                    act.activation(std[:, n:n + 1], ss[:, n:n + 1], ACT.Sqrt, bias=eps[:, 0:1], scale=1.0 / D)\
                       .then_inc(std_ready, 1)

                def round_half(g, half):
                    act.wait_ge(xT_done, 2 * g + half + 1)
                    for k in range(half * KD // 2, (half + 1) * KD // 2):
                        act.activation(hT_hi[:, k, g * BLK:(g + 1) * BLK], bank[:, B_XT + k % 4], ACT.Copy,
                                       scale=gain[:, k:k + 1]).then_inc(hT_hi_ready, 1)

                for g in range(NB + 1):
                    for half in range(2):
                        if g < NB:
                            for j in range(half * TPB // 2, (half + 1) * TPB // 2):
                                squares(g, j)
                        if g >= 1:
                            round_half(g - 1, half)

                def tile_out(n, u, func):
                    for blk in range(NB):
                        act.wait_ge(fm_done, n * NB + (8 + blk + 1))
                        act.wait_ge(stored[blk], n * 16 + 16)
                        src = bank[:, u * NB + blk]
                        act.activation(stage[:, blk], src, func).then_inc(bank_free, 1)
                        act.wait_ge(bank_free, n * NB + (8 + blk + 1))
                        act.dma_start(projT[ds(n, 1), :, blk * BLK:(blk + 1) * BLK].rearrange("o p n -> (o p) n"),
                                      stage[:, blk]).then_inc(stored[blk], 16)

                for s in stored:
                    act.sem_inc(s, 16)
                with act.Fori(0, T_HF // 2) as i:
                    for u in range(2):
                        tile_out(i * 2 + u, u, ACT.Copy)
                with act.Fori(0, (T_PE - T_HF) // 2) as i:
                    for u in range(2):
                        tile_out(i * 2 + (T_HF + u), u, ACT.Sigmoid)
                tile_out(T_PE, 0, ACT.Copy)

                for t in range(TT):
                    act.wait_ge(tm_done, TT + t + 1)
                    act.wait_ge(v_stored[t % 2], 16 * (t // 2 + 1))
                    act.activation(v_out[:, t % 2, :, 0], bank[:, t % 8].rearrange("p (h n) -> p h n", n=VD), ACT.Copy)\
                       .then_inc(v_hi, 1)
                with act.Fori(1, len(SEG_COLS)) as s:
                    for t in range(TT):
                        act.wait_ge(tm_done, s * TT + (TT + t + 1))
                        act.wait_ge(stored[t % 4], s * (TT // 4 * 16) + (N_TILES + t // 4 + 1 - TT // 4) * 16)
                        act.activation(stage[:, t % 4], bank[:, t % 8], ACT.Copy).then_inc(tm_free, 1)
                        act.wait_ge(tm_free, s * TT + (8 + t + 1))
                        act.dma_start(gateTok[ds(s - 1, 1), t].rearrange("o p n -> (o p) n"), stage[:, t % 4])\
                           .then_inc(stored[t % 4], 16)
                for s in stored:
                    act.wait_ge(s, 16 * (1 + N_TILES + (len(SEG_COLS) - 1) * TT // 4))

            @block.vector
            def _(dve):
                dve.wait_ge(const_in, 32)

                def normalise(g, j):
                    n = g * TPB + j
                    dve.wait_ge(std_ready, n + 1)
                    dve.reciprocal(rstd[:, n:n + 1], std[:, n:n + 1]).then_inc(rstd_ready, 1)
                    dve.wait_ge(rstd_ready, n + 1)
                    dve.tensor_scalar(x_tile[g % 2][:, j], x_tile[g % 2][:, j], rstd[:, n:n + 1], None, ALU.mult)\
                       .then_inc(xn_ready, 1)

                def lo_half(g, half):
                    for k in range(half * KD // 2, (half + 1) * KD // 2):
                        dve.wait_ge(hT_hi_ready, g * KD + (k + 1))
                        cols = slice(g * BLK, (g + 1) * BLK)
                        dve.scalar_tensor_tensor(hT_lo[:, k, cols], bank[:, B_XT + k % 4], gain[:, k:k + 1],
                                                 hT_hi[:, k, cols].bitcast(F32), ALU.mult, ALU.subtract).then_inc(hT_lo_ready, 1)

                for g in range(NB + 1):
                    for half in range(2):
                        if g < NB:
                            for j in range(half * TPB // 2, (half + 1) * TPB // 2):
                                normalise(g, j)
                        if g >= 1:
                            lo_half(g - 1, half)

                for t in range(TT):
                    dve.wait_ge(v_hi, t + 1)
                    dve.tensor_tensor(v_out[:, t % 2, :, 1], bank[:, t % 8].rearrange("p (h n) -> p h n", n=VD),
                                      v_out[:, t % 2, :, 0].bitcast(F32), ALU.subtract).then_inc(tm_free, 1)

            @block.tensor
            def _(pe):
                pe.wait_ge(const_in, 32)
                pe.sem_inc(bank_free, 8)
                pe.sem_inc(fm_done, 8)

                def turn_half(g, half):
                    pe.wait_ge(xn_ready, g * TPB + TPB)
                    for k in range(half * KD // 2, (half + 1) * KD // 2):
                        if g + half:
                            pe.wait_ge(hT_lo_ready, g * KD + (k - 3))
                        for j in range(TPB):
                            last = pe.transpose(bank[:, B_XT + k % 4, j * P:(j + 1) * P],
                                                x_tile[g % 2][:, j, k * P:(k + 1) * P], ident[:])
                    last.then_inc(xT_done, 1)

                def first_products(g, half):
                    pe.wait_ge(w_ready, 1)
                    pe.wait_ge(hT_lo_ready, g * KD + (half + 1) * KD // 2)
                    cols = slice(g * BLK, (g + 1) * BLK)
                    for k in range(half * KD // 2, (half + 1) * KD // 2):
                        last = three_products(pe, bank[:, g], (w_hi[:, 0, k], w_lo[:, 0, k]),
                                              (hT_hi[:, k, cols], hT_lo[:, k, cols]), k == 0, k == KD - 1)
                    if half == 1:
                        last.then_inc(fm_done, 1)

                for g in range(NB + 1):
                    for half in range(2):
                        if g < NB:
                            turn_half(g, half)
                        if g >= 1:
                            first_products(g - 1, half)

                def tile_products(u, n):
                    pe.wait_ge(w_ready, n + 1)
                    for blk in range(NB):
                        pe.wait_ge(bank_free, n * NB + (blk + 1))
                        cols = slice(blk * BLK, (blk + 1) * BLK)
                        for k in range(KD):
                            last = three_products(pe, bank[:, u * NB + blk], (w_hi[:, u, k], w_lo[:, u, k]),
                                                  (hT_hi[:, k, cols], hT_lo[:, k, cols]), k == 0, k == KD - 1)
                        last.then_inc(fm_done, 1)

                tile_products(1, 1)
                with pe.Fori(1, T_PE // 2) as i:
                    for u in range(2):
                        tile_products(u, i * 2 + u)
                tile_products(0, T_PE)

                pe.wait_ge(bank_free, 8 + N_TILES * NB)
                pe.sem_inc(tm_free, 8)
                pe.sem_inc(tm_done, TT)
                with pe.Fori(0, len(SEG_COLS)) as s:
                    for half in range(2):
                        for k in range(KD):
                            if half == 0:
                                pe.wait_ge(wt_ready, s * KD + (k + 1))
                            for b in range(8):
                                t = half * 8 + b
                                if k == 0:
                                    pe.wait_ge(tm_free, s * TT + (t + 1))
                                rows = slice(t * P, (t + 1) * P)
                                last = three_products(pe, bank[:, b], (hT_hi[:, k, rows], hT_lo[:, k, rows]),
                                                      (wt_hi[:, k], wt_lo[:, k]), k == 0, k == KD - 1)
                                if k == KD - 1:
                                    last.then_inc(tm_done, 1)
                                elif half == 1 and b == 7:
                                    last.then_inc(wt_used, 1)
    clear_semaphores(nc, sems)


def merge_logits_and_recurrence(nc, hT_hi, hT_lo, w_in, b_gate, lb_logits, g_hgrn, ident_d, causal_d, projT, hgTok, oB):
    UNITS = PAIRS * NB
    CPB = BLK // HG_BLOCK
    CPT = P // HG_BLOCK
    AT_SCORES, AT_TURN_K, AT_UPDATES, AT_OUTPUTS, AT_TURN = 0, 5, 8, 18, (22, 26)
    HALVES = (slice(0, 64), slice(64, P))

    sems = []
    with ExitStack() as ctx:
        def sb(name, shape, dt=F32):
            return ctx.enter_context(nc.sbuf_tensor("d_" + name, shape, dt))

        def sem(name):
            sems.append(nc.alloc_semaphore("d_" + name))
            return sems[-1]

        w_raw = sb("w_raw", [P, KD, P])
        w_hi = sb("w_hi", [P, KD, P], F32R)
        w_lo = sb("w_lo", [P, KD, P], F32R)
        stage = sb("stage", [P, 2, BLK])
        q_in = sb("q_in", [P, BLK])
        f_in = sb("f_in", [P, BLK])
        e = sb("e", [P, BLK])
        cum = sb("cum", [P, BLK])
        k_end = sb("k_end", [P, BLK])
        qd = sb("qd", [P, 2, BLK], F32R)
        ki = sb("ki", [P, 2, BLK], F32R)
        ket = sb("ket", [P, 2, BLK], F32R)
        v = sb("v", [P, TPB, 2, 2 * VD], F32R)
        masked = sb("masked", [P, BLK])
        a_hl = sb("a_hl", [P, 2, 2, BLK], F32R)
        states = sb("states", [P, VD, CPB + 1])
        decay = sb("decay", [P, VD, CPB + 1])
        s_hl = sb("s_hl", [P, CPB, 2, VD], F32R)
        o_fm = sb("o_fm", [P, BLK])
        o_lo = sb("o_lo", [P, 2, TPB, VD])
        o_sum = sb("o_sum", [P, 2, TPB, VD])
        o_out = sb("o_out", [P, TPB, 2, VD])
        mean = sb("mean", [P, 2 * TPB])
        logm = sb("logm", [P, 2 * TPB])
        rms = sb("rms", [P, 2 * TPB])
        ident = sb("ident", [P, P])
        causal = sb("causal", [P, P], mybir.dt.int32)
        inside = sb("inside", [P, BLK], mybir.dt.bfloat16)
        bias = sb("bias", [P, 2 * KD])
        gain = sb("gain", [P, VD])
        eps = sb("eps", [P, 1])
        lb_in = sb("lb_in", [P, 2, PAIRS])
        lb_tmp = sb("lb_tmp", [P, 3, PAIRS])
        lb = sb("lb", [P, PAIRS])
        span = sb("span", [P, PAIRS])
        bank = ctx.enter_context(nc.psum_tensor("bankD", [P, 8, BLK], F32))
        B_SCORE, B_TURN, B_UPD = 2, (4, 7), 4

        const_in = sem("const_in")
        const_set = sem("const_set")
        waited_act = sem("waited_act")
        waited_dve = sem("waited_dve")
        lb_step = sem("lb_step")
        lb_exp = sem("lb_exp")
        w_arrived = sem("w_arrived")
        w_hi_done = sem("w_hi_done")
        w_split = sem("w_split")
        half_used = sem("half_used")
        prod_done = sem("prod_done")
        logits_out = sem("logits_out")
        stored = [sem("stored0"), sem("stored1")]
        qf_in = sem("qf_in")
        v_in = sem("v_in")
        f_ready = sem("f_ready")
        ln_ready = sem("ln_ready")
        k_ready = sem("k_ready")
        cum_ready = sem("cum_ready")
        up_ready = sem("up_ready")
        decay_ready = sem("decay_ready")
        q_ready = sem("q_ready")
        diff_ready = sem("diff_ready")
        qd_hi = sem("qd_hi")
        qd_lo = sem("qd_lo")
        down_ready = sem("down_ready")
        kd_ready = sem("kd_ready")
        ki_hi = sem("ki_hi")
        ki_lo = sem("ki_lo")
        to_end_ready = sem("to_end_ready")
        k_end_ready = sem("k_end_ready")
        scores_done = sem("scores_done")
        ket_turned = sem("ket_turned")
        ket_hi = sem("ket_hi")
        ket_lo = sem("ket_lo")
        masked_ready = sem("masked_ready")
        a_hi = sem("a_hi")
        a_lo = sem("a_lo")
        carried = sem("carried")
        updated = sem("updated")
        upd_act = sem("upd_act")
        upd_dve = sem("upd_dve")
        states_ready = sem("states_ready")
        s_hi = sem("s_hi")
        s_lo = sem("s_lo")
        o_done = sem("o_done")
        o_fm_ready = sem("o_fm_ready")
        o_turned = sem("o_turned")
        o_lo_ready = sem("o_lo_ready")
        o_sum_ready = sem("o_sum_ready")
        sq_ready = sem("sq_ready")
        mean_ready = sem("mean_ready")
        log_ready = sem("log_ready")
        rms_ready = sem("rms_ready")
        normed = sem("normed")
        o_ready = sem("o_ready")
        o_stored = sem("o_stored")

        w_v = w_in.rearrange("(k p) n -> p k n", p=P)

        def chunk_c(rows, c):
            return states[rows, :, 1:].rearrange("p v (t c) -> p c t v", c=CPT)[:, c]

        def by_chunk(ap):
            return ap.rearrange("p (c n) -> p c n", n=HG_BLOCK)

        def is_first(n):
            return isinstance(n, int) and n == 0

        with nc.Block() as block:

            @block.sync
            def _(sp):
                sp.dma_start(ident[:], ident_d).then_inc(const_in, 16)
                sp.dma_start(causal[:], causal_d).then_inc(const_in, 16)
                sp.dma_start(bias[:], b_gate.rearrange("o (k p) -> p (o k)", p=P),
                             allow_slow_non_contiguous=True).then_inc(const_in, 16)
                for row in range(2):
                    sp.dma_start(lb_in[:, row], lb_logits[row:row + 1].rearrange("o (h p) -> p (o h)", p=P),
                                 allow_slow_non_contiguous=True).then_inc(const_in, 16)
                sp.dma_start(gain[:], g_hgrn[0:1, :].to_broadcast([P, VD])).then_inc(const_in, 16)

                def load_weights(n):
                    sp.dma_start(w_raw[:], w_v[:, :, ds(n * P + C_ML, P)]).then_inc(w_arrived, 16)

                def load_qf(pair, blk):
                    cols = slice(blk * BLK, (blk + 1) * BLK)
                    for dst, t in ((q_in, T_HQ), (f_in, T_HF)):
                        sp.dma_start(dst[:], projT[ds(pair + t, 1), :, cols].rearrange("o p n -> (o p) n")).then_inc(qf_in, 16)

                def load_v(pair, blk):
                    sp.dma_start(v[:].rearrange("p t h n -> p t (h n)").bitcast(F32),
                                 hgTok[blk * TPB:(blk + 1) * TPB, :, ds(pair * (4 * VD), 4 * VD)].rearrange("t p n -> p t n"))\
                      .then_inc(v_in, 16)

                def store_o(pair, blk, n):
                    sp.wait_ge(o_ready, n + 1)
                    sp.dma_start(oB[blk * TPB:(blk + 1) * TPB, :, ds(pair * P, P)].rearrange("t p n -> p t n"),
                                 o_out[:].rearrange("p t h n -> p t (h n)")).then_inc(o_stored, 16)

                def unit(pair, blk, after_pair, after_blk, n):
                    sp.wait_ge(w_split, n * 2 + 2)
                    load_weights(n + 1)
                    sp.wait_ge(qd_lo, n + 1)
                    sp.wait_ge(k_end_ready, n + 1)
                    load_qf(after_pair, after_blk)
                    sp.wait_ge(o_done, n * 2 + 2)
                    load_v(after_pair, after_blk)
                    store_o(pair, blk, n)

                sp.sem_inc(o_stored, 16)
                load_weights(0)
                load_qf(0, 0)
                load_v(0, 0)
                with sp.Fori(0, PAIRS - 1) as pair:
                    for blk in range(NB):
                        unit(pair, blk, pair + (blk + 1) // NB, (blk + 1) % NB, pair * NB + blk)
                for blk in range(NB - 1):
                    unit(PAIRS - 1, blk, PAIRS - 1, blk + 1, (PAIRS - 1) * NB + blk)
                store_o(PAIRS - 1, NB - 1, UNITS - 1)
                sp.wait_ge(o_stored, 16 + 16 * UNITS)

            @block.gpsimd
            def _(pool):
                pool.memset(eps[:], EPS).then_inc(const_set, 1)
                pool.memset(masked[:], 0.0).then_inc(const_set, 1)
                pool.memset(decay[:], 0.0).then_inc(const_set, 1)
                pool.memset(inside[:], 1.0).then_inc(const_set, 1)
                pool.wait_ge(const_set, 4)
                pool.memset(by_chunk(inside[:])[:, :, 0:1], 0.0).then_inc(const_set, 1)

                def split_weights(n):
                    for half in range(2):
                        ks = slice(half * KD // 2, (half + 1) * KD // 2)
                        pool.wait_ge(w_hi_done, n * 2 + (half + 1))
                        pool.tensor_tensor(w_lo[:, ks], w_raw[:, ks], w_hi[:, ks].bitcast(F32), ALU.subtract)\
                            .then_inc(w_split, 1)

                def split_unit(n):
                    pool.wait_ge(ki_hi, n + 1)
                    pool.tensor_tensor(ki[:, 1], e[:], ki[:, 0].bitcast(F32), ALU.subtract).then_inc(ki_lo, 1)
                    pool.wait_ge(qd_hi, n + 1)
                    pool.tensor_tensor(qd[:, 1], q_in[:], qd[:, 0].bitcast(F32), ALU.subtract).then_inc(qd_lo, 1)

                split_weights(0)
                split_unit(0)
                with pool.Fori(0, UNITS - 1) as n:
                    split_unit(n + 1)
                    split_weights(n + 1)

            @block.scalar
            def _(act):
                act.wait_ge(const_in, 96)
                act.wait_ge(const_set, 5)
                act.wait_ge(lb_step, 2)
                act.activation(lb_in[:], lb_in[:], ACT.Exp).then_inc(lb_exp, 1)

                def logits(n, j):
                    act.wait_ge(prod_done, n * NB + (4 + j + 1))
                    act.wait_ge(stored[j % 2], n * 32 + (j // 2 + 1) * 16)
                    act.sem_inc(waited_act, 1)
                    act.activation(stage[:, j % 2], bank[:, j % 2], ACT.Identity, bias=bias[:, ds(n, 1)]).then_inc(logits_out, 1)
                    act.wait_ge(logits_out, n * NB + (2 + j + 1))
                    act.dma_start(projT[ds(n + T_ML, 1), :, j * BLK:(j + 1) * BLK].rearrange("o p n -> (o p) n"), stage[:, j % 2])\
                       .then_inc(stored[j % 2], 16)

                for s in stored:
                    act.sem_inc(s, 16)

                def log_f(n):
                    act.wait_ge(f_ready, n + 1)
                    act.wait_ge(ki_lo, n + 1)
                    act.activation(e[:], f_in[:], ACT.Ln).then_inc(ln_ready, 1)

                def exp_up(n):
                    act.wait_ge(cum_ready, n + 1)
                    act.activation(e[:], cum[:], ACT.Exp).then_inc(up_ready, 1)

                def factors(n):
                    act.wait_ge(up_ready, n + 1)
                    if not is_first(n):
                        act.wait_ge(states_ready, n)
                    act.activation(decay[:, :, 1:], by_chunk(e[:])[:, :, HG_BLOCK - 1].unsqueeze(1).to_broadcast([P, VD, CPB]),
                                   ACT.Copy).then_inc(decay_ready, 1)
                    act.wait_ge(q_ready, n + 1)
                    act.wait_ge(decay_ready, n + 1)
                    act.activation(e[:], cum[:], ACT.Exp, scale=-1.0).then_inc(down_ready, 1)
                    act.wait_ge(diff_ready, n + 1)
                    act.activation(k_end[:], k_end[:], ACT.Exp).then_inc(to_end_ready, 1)

                def round_unit(n):
                    act.wait_ge(kd_ready, n + 1)
                    if not is_first(n):
                        act.wait_ge(scores_done, n * 2)
                    act.activation(ki[:, 0], e[:], ACT.Copy).then_inc(ki_hi, 1)
                    act.wait_ge(q_ready, n + 1)
                    if not is_first(n):
                        act.wait_ge(o_done, n * 2)
                    act.activation(qd[:, 0], q_in[:], ACT.Copy).then_inc(qd_hi, 1)

                def unit(n, more):
                    for hh in range(2):
                        act.wait_ge(masked_ready, n * 2 + (hh + 1))
                        act.activation(a_hl[:, hh, 0], masked[:], ACT.Copy).then_inc(a_hi, 1)
                        if hh == 0:
                            act.wait_ge(ket_turned, n + 1)
                            act.activation(ket[:, 0], bank[:, B_TURN[0]], ACT.Copy).then_inc(ket_hi, 1)
                    if more:
                        log_f(n + 1)
                    logits(n, 0)
                    act.wait_ge(carried, n + 1)
                    for c in range(CPT):
                        act.wait_ge(updated, n * CPT + (c + 1))
                        act.activation(chunk_c(HALVES[1], c),
                                       bank[HALVES[1], B_UPD + c].rearrange("p (t h v) -> p t h v", h=2, v=VD)[:, :, 1],
                                       ACT.Copy).then_inc(upd_act, 1)
                    act.wait_ge(states_ready, n + 1)
                    act.activation(s_hl[:, :, 0], states[:, :, 0:CPB].rearrange("p v c -> p c v"), ACT.Copy).then_inc(s_hi, 1)
                    if more:
                        exp_up(n + 1)
                    logits(n, 1)
                    if more:
                        factors(n + 1)
                    for hh in range(2):
                        act.wait_ge(o_done, n * 2 + (hh + 1))
                        act.wait_ge(o_turned, n * 2 + (hh + 1))
                        act.activation(o_fm[:], bank[:, B_SCORE + hh], ACT.Copy).then_inc(o_fm_ready, 1)
                    if more:
                        round_unit(n + 1)
                    logits(n, 2)
                    for hh in range(2):
                        act.wait_ge(o_turned, n * 2 + (hh + 2))
                        act.activation(o_lo[:, hh], bank[:, B_TURN[hh]].rearrange("p (t n) -> p t n", n=P)[:, :, VD:], ACT.Copy)\
                           .then_inc(o_lo_ready, 1)
                    act.wait_ge(mean_ready, n + 1)
                    act.activation(logm[:], mean[:], ACT.Ln, bias=eps[:, 0:1], scale=1.0 / VD).then_inc(log_ready, 1)
                    act.wait_ge(log_ready, n + 1)
                    act.activation(rms[:], logm[:], ACT.Exp, scale=-0.5).then_inc(rms_ready, 1)
                    logits(n, 3)

                log_f(0)
                exp_up(0)
                factors(0)
                round_unit(0)
                with act.Fori(0, UNITS - 1) as n:
                    unit(n, True)
                unit(UNITS - 1, False)
                for s in stored:
                    act.wait_ge(s, 16 + 16 * UNITS * NB // 2)

            @block.vector
            def _(dve):
                dve.wait_ge(const_in, 96)
                dve.tensor_tensor(lb_tmp[:, 0], lb_in[:, 0], lb_in[:, 1], ALU.max).then_inc(lb_step, 1)
                dve.wait_ge(lb_step, 1)
                dve.tensor_tensor(lb_in[:], lb_in[:], lb_tmp[:, 0:1].to_broadcast([P, 2, PAIRS]), ALU.subtract).then_inc(lb_step, 1)
                dve.wait_ge(lb_exp, 1)
                dve.tensor_tensor(lb_tmp[:, 1], lb_in[:, 0], lb_in[:, 1], ALU.add).then_inc(lb_step, 1)
                dve.wait_ge(lb_step, 3)
                dve.reciprocal(lb_tmp[:, 2], lb_tmp[:, 1]).then_inc(lb_step, 1)
                dve.wait_ge(lb_step, 4)
                dve.tensor_tensor(lb[:], lb_in[:, 0], lb_tmp[:, 2], ALU.mult).then_inc(lb_step, 1)
                dve.wait_ge(lb_step, 5)
                dve.tensor_scalar(span[:], lb[:], -1.0, 1.0, ALU.mult, ALU.add).then_inc(lb_step, 1)
                dve.wait_ge(lb_step, 6)
                dve.wait_ge(const_set, 5)

                dve.sem_inc(ki_lo, 1)

                def round_weights(n, half):
                    if half == 0:
                        dve.wait_ge(w_arrived, n * 16 + 16)
                        dve.wait_ge(half_used, n + 1)
                    else:
                        dve.wait_ge(prod_done, n * NB + NB)
                    ks = slice(half * KD // 2, (half + 1) * KD // 2)
                    dve.tensor_copy(w_hi[:, ks], w_raw[:, ks]).then_inc(w_hi_done, 1)

                def lower_bounded(pair, n):
                    dve.wait_ge(qf_in, n * 32 + 32)
                    dve.tensor_scalar(f_in[:], f_in[:], span[:, ds(pair, 1)], lb[:, ds(pair, 1)], ALU.mult, ALU.add)\
                       .then_inc(f_ready, 1)

                def accumulated(n):
                    dve.wait_ge(ln_ready, n + 1)
                    dve.tensor_tensor_scan(cum[:], inside[:], e[:], 0.0, ALU.mult, ALU.add).then_inc(cum_ready, 1)
                    dve.tensor_scalar(f_in[:], f_in[:], -1.0, 1.0, ALU.mult, ALU.add).then_inc(k_ready, 1)
                    dve.wait_ge(cum_ready, n + 1)
                    if not is_first(n):
                        dve.wait_ge(ket_turned, n)
                    dve.tensor_tensor(by_chunk(k_end[:]), by_chunk(cum[:])[:, :, HG_BLOCK - 1:].to_broadcast([P, CPB, HG_BLOCK]),
                                      by_chunk(cum[:]), ALU.subtract).then_inc(diff_ready, 1)

                def decayed_q(n):
                    dve.wait_ge(up_ready, n + 1)
                    dve.tensor_tensor(q_in[:], q_in[:], e[:], ALU.mult).then_inc(q_ready, 1)

                def decayed_k(n):
                    dve.wait_ge(k_ready, n + 1)
                    dve.wait_ge(down_ready, n + 1)
                    dve.tensor_tensor(e[:], f_in[:], e[:], ALU.mult).then_inc(kd_ready, 1)
                    dve.wait_ge(to_end_ready, n + 1)
                    dve.tensor_tensor(k_end[:], f_in[:], k_end[:], ALU.mult).then_inc(k_end_ready, 1)

                def unit(blk, n, after_pair, more):
                    for hh in range(2):
                        dve.wait_ge(scores_done, n * 2 + (hh + 1))
                        if hh == 1:
                            dve.wait_ge(a_lo, n * 2 + 1)
                        dve.sem_inc(waited_dve, 1)
                        dve.copy_predicated(masked[:].rearrange("p (t n) -> p t n", n=P),
                                            causal[:].unsqueeze(1).to_broadcast([P, TPB, P]),
                                            bank[:, B_SCORE + hh].rearrange("p (t n) -> p t n", n=P)).then_inc(masked_ready, 1)
                        if hh == 1:
                            dve.wait_ge(ket_hi, n + 1)
                            dve.tensor_tensor(ket[:, 1], bank[:, B_TURN[0]], ket[:, 0].bitcast(F32), ALU.subtract).then_inc(ket_lo, 1)
                        dve.wait_ge(a_hi, n * 2 + (hh + 1))
                        dve.tensor_tensor(a_hl[:, hh, 1], masked[:], a_hl[:, hh, 0].bitcast(F32), ALU.subtract).then_inc(a_lo, 1)
                    if more:
                        lower_bounded(after_pair, n + 1)
                    if blk == 0:
                        dve.memset(states[:, :, 0:1], 0.0).then_inc(carried, 1)
                    else:
                        dve.tensor_copy(states[:, :, 0:1], states[:, :, CPB:]).then_inc(carried, 1)
                    dve.wait_ge(carried, n + 1)
                    for c in range(CPT):
                        dve.wait_ge(updated, n * CPT + (c + 1))
                        dve.tensor_copy(chunk_c(HALVES[0], c),
                                        bank[HALVES[0], B_UPD + c].rearrange("p (t h v) -> p t h v", h=2, v=VD)[:, :, 0])\
                           .then_inc(upd_dve, 1)
                    dve.wait_ge(decay_ready, n + 1)
                    dve.wait_ge(upd_act, n * CPT + CPT)
                    dve.wait_ge(upd_dve, n * CPT + CPT)
                    flat = states[:].rearrange("p v c -> p (v c)")
                    dve.tensor_tensor_scan(flat, decay[:].rearrange("p v c -> p (v c)"), flat, 0.0, ALU.mult, ALU.add)\
                       .then_inc(states_ready, 1)
                    if more:
                        accumulated(n + 1)
                    dve.wait_ge(s_hi, n + 1)
                    dve.tensor_tensor(s_hl[:, :, 1], states[:, :, 0:CPB].rearrange("p v c -> p c v"), s_hl[:, :, 0].bitcast(F32),
                                      ALU.subtract).then_inc(s_lo, 1)
                    if more:
                        decayed_q(n + 1)
                        decayed_k(n + 1)
                    for hh in range(2):
                        dve.wait_ge(o_lo_ready, n * 2 + (hh + 1))
                        dve.tensor_tensor(o_sum[:, hh], bank[:, B_TURN[hh]].rearrange("p (t n) -> p t n", n=P)[:, :, 0:VD],
                                          o_lo[:, hh], ALU.add).then_inc(o_sum_ready, 1)
                    if more:
                        round_weights(n + 1, 0)
                    dve.wait_ge(o_sum_ready, n * 2 + 4)
                    dve.tensor_tensor(o_lo[:], o_sum[:], o_sum[:], ALU.mult).then_inc(sq_ready, 1)
                    dve.wait_ge(sq_ready, n + 1)
                    dve.reduce_sum(mean[:].rearrange("p (h t) -> p h t", h=2), o_lo[:], AX.X).then_inc(mean_ready, 1)
                    dve.wait_ge(rms_ready, n + 1)
                    dve.tensor_tensor(o_sum[:].rearrange("p h t n -> p (h t) n"), o_sum[:].rearrange("p h t n -> p (h t) n"),
                                      rms[:].unsqueeze(2).to_broadcast([P, 2 * TPB, VD]), ALU.mult).then_inc(normed, 1)
                    dve.wait_ge(normed, n + 1)
                    dve.wait_ge(o_stored, n * 16 + 16)
                    dve.tensor_tensor(o_out[:].rearrange("p t h n -> p h t n"), o_sum[:],
                                      gain[:].unsqueeze(1).unsqueeze(1).to_broadcast([P, 2, TPB, VD]), ALU.mult).then_inc(o_ready, 1)
                    if more:
                        round_weights(n + 1, 1)

                round_weights(0, 0)
                round_weights(0, 1)
                lower_bounded(0, 0)
                accumulated(0)
                decayed_q(0)
                decayed_k(0)
                with dve.Fori(0, PAIRS - 1) as pair:
                    for blk in range(NB):
                        unit(blk, pair * NB + blk, pair + (blk + 1) // NB, True)
                for blk in range(NB):
                    unit(blk, (PAIRS - 1) * NB + blk, PAIRS - 1, blk < NB - 1)

            @block.tensor
            def _(pe):
                pe.wait_ge(const_in, 96)

                def scores(n, part):
                    hh, rows = part // 2, HALVES[part // 2]
                    if part == 0:
                        pe.wait_ge(qd_lo, n + 1)
                        pe.wait_ge(ki_lo, n + 2)
                    for t in range(part % 2 * 2, part % 2 * 2 + 2):
                        cols = slice(t * P, (t + 1) * P)
                        last = three_products(pe, bank[:, B_SCORE + hh, cols], (ki[rows, 0, cols], ki[rows, 1, cols]),
                                              (qd[rows, 0, cols], qd[rows, 1, cols]), True, True)
                    if part % 2:
                        last.then_inc(scores_done, 1)

                def turn_k(n):
                    pe.wait_ge(k_end_ready, n + 1)
                    pe.wait_ge(o_sum_ready, n * 2 + 2)
                    for t in range(TPB):
                        cols = slice(t * P, (t + 1) * P)
                        last = pe.transpose(bank[:, B_TURN[0], cols], k_end[:, cols], ident[:])
                    last.then_inc(ket_turned, 1)

                def updates(n, t):
                    if t == 0:
                        pe.wait_ge(ket_lo, n + 1)
                        pe.wait_ge(v_in, n * 16 + 16)
                    for c in range(CPT):
                        rows = slice(c * HG_BLOCK, (c + 1) * HG_BLOCK)
                        last = three_products(pe, bank[:, B_UPD + c, t * P:(t + 1) * P],
                                              (ket[rows, 0, t * P:(t + 1) * P], ket[rows, 1, t * P:(t + 1) * P]),
                                              (v[rows, t, :, 0:VD], v[rows, t, :, VD:]), True, True)
                        if t == TPB - 1:
                            last.then_inc(updated, 1)

                def outputs(n, part):
                    hh, t = part // TPB, part % TPB
                    if part == 0:
                        pe.wait_ge(a_lo, n * 2 + 2)
                        pe.wait_ge(s_lo, n + 1)
                    cols = slice(t * P, (t + 1) * P)
                    dst = bank[:, B_SCORE + hh]
                    for half in range(2):
                        pe.matmul(dst[:, cols], v[:, t, hh], a_hl[:, hh, half, cols], start=half == 0, stop=False)
                    for c in range(t * CPT, (t + 1) * CPT):
                        own = slice(c * HG_BLOCK, (c + 1) * HG_BLOCK)
                        for half in range(2):
                            last = pe.matmul(dst[:, own], s_hl[HALVES[hh], c].rearrange("p a n -> p (a n)"),
                                             qd[HALVES[hh], half, own], start=False, stop=half == 1 and c == (t + 1) * CPT - 1)
                    if t == TPB - 1:
                        last.then_inc(o_done, 1)

                def turn_outputs(n, hh):
                    pe.wait_ge(o_fm_ready, n * 2 + (hh + 1))
                    for t in range(TPB):
                        cols = slice(t * P, (t + 1) * P)
                        last = pe.transpose(bank[:, B_TURN[hh], cols], o_fm[:, cols], ident[:])
                    last.then_inc(o_turned, 1)

                pe.sem_inc(prod_done, 4)
                pe.sem_inc(logits_out, 2)
                pe.sem_inc(half_used, 1)
                pe.sem_inc(o_turned, 1)
                pe.sem_inc(o_sum_ready, 2)
                with pe.Fori(0, UNITS) as n:
                    for g in range(NB * KD):
                        j, k = g // KD, g % KD
                        if 0 <= g - AT_SCORES < 4:
                            scores(n, g - AT_SCORES)
                        if g == AT_TURN_K:
                            turn_k(n)
                        if 0 <= g - AT_UPDATES < TPB:
                            updates(n, g - AT_UPDATES)
                        if 0 <= g - AT_OUTPUTS < 2 * TPB:
                            outputs(n, g - AT_OUTPUTS)
                        if g in AT_TURN:
                            turn_outputs(n, AT_TURN.index(g))
                        if j == 0 and k in (0, KD // 2):
                            pe.wait_ge(w_split, n * 2 + (k // (KD // 2) + 1))
                        if k == 0:
                            pe.wait_ge(logits_out, n * NB + (j + 1))
                        cols = slice(j * BLK, (j + 1) * BLK)
                        last = three_products(pe, bank[:, j % 2], (w_hi[:, k], w_lo[:, k]),
                                              (hT_hi[:, k, cols], hT_lo[:, k, cols]), k == 0, k == KD - 1)
                        if k == KD - 1:
                            last.then_inc(prod_done, 1)
                        elif j == NB - 1 and k == KD // 2 - 1:
                            last.then_inc(half_used, 1)
    clear_semaphores(nc, sems)


PE_ROWS, ROT_ROWS = slice(NOPE, QK), slice(QK, P)


def latent_projections(nc, projT, g_q, g_kv, w_uq, w_ukv, rope_d, ident_d, qT, knT, kpT, vTok):
    sems = []
    with ExitStack() as ctx:
        def sb(name, shape, dt=F32):
            return ctx.enter_context(nc.sbuf_tensor(name, shape, dt))

        def sem(name):
            sems.append(nc.alloc_semaphore("b_" + name))
            return sems[-1]

        HALF, QTR = S // 2, S // 4
        c_hi = sb("c_hi", [P, N_LORA, S], F32R)
        c_lo = sb("c_lo", [P, N_LORA, S], F32R)
        rope = sb("rope_b", [P, S])
        acc_rs = sb("acc_rs", [P, S])
        sq = sb("sq", [P, 2, QTR])
        scaled = sb("scaled", [P, 2, HALF])
        wq_raw = sb("wq_raw", [P, 2, KQ, P])
        wq_hi = sb("wq_hi", [P, 2, KQ, P], F32R)
        wq_lo = sb("wq_lo", [P, 2, KQ, P], F32R)
        wk_hi = sb("wk_hi", [P, KKV, W], F32R)
        wk_lo = sb("wk_lo", [P, KKV, W], F32R)
        wv_hi = sb("wv_hi", [P, KKV, W], F32R)
        wv_lo = sb("wv_lo", [P, KKV, W], F32R)
        out = sb("out_b", [P, 2, 2, BLK], F32R)
        turned = sb("turned", [P, 2, BLK])
        rot = sb("rot", [P, BLK])
        ident = sb("ident_b", [P, P])
        ones = sb("ones_b", [P, 1])
        gain = sb("gain_b", [P, N_LORA])
        eps = sb("eps_b", [P, 1])
        std = sb("std_b", [P, 2, TT])
        rstd = sb("rstd_b", [P, 2, TT])
        bank = ctx.enter_context(nc.psum_tensor("bankB", [P, 8, BLK], F32))
        SUMS, SPREAD = 4, 4

        const_in = sem("const_in")
        const_set = sem("const_set")
        waited_pool = sem("waited_pool")
        c_in = [sem(f"c_in{k}") for k in range(N_LORA)]
        wkv_in = sem("wkv_in")
        wkv_hi = sem("wkv_hi")
        wkv_ready = sem("wkv_ready")
        wq_in = [sem("wq_in0"), sem("wq_in1")]
        wq_raw_free = sem("wq_raw_free")
        wq_hi_ready = sem("wq_hi_ready")
        wq_ready = sem("wq_ready")
        kpe_in = sem("kpe_in")
        sq_ready = sem("sq_ready")
        sq_added = sem("sq_added")
        sums_done = sem("sums_done")
        std_ready = sem("std_ready")
        rstd_ready = sem("rstd_ready")
        spread_done = sem("spread_done")
        rs_ready = sem("rs_ready")
        scaled_ready = sem("scaled_ready")
        c_hi_ready = sem("c_hi_ready")
        c_ready = sem("c_ready")
        prod_done = sem("prod_done")
        bank_free = sem("bank_free")
        turned_ready = sem("turned_ready")
        rot_ready = sem("rot_ready")
        out_hi = sem("out_hi")
        out_lo = sem("out_lo")
        stored = [sem("stored0"), sem("stored1")]

        E_V = PAIRS * NB
        E_PE = E_V + TT
        E_Q = E_PE + NB
        E_END = E_Q + HEADS * NB
        SQ_KV = KKV * 4
        kv_tiles, q_tiles = range(KQ, N_LORA), range(KQ)

        def part_of(m):
            return (kv_tiles[m % KKV], m // KKV) if m < 2 * KKV else (q_tiles[m // 2 - KKV], m % 2)

        wkv_v = w_ukv.rearrange("(k p) (h n) -> p k h n", p=P, n=P)
        wq_v = w_uq.rearrange("(k p) n -> p k n", p=P)

        with nc.Block() as block:

            @block.sync
            def _(sp):
                sp.dma_start(ident[:], ident_d).then_inc(const_in, 16)
                sp.dma_start(gain[:, 0:KQ], g_q.rearrange("o (k p) -> p (o k)", p=P),
                             allow_slow_non_contiguous=True).then_inc(const_in, 16)
                sp.dma_start(gain[:, KQ:], g_kv.rearrange("o (k p) -> p (o k)", p=P),
                             allow_slow_non_contiguous=True).then_inc(const_in, 16)
                for k in kv_tiles:
                    sp.dma_start(c_lo[:, k].bitcast(F32), projT[k]).then_inc(c_in[k], 16)
                for k in range(KKV):
                    sp.dma_start(scaled[:, 0, k * W:(k + 1) * W].rearrange("p (h n) -> p h n", n=NOPE),
                                 wkv_v[:, k, :, 0:NOPE]).then_inc(wkv_in, 16)
                    sp.dma_start(scaled[:, 1, k * W:(k + 1) * W].rearrange("p (h n) -> p h n", n=VD),
                                 wkv_v[:, k, :, NOPE:P]).then_inc(wkv_in, 16)
                for k in q_tiles:
                    sp.dma_start(c_lo[:, k].bitcast(F32), projT[k]).then_inc(c_in[k], 16)
                sp.dma_start(rope[:], rope_d).then_inc(kpe_in, 16)
                def load_wq(u, h):
                    for to, of, n in ((0, 0, QK), (QK, NOPE + 16, 16), (QK + 16, NOPE, 16)):
                        sp.dma_start(wq_raw[:, u, :, to:to + n], wq_v[:, :, ds(h * QK + of, n)]).then_inc(wq_in[u], 16)

                load_wq(0, 0)
                load_wq(1, 1)
                for s in stored:
                    sp.sem_inc(s, 32)
                for e in range(E_V):
                    p, blk = e // NB, e % NB
                    sp.wait_ge(bank_free, 4 + e + 1)
                    for part in range(2):
                        sp.dma_start(knT[p, part, :, blk * BLK:(blk + 1) * BLK], out[:, e % 2, part].bitcast(F32))\
                          .then_inc(stored[e % 2], 16)
                for t in range(TT):
                    e = E_V + t
                    if t == 2 * KQ:
                        sp.wait_ge(scaled_ready, 2 * N_LORA)
                        sp.dma_start(acc_rs[NOPE:P], projT[T_PE, NOPE:P, :]).then_inc(kpe_in, 16)
                    sp.wait_ge(bank_free, 4 + e + 1)
                    for part in range(2):
                        sp.dma_start(vTok[part * 4:(part + 1) * 4, :, t, :].rearrange("h p n -> p h n"),
                                     out[:, e % 2, part].bitcast(F32).rearrange("p (h n) -> p h n", n=2 * VD))\
                          .then_inc(stored[e % 2], 16)
                for blk in range(NB):
                    sp.wait_ge(out_lo, blk + 3)
                    for part in range(2):
                        sp.dma_start(kpT[part, :, blk * BLK:(blk + 1) * BLK], out[PE_ROWS, blk % 2, part].bitcast(F32))\
                          .then_inc(stored[blk % 2], 16)

                def store_q(h, n0):
                    for blk in range(NB):
                        sp.wait_ge(out_lo, n0 + (NB + blk + 3))
                        for part in range(2):
                            sp.dma_start(qT[ds(h, 1), part, :, blk * BLK:(blk + 1) * BLK].rearrange("o p n -> (o p) n"),
                                         out[0:QK, blk % 2, part].bitcast(F32)).then_inc(stored[blk % 2], 16)

                with sp.Fori(0, HEADS // 2 - 1) as i:
                    for u in range(2):
                        sp.wait_ge(wq_raw_free, i * 2 + (u + 1))
                        load_wq(u, i * 2 + (2 + u))
                        store_q(i * 2 + u, i * (2 * NB) + u * NB)
                for h in range(HEADS - 2, HEADS):
                    store_q(h, h * NB)
                for s in stored:
                    sp.wait_ge(s, 32 + 32 * (E_END // 2))

            @block.gpsimd
            def _(pool):
                pool.memset(eps[:], EPS).then_inc(const_set, 1)
                pool.memset(ones[:], 1.0).then_inc(const_set, 1)
                for n, (hi, lo) in enumerate(((wk_hi, wk_lo), (wv_hi, wv_lo))):
                    pool.wait_ge(wkv_hi, n + 1)
                    pool.tensor_tensor(lo[:].rearrange("p k n -> p (k n)"), scaled[:, n],
                                       hi[:].rearrange("p k n -> p (k n)").bitcast(F32), ALU.subtract).then_inc(wkv_ready, 1)

                def split_c(m):
                    tile, half = part_of(m)
                    cols = slice(half * HALF, (half + 1) * HALF)
                    pool.wait_ge(c_hi_ready, m + 1)
                    pool.tensor_tensor(c_lo[:, tile, cols], scaled[:, m % 2], c_hi[:, tile, cols].bitcast(F32),
                                       ALU.subtract).then_inc(c_ready, 1)

                def split_wq(u, i):
                    pool.wait_ge(wq_in[u], i * 48 + 48)
                    pool.wait_ge(prod_done, (i * 2 + u) * NB + (E_PE + 4))
                    pool.sem_inc(waited_pool, 1)
                    pool.tensor_scalar(wq_hi[:, u], wq_raw[:, u], 1.0, None, ALU.mult).then_inc(wq_hi_ready, 1)
                    pool.wait_ge(wq_hi_ready, i * 2 + (u + 1))
                    pool.tensor_tensor(wq_lo[:, u], wq_raw[:, u], wq_hi[:, u].bitcast(F32), ALU.subtract)\
                        .then_inc(wq_ready, 1)
                    pool.wait_ge(wq_ready, i * 2 + (u + 1))
                    pool.sem_inc(wq_raw_free, 1)

                for m in range(2 * N_LORA):
                    split_c(m)
                with pool.Fori(0, HEADS // 2) as i:
                    for u in range(2):
                        split_wq(u, i)

            @block.scalar
            def _(act):
                act.wait_ge(const_in, 48)
                act.wait_ge(const_set, 2)

                def square(m):
                    n = m if m < SQ_KV else m - SQ_KV
                    tile, quarter = (kv_tiles if m < SQ_KV else q_tiles)[n // 4], n % 4
                    cols = slice(quarter * QTR, (quarter + 1) * QTR)
                    act.wait_ge(c_in[tile], 16)
                    if n < 4:
                        if m >= SQ_KV:
                            act.wait_ge(scaled_ready, 2 * KKV)
                        dst = acc_rs[:, cols]
                    else:
                        if m >= 2:
                            act.wait_ge(sq_added, m - 1)
                        dst = sq[:, m % 2]
                    act.activation(dst, c_lo[:, tile, cols].bitcast(F32), ACT.Square).then_inc(sq_ready, 1)

                def root(g, width):
                    act.wait_ge(sums_done, g + 1)
                    act.activation(std[:, g], bank[:, SUMS, 0:TT], ACT.Sqrt, bias=eps[:, 0:1], scale=1.0 / width)\
                       .then_inc(std_ready, 1)

                def take_spread(g):
                    act.wait_ge(spread_done, g + 1)
                    act.activation(acc_rs[:].rearrange("p (b n) -> p b n", n=BLK), bank[:, SPREAD:SPREAD + NB], ACT.Copy)\
                       .then_inc(rs_ready, 1)

                def round_c(m):
                    tile, half = part_of(m)
                    act.wait_ge(scaled_ready, m + 1)
                    act.activation(c_hi[:, tile, half * HALF:(half + 1) * HALF], scaled[:, m % 2], ACT.Copy)\
                       .then_inc(c_hi_ready, 1)

                for m in range(SQ_KV):
                    square(m)
                act.wait_ge(wkv_in, 2 * KKV * 16)
                for n, hi in enumerate((wk_hi, wv_hi)):
                    act.activation(hi[:].rearrange("p k n -> p (k n)"), scaled[:, n], ACT.Copy).then_inc(wkv_hi, 1)
                root(0, KV_LORA)
                take_spread(0)
                for m in range(2 * KKV):
                    round_c(m)
                for e in range(E_V):
                    act.wait_ge(prod_done, 8 + e + 1)
                    act.wait_ge(stored[e % 2], e // 2 * 32 + 32)
                    act.activation(out[:, e % 2, 0], bank[:, e % 4], ACT.Copy).then_inc(out_hi, 1)
                    for m in range(2 * e, 2 * e + 2):
                        if m < 4 * KQ:
                            square(SQ_KV + m)
                root(1, Q_LORA)
                take_spread(1)
                for t in range(TT):
                    e = E_V + t
                    act.wait_ge(prod_done, 8 + e + 1)
                    act.wait_ge(stored[e % 2], e // 2 * 32 + 32)
                    act.activation(out[:, e % 2].rearrange("p a (h c n) -> p (a h) c n", c=2, n=VD)[:, :, 0],
                                   bank[:, e % 4].rearrange("p (h n) -> p h n", n=VD), ACT.Copy).then_inc(out_hi, 1)
                    if t < 2 * KQ:
                        round_c(2 * KKV + t)

                def round_turned(e, slot, rows):
                    act.wait_ge(turned_ready, e + (1 - E_PE))
                    act.wait_ge(stored[slot], (e - slot) * 16 + 32)
                    act.activation(out[rows, slot, 0], turned[rows, slot], ACT.Copy).then_inc(out_hi, 1)

                for blk in range(NB):
                    round_turned(E_PE + blk, blk % 2, PE_ROWS)
                with act.Fori(0, HEADS) as h:
                    for blk in range(NB):
                        round_turned(h * NB + (E_Q + blk), blk % 2, slice(0, QK))

            @block.vector
            def _(dve):
                dve.wait_ge(const_in, 48)

                def add_square(m):
                    n = m if m < SQ_KV else m - SQ_KV
                    dve.wait_ge(sq_ready, m + 1)
                    if n < 4:
                        dve.sem_inc(sq_added, 1)
                        return
                    cols = slice(n % 4 * QTR, (n % 4 + 1) * QTR)
                    if n >= 8:
                        dve.wait_ge(sq_added, m - 3)
                    dve.tensor_tensor(acc_rs[:, cols], acc_rs[:, cols], sq[:, m % 2], ALU.add).then_inc(sq_added, 1)

                def inverse(g):
                    dve.wait_ge(std_ready, g + 1)
                    dve.reciprocal(rstd[:, g], std[:, g]).then_inc(rstd_ready, 1)

                def scale(m):
                    tile, half = part_of(m)
                    cols = slice(half * HALF, (half + 1) * HALF)
                    if m < 2:
                        dve.wait_ge(wkv_ready, m + 1)
                    else:
                        dve.wait_ge(c_ready, m - 1)
                    dve.scalar_tensor_tensor(scaled[:, m % 2], c_lo[:, tile, cols].bitcast(F32), gain[:, tile:tile + 1],
                                             acc_rs[:, cols], ALU.mult, ALU.mult).then_inc(scaled_ready, 1)

                for m in range(SQ_KV):
                    add_square(m)
                inverse(0)
                dve.wait_ge(rs_ready, 1)
                for m in range(2 * KKV):
                    scale(m)
                for e in range(E_V):
                    dve.wait_ge(out_hi, e + 1)
                    dve.tensor_tensor(out[:, e % 2, 1], bank[:, e % 4], out[:, e % 2, 0].bitcast(F32), ALU.subtract)\
                       .then_inc(bank_free, 1)
                    for m in range(2 * e, 2 * e + 2):
                        if m < 4 * KQ:
                            add_square(SQ_KV + m)
                inverse(1)
                dve.wait_ge(rs_ready, 2)
                for t in range(TT):
                    e = E_V + t
                    if t < 2 * KQ:
                        scale(2 * KKV + t)
                    dve.wait_ge(out_hi, e + 1)
                    o = out[:, e % 2].rearrange("p a (h c n) -> p (a h) c n", c=2, n=VD)
                    dve.tensor_tensor(o[:, :, 1], bank[:, e % 4].rearrange("p (h n) -> p h n", n=VD),
                                      o[:, :, 0].bitcast(F32), ALU.subtract).then_inc(bank_free, 1)

                def turn(e, slot, rows, src, rot_src, cols):
                    dve.wait_ge(out_lo, e + (1 - E_PE))
                    dve.tensor_tensor(rot[PE_ROWS], rot_src, rope[ROT_ROWS, cols], ALU.mult).then_inc(rot_ready, 1)
                    last = dve.tensor_tensor(turned[rows, slot], src, rope[rows, cols], ALU.mult)
                    last.then_inc(bank_free, 1)
                    dve.wait_ge(rot_ready, e + (1 - E_PE))
                    dve.wait_ge(bank_free, e + 5)
                    dve.tensor_tensor(turned[PE_ROWS, slot], turned[PE_ROWS, slot], rot[PE_ROWS], ALU.add)\
                       .then_inc(turned_ready, 1)
                    dve.wait_ge(out_hi, e + 1)
                    dve.tensor_tensor(out[rows, slot, 1], turned[rows, slot], out[rows, slot, 0].bitcast(F32),
                                      ALU.subtract).then_inc(out_lo, 1)

                dve.sem_inc(out_lo, 2)
                dve.wait_ge(kpe_in, 32)
                for blk in range(NB):
                    cols = slice(blk * BLK, (blk + 1) * BLK)
                    turn(E_PE + blk, blk % 2, PE_ROWS, acc_rs[PE_ROWS, cols], acc_rs[ROT_ROWS, cols], cols)
                with dve.Fori(0, HEADS) as h:
                    for blk in range(NB):
                        src = bank[:, blk]
                        dve.wait_ge(prod_done, h * NB + (8 + E_PE + blk + 1))
                        turn(h * NB + (E_Q + blk), blk % 2, slice(0, QK), src[0:QK], src[ROT_ROWS],
                             slice(blk * BLK, (blk + 1) * BLK))

            @block.tensor
            def _(pe):
                pe.wait_ge(const_in, 48)
                pe.wait_ge(const_set, 2)

                def norm(g, added):
                    pe.wait_ge(sq_added, added)
                    for t in range(TT):
                        last = pe.matmul(bank[:, SUMS, t:t + 1], acc_rs[:, t * P:(t + 1) * P], ones[:], start=True, stop=True)
                    last.then_inc(sums_done, 1)
                    pe.wait_ge(rstd_ready, g + 1)
                    for t in range(TT):
                        last = pe.matmul(bank[:, SPREAD + t // TPB, t % TPB * P:(t % TPB + 1) * P],
                                         rstd[:, g, t:t + 1].to_broadcast([P, P]), ident[:], start=True, stop=True)
                    last.then_inc(spread_done, 1)

                norm(0, SQ_KV)
                pe.wait_ge(wkv_ready, 2)
                pe.sem_inc(bank_free, 4)
                pe.sem_inc(prod_done, 8)
                pe.wait_ge(c_ready, KKV)
                for p in range(PAIRS):
                    for blk in range(NB):
                        e = p * NB + blk
                        if e == NB // 2:
                            pe.wait_ge(c_ready, 2 * KKV)
                        pe.wait_ge(bank_free, e + 1)
                        cols, of = slice(blk * BLK, (blk + 1) * BLK), slice(p * P, (p + 1) * P)
                        for k in range(KKV):
                            last = three_products(pe, bank[:, e % 4], (wk_hi[:, k, of], wk_lo[:, k, of]),
                                                  (c_hi[:, KQ + k, cols], c_lo[:, KQ + k, cols]), k == 0, k == KKV - 1)
                        last.then_inc(prod_done, 1)
                norm(1, SQ_KV + 4 * KQ)
                for t in range(TT):
                    e = E_V + t
                    pe.wait_ge(bank_free, e + 1)
                    rows = slice(t * P, (t + 1) * P)
                    for k in range(KKV):
                        last = three_products(pe, bank[:, e % 4], (c_hi[:, KQ + k, rows], c_lo[:, KQ + k, rows]),
                                              (wv_hi[:, k], wv_lo[:, k]), k == 0, k == KKV - 1)
                    last.then_inc(prod_done, 1)
                pe.wait_ge(c_ready, 2 * N_LORA)
                with pe.Fori(0, HEADS // 2) as i:
                    for u in range(2):
                        pe.wait_ge(wq_ready, i * 2 + (u + 1))
                        for blk in range(NB):
                            pe.wait_ge(bank_free, i * (2 * NB) + (E_Q + u * NB + blk + 1))
                            cols = slice(blk * BLK, (blk + 1) * BLK)
                            for k in range(KQ):
                                last = three_products(pe, bank[:, blk], (wq_hi[:, u, k], wq_lo[:, u, k]),
                                                      (c_hi[:, k, cols], c_lo[:, k, cols]), k == 0, k == KQ - 1)
                            last.then_inc(prod_done, 1)
    clear_semaphores(nc, sems)


AHEAD = 2
LED = 2 * TPB


def attention_schedule():
    def tiles(*blocks):
        return [(b, j) for b in blocks for j in range(TPB * (b + 1))]

    def dealt(some, n):
        return [some[i * len(some) // n:(i + 1) * len(some) // n] for i in range(n)]

    steps = [[LED + r, some, None, None] for r, some in enumerate(dealt(tiles(0, 1), TPB) + dealt(tiles(2), TPB))]
    steps += [[r, some, None, None] for r, some in enumerate(dealt(tiles(3), LED))]
    steps += [[None, [], None, None], [None, [], None, None]]
    for s in range(len(steps) - 1):
        for b, j in steps[s][1]:
            if j == TPB * (b + 1) - 1:
                steps[s + 1][2] = b
                steps[s + 2][3] = b
    return steps


def attention(nc, qT, knT, kpT, vTok, ident_d, oA):
    STEPS = attention_schedule()
    CHUNK_AT, CHUNKS = {}, 0
    PIECE_AT, PIECES = {}, 0
    TURN_AT, TURNS = {}, 0
    TILE_AT, TILES = {}, 0
    for i in range(TT):
        for c in range(i // TPB + 1):
            CHUNK_AT[i, c] = CHUNKS
            CHUNKS += 1
        for piece in range(i // (2 * TPB) + 1):
            PIECE_AT[i, piece] = PIECES
            PIECES += 1
    for _, tiles, _, o_block in STEPS:
        for tile in tiles:
            TURN_AT[tile], TILE_AT[tile] = TURNS, TILES
            TURNS += 1
            TILES += 1
        if o_block is not None:
            TURN_AT["o", o_block] = TURNS
            TURNS += 1

    def s_bank(i, c):
        b, r = i // TPB, i % TPB
        return c + (r if b == 0 else 2 * (r % 2) if b == 1 else 0)

    def pieces_before(i, c):
        need = 0
        for (t, piece), at in PIECE_AT.items():
            if t < i:
                b = t // TPB
                used = {s_bank(t, x) for x in range(2 * piece, min(2 * piece + 2, b + 1))}
                if s_bank(i, c) in used:
                    need = max(need, at + 1)
        return need

    def width(i, c):
        return BLK if c < i // TPB else (i % TPB + 1) * P

    sems = []
    with ExitStack() as ctx:
        def sb(name, shape, dt=F32):
            return ctx.enter_context(nc.sbuf_tensor(name, shape, dt))

        def sem(name):
            sems.append(nc.alloc_semaphore("c_" + name))
            return sems[-1]

        q_sb = sb("q_sb", [P, 2, 2, S], F32R)
        k_sb = sb("k_sb", [P, 2, 2, S], F32R)
        v_sb = sb("v_sb", [P, 2, TT, 2 * VD], F32R)
        probs = [sb(f"probs{b}", [P, TPB, (b + 1) * BLK]) for b in range(NB)]
        RING = 6
        pT = sb("pT", [P, RING, 2, BLK], F32R)
        oT = sb("oT", [P, BLK])
        o_lo = sb("o_lo", [P, TPB, VD])
        o_sum = sb("o_sum", [P, TPB, VD])
        o_out = sb("o_out", [P, 2, TPB, VD])
        ident = sb("ident_c", [P, P])
        early_q = sb("early_q", [1, P], F32R)
        late_k = sb("late_k", [1, P], F32R)
        mask_raw = sb("mask_raw", [1, 2, P])
        chunk_max = sb("chunk_max", [P, NB])
        row_max = sb("row_max", [P, 1])
        neg_max = sb("neg_max", [P, 2])
        sums = sb("sums", [P, NB, TPB, 2])
        total = sb("total", [P, TPB])
        inv = sb("inv", [P, TPB])
        scores = ctx.enter_context(nc.psum_tensor("scores", [P, 4, BLK], F32))
        turn = ctx.enter_context(nc.psum_tensor("turn", [P, 3, BLK], F32))
        o_acc = ctx.enter_context(nc.psum_tensor("o_acc", [P, BLK], F32))

        const_in = sem("const_in")
        const_set = sem("const_set")
        mask_set = sem("mask_set")
        kp_in = sem("kp_in")
        head_in = [sem("head_in0"), sem("head_in1")]
        head_done = sem("head_done")
        qk_done = sem("qk_done")
        chunk_max_done = sem("chunk_max_done")
        row_max_done = sem("row_max_done")
        max_ready = sem("max_ready")
        exp_done = sem("exp_done")
        turned = sem("turned")
        hi_ready = sem("hi_ready")
        turn_read = sem("turn_read")
        pv_done = sem("pv_done")
        o_copied = sem("o_copied")
        o_lo_ready = sem("o_lo_ready")
        total_ready = sem("total_ready")
        inv_ready = sem("inv_ready")
        o_sum_ready = sem("o_sum_ready")
        o_ready = sem("o_ready")
        o_stored = [sem("o_stored0"), sem("o_stored1")]

        def is_first(h):
            return isinstance(h, int) and h == 0

        with nc.Block() as block:

            @block.sync
            def _(sp):
                sp.dma_start(ident[:], ident_d).then_inc(const_in, 16)
                for u in range(2):
                    for part in range(2):
                        sp.dma_start(k_sb[PE_ROWS, u, part].bitcast(F32), kpT[part]).then_inc(kp_in, 16)
                def load_head(i, u):
                    for part in range(2):
                        sp.dma_start(q_sb[0:QK, u, part].bitcast(F32),
                                     qT[ds(i * 2 + u, 1), part].rearrange("o p n -> (o p) n")).then_inc(head_in[u], 16)
                        sp.dma_start(k_sb[0:NOPE, u, part].bitcast(F32),
                                     knT[ds(i, 1), part, u * NOPE:(u + 1) * NOPE].rearrange("o p n -> (o p) n"))\
                          .then_inc(head_in[u], 16)
                    sp.dma_start(v_sb[:, u].bitcast(F32),
                                 vTok[ds(i * 2 + u, 1)].rearrange("o p t n -> (o p) t n")).then_inc(head_in[u], 16)

                def store_head(i, u):
                    h = i * 2 + u
                    for b in range(NB):
                        sp.wait_ge(o_ready, h * NB + (b + 1))
                        sp.dma_start(oA[b * TPB:(b + 1) * TPB, :, ds(h * VD, VD)].rearrange("t p n -> p t n"),
                                     o_out[:, b % 2]).then_inc(o_stored[b % 2], 16)

                for u in range(2):
                    load_head(0, u)
                with sp.Fori(0, PAIRS - 1) as i:
                    for u in range(2):
                        store_head(i, u)
                        sp.wait_ge(head_done, i * 2 + (u + 1))
                        load_head(i + 1, u)
                for u in range(2):
                    store_head(PAIRS - 1, u)
                for s in o_stored:
                    sp.wait_ge(s, 16 + 16 * HEADS * NB // 2)

            @block.gpsimd
            def _(pool):
                pool.memset(mask_raw[:], 0.0).then_inc(mask_set, 1)
                pool.wait_ge(mask_set, 1)
                pool.memset(mask_raw[:, 0, 0:CHUNK], 1.0).then_inc(mask_set, 1)
                pool.memset(mask_raw[:, 1, CHUNK:P], MASKED).then_inc(mask_set, 1)
                pool.wait_ge(mask_set, 3)
                pool.tensor_scalar(early_q[:], mask_raw[:, 0], 1.0, None, ALU.mult).then_inc(const_set, 1)
                pool.tensor_scalar(late_k[:], mask_raw[:, 1], 1.0, None, ALU.mult).then_inc(const_set, 1)

            @block.scalar
            def _(act):
                def exponentials(h, i, piece):
                    b, r = i // TPB, i % TPB
                    first, end = 2 * piece, min(2 * piece + 2, b + 1)
                    n = min(end * BLK, (i + 1) * P) - first * BLK
                    bank = s_bank(i, 0)
                    src = scores[:].rearrange("p b n -> p (b n)")[:, (bank + first) * BLK:(bank + first) * BLK + n]
                    if piece == 0:
                        act.wait_ge(max_ready, h * TT + (i + 1))
                        if r == 0 and i < LED and not is_first(h):
                            act.wait_ge(turned, h * TURNS + (TURN_AT[b, TPB * (b + 1) - 1] + 1 - TURNS))
                    act.activation(probs[b][:, r, first * BLK:first * BLK + n], src, ACT.Exp,
                                   bias=neg_max[:, i % 2:i % 2 + 1], scale=SCALE,
                                   accum_out=sums[:, b, r, piece:piece + 1]).then_inc(exp_done, 1)

                def hi_part(h, tile):
                    b, j = tile
                    r0 = max(0, j - TPB * b)
                    at = TILE_AT[tile]
                    act.wait_ge(turned, h * TURNS + (TURN_AT[tile] + 1))
                    act.wait_ge(pv_done, h * TILES + (at + 2))
                    act.activation(pT[:, at % RING, 0, r0 * P:], turn[:, TURN_AT[tile] % 3, r0 * P:], ACT.Copy)\
                       .then_inc(hi_ready, 1)

                act.sem_inc(exp_done, 1)
                act.sem_inc(o_copied, 1)

                def head(h, more):
                    for i, tiles, done, o_block in STEPS:
                        for tile in tiles[:AHEAD]:
                            hi_part(h, tile)
                        if done is not None:
                            act.wait_ge(pv_done, h * TILES + (TILE_AT[done, TPB * (done + 1) - 1] + RING + 2))
                            if done > 0:
                                act.wait_ge(turned, h * TURNS + (TURN_AT["o", done - 1] + 1))
                            act.activation(oT[:], o_acc[:], ACT.Copy).then_inc(o_copied, 1)
                        if i is not None and (more or i >= LED):
                            exponentials(h + 1 if i < LED else h, i, 0)
                        for tile in tiles[AHEAD:]:
                            hi_part(h, tile)
                        if i is not None and i >= 2 * TPB:
                            exponentials(h, i, 1)
                        if o_block is not None:
                            at = TURN_AT["o", o_block]
                            act.wait_ge(turned, h * TURNS + (at + 1))
                            if o_block > 0:
                                act.wait_ge(o_sum_ready, h * NB + o_block)
                            act.activation(o_lo[:], turn[:, at % 3].rearrange("p (t n) -> p t n", n=P)[:, :, VD:], ACT.Copy)\
                               .then_inc(o_lo_ready, 1)

                for i in range(LED):
                    exponentials(0, i, 0)
                with act.Fori(0, HEADS - 1) as h:
                    head(h, True)
                head(HEADS - 1, False)

            @block.vector
            def _(dve):
                def maxima(h, i):
                    b = i // TPB
                    for c in range(b + 1):
                        dve.wait_ge(qk_done, h * CHUNKS + (CHUNK_AT[i, c] + 1))
                        dve.reduce_max(chunk_max[:, c:c + 1], scores[:, s_bank(i, c), 0:width(i, c)], AX.X)\
                           .then_inc(chunk_max_done, 1)
                    dve.wait_ge(chunk_max_done, h * CHUNKS + (CHUNK_AT[i, b] + 1))
                    dve.reduce_max(row_max[:], chunk_max[:, 0:b + 1], AX.X).then_inc(row_max_done, 1)
                    dve.wait_ge(row_max_done, h * TT + (i + 1))
                    if not is_first(h) or i >= 2:
                        before = (i - 2) % TT
                        at = PIECE_AT[before, before // (2 * TPB)] - (PIECES if i < 2 else 0)
                        dve.wait_ge(exp_done, h * PIECES + (at + 2))
                    dve.tensor_scalar(neg_max[:, i % 2:i % 2 + 1], row_max[:], -SCALE, None, ALU.mult).then_inc(max_ready, 1)

                def lo_part(h, tile):
                    b, j = tile
                    r0 = max(0, j - TPB * b)
                    at = TILE_AT[tile]
                    dve.wait_ge(hi_ready, h * TILES + (at + 1))
                    dve.tensor_tensor(pT[:, at % RING, 1, r0 * P:], turn[:, TURN_AT[tile] % 3, r0 * P:],
                                      pT[:, at % RING, 0, r0 * P:].bitcast(F32), ALU.subtract).then_inc(turn_read, 1)

                def outputs(h, b):
                    at = TURN_AT["o", b]
                    n = h * NB + (b + 1)
                    if b >= 2:
                        dve.tensor_tensor(total[:], sums[:, b, :, 0], sums[:, b, :, 1], ALU.add).then_inc(total_ready, 1)
                    else:
                        dve.tensor_copy(total[:], sums[:, b, :, 0]).then_inc(total_ready, 1)
                    dve.wait_ge(total_ready, n)
                    dve.reciprocal(inv[:], total[:]).then_inc(inv_ready, 1)
                    dve.wait_ge(o_lo_ready, n)
                    dve.tensor_tensor(o_sum[:], turn[:, at % 3].rearrange("p (t n) -> p t n", n=P)[:, :, 0:VD], o_lo[:],
                                      ALU.add).then_inc(o_sum_ready, 1)
                    dve.wait_ge(o_sum_ready, n)
                    dve.wait_ge(inv_ready, n)
                    dve.sem_inc(turn_read, 1)
                    dve.wait_ge(o_stored[b % 2], h * 32 + (b // 2 * 16 + 16))
                    dve.tensor_tensor(o_out[:, b % 2], o_sum[:], inv[:].unsqueeze(2).to_broadcast([P, TPB, VD]), ALU.mult)\
                       .then_inc(o_ready, 1)

                dve.sem_inc(turn_read, 1)
                for s in o_stored:
                    dve.sem_inc(s, 16)

                def head(h, more):
                    for i, tiles, _, o_block in STEPS:
                        if i is not None and (more or i >= LED):
                            maxima(h + 1 if i < LED else h, i)
                        for tile in tiles:
                            lo_part(h, tile)
                        if o_block is not None:
                            outputs(h, o_block)

                for i in range(LED):
                    maxima(0, i)
                with dve.Fori(0, HEADS - 1) as h:
                    head(h, True)
                head(HEADS - 1, False)

            @block.tensor
            def _(pe):
                def queries(h, i, u):
                    b, r = i // TPB, i % TPB
                    rows = slice(i * P, (i + 1) * P)
                    q = q_sb[0:QK, u, 0, rows], q_sb[0:QK, u, 1, rows]
                    for c in range(b + 1):
                        n = width(i, c)
                        cols = slice(c * BLK, c * BLK + n)
                        dst = scores[:, s_bank(i, c), 0:n]
                        pe.wait_ge(exp_done, h * PIECES + (pieces_before(i, c) + 1))
                        diagonal = c == b
                        last = three_products(pe, dst, q, (k_sb[0:QK, u, 0, cols], k_sb[0:QK, u, 1, cols]), True, not diagonal)
                        if diagonal:
                            last = pe.matmul(dst[:, n - P:n], early_q[:], late_k[:], start=False, stop=True)
                        last.then_inc(qk_done, 1)

                def transposes(h, tile):
                    b, j = tile
                    at = TURN_AT[tile]
                    if at < 3:
                        pe.wait_ge(turn_read, h * TURNS + 1)
                    else:
                        pe.wait_ge(turn_read, h * TURNS + (at - 1))
                    if j == 0 or j >= TPB * b:
                        i = TPB * b + (TPB - 1 if j == 0 else j - TPB * b)
                        pe.wait_ge(exp_done, h * PIECES + (PIECE_AT[i, i // (2 * TPB)] + 2))
                    for r in range(max(0, j - TPB * b), TPB):
                        last = pe.transpose(turn[:, at % 3, r * P:(r + 1) * P], probs[b][:, r, j * P:(j + 1) * P], ident[:])
                    last.then_inc(turned, 1)

                def values(h, tile, u):
                    b, j = tile
                    r0 = max(0, j - TPB * b)
                    at = TILE_AT[tile]
                    pe.wait_ge(turn_read, h * TURNS + (TURN_AT[tile] + 2))
                    if j == 0:
                        pe.wait_ge(o_copied, h * NB + (b + 1))
                    dst = o_acc[:, r0 * P:]
                    end = TPB * (b + 1) - 1
                    pe.matmul(dst, v_sb[:, u, j], pT[:, at % RING, 0, r0 * P:], start=j == 0, stop=False)
                    pe.matmul(dst, v_sb[:, u, j], pT[:, at % RING, 1, r0 * P:], start=False, stop=j == end)\
                      .then_inc(pv_done, 1)

                pe.wait_ge(const_in, 16)
                pe.wait_ge(const_set, 2)
                pe.wait_ge(kp_in, 64)
                pe.sem_inc(pv_done, 1 + RING)

                def head(pair, u, more):
                    h = pair * 2 + u
                    before = []
                    for i, tiles, _, o_block in STEPS:
                        if i is not None and i >= LED:
                            queries(h, i, u)
                        elif i is not None and more:
                            if i == 0:
                                pe.wait_ge(head_in[1 - u], (pair + u) * 80 + 80)
                            queries(h + 1, i, 1 - u)
                        for tile in tiles:
                            transposes(h, tile)
                        for tile in before:
                            values(h, tile, u)
                        before = tiles
                        if o_block is not None:
                            at = TURN_AT["o", o_block]
                            pe.wait_ge(o_copied, h * NB + (o_block + 2))
                            pe.wait_ge(turn_read, h * TURNS + (at - 1))
                            for r in range(TPB):
                                last = pe.transpose(turn[:, at % 3, r * P:(r + 1) * P], oT[:, r * P:(r + 1) * P], ident[:])
                            last.then_inc(turned, 1)
                            if o_block == NB - 1:
                                pe.wait_ge(turned, h * TURNS + TURNS)
                                pe.sem_inc(head_done, 1)

                pe.wait_ge(head_in[0], 80)
                for i in range(LED):
                    queries(0, i, 0)
                with pe.Fori(0, PAIRS - 1) as pair:
                    for u in range(2):
                        head(pair, u, True)
                for u in range(2):
                    head(PAIRS - 1, u, u == 0)
    clear_semaphores(nc, sems)


def merge_and_output(nc, x, oA, oB, gateTok, projT, w_branch_a, w_branch_b, w_out, g_post, ident_d, result):
    sems = []
    with ExitStack() as ctx:
        def sb(name, shape, dt=F32):
            return ctx.enter_context(nc.sbuf_tensor("e_" + name, shape, dt))

        def sem(name):
            sems.append(nc.alloc_semaphore("e_" + name))
            return sems[-1]

        wo_hi = sb("wo_hi", [P, KD, D], F32R)
        wo_lo = sb("wo_lo", [P, KD, D], F32R)
        wb_raw = sb("wb_raw", [P, 2, 2, KW, P])
        wb_hi = sb("wb_hi", [P, 2, 2, KW, P], F32R)
        wb_lo = sb("wb_lo", [P, 2, 2, KW, P], F32R)
        uT = sb("uT", [P, 2, KW, 2, BLK], F32R)
        with nc.sbuf_tensor("e_first_in", [P, 2 * TPB, 2, BLK], F32) as first_in:
            pass
        mT = sb("mT", [P, KD, 2, BLK], F32R)
        o_in = sb("o_in", [P, 2, BLK])
        g_in = sb("g_in", [P, 2, BLK])
        sg = sb("sg", [P, 2, BLK])
        u = sb("u", [P, TPB, BLK])
        l_in = sb("l_in", [P, 2, 2, BLK])
        part_a = sb("part_a", [P, BLK])
        part_b = sb("part_b", [P, BLK])
        x_in = sb("x_in", [P, D])
        y = sb("y", [P, 2, D])
        gain = sb("gain", [P, D])
        ident = sb("ident", [P, P])
        eps = sb("eps", [P, 1])
        ss = sb("ss", [P, 2])
        std = sb("std", [P, 1])
        rstd = sb("rstd", [P, 1])
        bank = ctx.enter_context(nc.psum_tensor("bankE", [P, 8, BLK], F32))
        B_TURN = 4

        const_in = sem("const_in")
        const_set = sem("const_set")
        wo_in = [sem("wo_in0"), sem("wo_in1")]
        wo_rounded = sem("wo_rounded")
        wo_ready = sem("wo_ready")
        wb_in = [sem("wb_in0"), sem("wb_in1")]
        wb_rounded = sem("wb_rounded")
        wb_ready = sem("wb_ready")
        first_arrived = [sem(f"first_arrived{q}") for q in range(2 * TPB)]
        og_in = [sem("og_in0"), sem("og_in1")]
        sg_ready = sem("sg_ready")
        gated = sem("gated")
        u_ready = sem("u_ready")
        turned = sem("turned")
        uT_hi = sem("uT_hi")
        uT_lo = sem("uT_lo")
        l_arrived = [sem("l_arrived0"), sem("l_arrived1")]
        l_ready = sem("l_ready")
        pair_done = sem("pair_done")
        pair_free = sem("pair_free")
        parts_ready = sem("parts_ready")
        m_ready = sem("m_ready")
        m_hi = sem("m_hi")
        m_lo = sem("m_lo")
        x_arrived = sem("x_arrived")
        ss_ready = sem("ss_ready")
        std_ready = sem("std_ready")
        rstd_ready = sem("rstd_ready")
        y_scaled = sem("y_scaled")
        y_ready = sem("y_ready")
        stored = [sem("stored0"), sem("stored1")]

        PAIRS_PB = KD + TPB
        Q = 2 * TPB
        TURN_AFTER = (0, 2)
        EARLY = TPB + 2

        wa_v = w_branch_a.rearrange("(k p) n -> p k n", p=P)
        wb_v = w_branch_b.rearrange("(k p) n -> p k n", p=P)

        def is_first(blk):
            return isinstance(blk, int) and blk == 0

        with nc.Block() as block:

            @block.sync
            def _(sp):
                sp.dma_start(ident[:], ident_d).then_inc(const_in, 16)
                sp.dma_start(gain[:], g_post[0:1, :].to_broadcast([P, D])).then_inc(const_in, 16)

                def load_gated(blk, q, o_to, g_to, arrived):
                    br, t = q // TPB, q % TPB
                    sp.dma_start(o_to, (oA, oB)[br][ds(blk * TPB + t, 1)].rearrange("o p n -> (o p) n")).then_inc(arrived, 16)
                    sp.dma_start(g_to, gateTok[br, ds(blk * TPB + t, 1)].rearrange("o p n -> (o p) n")).then_inc(arrived, 16)

                def next_gated(blk, q):
                    sp.wait_ge(u_ready, blk * Q + (q + 1))
                    load_gated(blk, q, o_in[:, q % 2], g_in[:, q % 2], og_in[q % 2])

                def load_wb(m):
                    cols = slice(m * P, (m + 1) * P)
                    sp.dma_start(wb_raw[:, m % 2, 0], wa_v[:, :, cols]).then_inc(wb_in[m % 2], 16)
                    sp.dma_start(wb_raw[:, m % 2, 1], wb_v[:, :, cols]).then_inc(wb_in[m % 2], 16)

                def load_logits(blk, m):
                    for br in range(2):
                        sp.dma_start(l_in[:, m % 2, br], projT[T_ML + br * KD + m, :, ds(blk * BLK, BLK)])\
                          .then_inc(l_arrived[m % 2], 16)

                for s in stored:
                    sp.sem_inc(s, 16)
                for q in range(Q):
                    load_gated(0, q, first_in[:, q, 0], first_in[:, q, 1], first_arrived[q])
                    if q == TPB - 1:
                        load_wb(0)
                load_wb(1)
                for m in range(2):
                    load_logits(0, m)

                def block_io(blk, more):
                    for m in range(KD):
                        if more and m < EARLY:
                            next_gated(blk + 1, m)
                        if m < KD - 3 or more:
                            sp.wait_ge(wb_ready, blk * KD + (m + 2))
                            load_wb((m + 3) % KD)
                        if m < KD - 2 or more:
                            sp.wait_ge(parts_ready, blk * (2 * KD) + (2 * m + 2))
                            load_logits(blk + (m + 2) // KD, (m + 2) % KD)
                    for t in range(TPB):
                        sp.wait_ge(y_ready, blk * TPB + (t + 1))
                        sp.dma_start(result[ds(blk * BLK + t * P, P), :], y[:, t % 2]).then_inc(stored[t % 2], 16)
                        if t < TPB - 1 or more:
                            sp.dma_start(x_in[:], x[ds(blk * BLK + (t + 1) * P, P), :]).then_inc(x_arrived, 16)
                        if more and t == 0:
                            for q in range(EARLY, Q):
                                next_gated(blk + 1, q)

                sp.dma_start(x_in[:], x[0:P, :]).then_inc(x_arrived, 16)
                sp.wait_ge(wb_ready, 1)
                load_wb(2)
                with sp.Fori(0, NB - 1) as blk:
                    block_io(blk, True)
                block_io(NB - 1, False)
                for s in stored:
                    sp.wait_ge(s, 16 + 16 * TT // 2)

            @block.gpsimd
            def _(pool):
                pool.memset(eps[:], EPS).then_inc(const_set, 1)

                def split_weights(n, u):
                    pool.wait_ge(wb_rounded, n + 1)
                    pool.tensor_tensor(wb_lo[:, u], wb_raw[:, u], wb_hi[:, u].bitcast(F32), ALU.subtract).then_inc(wb_ready, 1)

                def load_w_out(k):
                    pool.dma_start(y[:, k % 2], w_out[k * P:(k + 1) * P, :]).then_inc(wo_in[k % 2], 16)

                for k in range(2):
                    load_w_out(k)
                split_weights(0, 0)
                split_weights(1, 1)
                for k in range(KD):
                    split_weights(k + 2, k % 2)
                    pool.wait_ge(wo_rounded, k + 1)
                    pool.tensor_tensor(wo_lo[:, k], y[:, k % 2], wo_hi[:, k].bitcast(F32), ALU.subtract).then_inc(wo_ready, 1)
                    if k < KD - 2:
                        pool.wait_ge(wo_ready, k + 1)
                        load_w_out(k + 2)
                with pool.Fori(KD // 2 + 1, NB * KD // 2) as i:
                    for u in range(2):
                        split_weights(i * 2 + u, u)

            @block.scalar
            def _(act):
                def sigmoid_of_gate(blk, q):
                    if is_first(blk):
                        act.wait_ge(first_arrived[q], 32)
                    else:
                        act.wait_ge(og_in[q % 2], blk * (16 * Q) + ((q // 2 + 1) * 32 - 16 * Q))
                    act.wait_ge(u_ready, blk * Q + (q + 1))
                    src = first_in[:, q, 1] if is_first(blk) else g_in[:, q % 2]
                    act.activation(sg[:, q % 2], src, ACT.Sigmoid).then_inc(sg_ready, 1)

                def round_weights(blk, m):
                    blk, m = blk + m // KD, m % KD
                    act.wait_ge(wb_in[m % 2], blk * (16 * KD) + (m // 2 + 1) * 32)
                    act.wait_ge(pair_done, blk * PAIRS_PB + (m + 5 if m >= 2 else m + 5 - TPB))
                    act.activation(wb_hi[:, m % 2], wb_raw[:, m % 2], ACT.Copy).then_inc(wb_rounded, 1)

                def round_uT(blk, br):
                    for k in range(KW):
                        act.wait_ge(turned, blk * (2 * KW) + (br * KW + k + 5))
                        if k == 0:
                            act.wait_ge(pair_done, blk * PAIRS_PB + (6 - TPB))
                        act.activation(uT[:, br, k, 0], bank[:, B_TURN + k], ACT.Copy).then_inc(uT_hi, 1)

                act.wait_ge(const_in, 32)
                act.wait_ge(const_set, 1)
                for q in range(Q):
                    sigmoid_of_gate(0, q)
                    if q % TPB == TPB - 1:
                        round_uT(0, q // TPB)
                        round_weights(0, q // TPB)

                def block_work(blk, more, first=False):
                    for m in range(KD):
                        act.wait_ge(l_arrived[m % 2], blk * (16 * KD) + (m // 2 + 1) * 32)
                        act.activation(l_in[:, m % 2], l_in[:, m % 2], ACT.Sigmoid).then_inc(l_ready, 1)
                        act.wait_ge(m_ready, blk * KD + (m + 1))
                        if m == 0:
                            act.wait_ge(pair_done, blk * PAIRS_PB + 6)
                        act.activation(mT[:, m, 0], part_a[:], ACT.Copy).then_inc(m_hi, 1)
                        if m < KD - 2 or more:
                            round_weights(blk, m + 2)
                        if more and m < EARLY:
                            sigmoid_of_gate(blk + 1, m)
                        if first:
                            act.wait_ge(wo_in[m % 2], 16 * (m // 2 + 1))
                            act.activation(wo_hi[:, m], y[:, m % 2], ACT.Copy).then_inc(wo_rounded, 1)
                    for t in range(TPB):
                        act.wait_ge(pair_done, blk * PAIRS_PB + (KD + t + 7))
                        slot = (KD + t) % 2
                        act.wait_ge(stored[t % 2], blk * 32 + (t // 2 + 1) * 16)
                        act.wait_ge(std_ready, blk * TPB + (t + 1))
                        act.activation(y[:, t % 2], bank[:, 2 * slot:2 * slot + 2].rearrange("p b n -> p (b n)"), ACT.Square,
                                       accum_out=ss[:, 0:1]).then_inc(ss_ready, 1)
                        act.wait_ge(ss_ready, blk * TPB + (t + 1))
                        act.wait_ge(rstd_ready, blk * TPB + (t + 1))
                        act.activation(std[:], ss[:, 0:1], ACT.Sqrt, bias=eps[:, 0:1], scale=1.0 / D).then_inc(std_ready, 1)
                        if more and t in TURN_AFTER:
                            round_uT(blk + 1, TURN_AFTER.index(t))
                        if more and t == 0:
                            for q in range(EARLY, Q):
                                sigmoid_of_gate(blk + 1, q)

                block_work(0, True, True)
                with act.Fori(1, NB - 1) as blk:
                    block_work(blk, True)
                block_work(NB - 1, False)

            @block.vector
            def _(dve):
                def gate(blk, q):
                    o_src, g_src = (first_in[:, q, 0], first_in[:, q, 1]) if is_first(blk) else (o_in[:, q % 2], g_in[:, q % 2])
                    dve.wait_ge(sg_ready, blk * Q + (q + 1))
                    dve.tensor_tensor(sg[:, q % 2], sg[:, q % 2], g_src, ALU.mult).then_inc(gated, 1)
                    if q % TPB == 0:
                        dve.wait_ge(turned, blk * (2 * KW) + (q // TPB * KW + 4))
                    dve.wait_ge(gated, blk * Q + (q + 1))
                    dve.tensor_tensor(u[:, q % TPB], sg[:, q % 2], o_src, ALU.mult).then_inc(u_ready, 1)

                def split_uT(blk, br):
                    for k in range(KW):
                        dve.wait_ge(uT_hi, blk * (2 * KW) + (br * KW + k + 1))
                        dve.tensor_tensor(uT[:, br, k, 1], bank[:, B_TURN + k], uT[:, br, k, 0].bitcast(F32), ALU.subtract)\
                           .then_inc(uT_lo, 1)

                dve.sem_inc(u_ready, 2)
                dve.sem_inc(rstd_ready, 1)
                dve.sem_inc(std_ready, 1)
                dve.wait_ge(const_in, 32)
                for q in range(Q):
                    gate(0, q)
                    if q % TPB == TPB - 1:
                        split_uT(0, q // TPB)

                def block_work(blk, more):
                    for m in range(KD):
                        dve.wait_ge(pair_done, blk * PAIRS_PB + (m + 7))
                        dve.wait_ge(l_ready, blk * KD + (m + 1))
                        slot = m % 2
                        dve.wait_ge(m_lo, blk * KD + (m + 1))
                        dve.tensor_tensor(part_a[:], bank[:, 2 * slot], l_in[:, slot, 0], ALU.mult).then_inc(parts_ready, 1)
                        dve.tensor_tensor(part_b[:], bank[:, 2 * slot + 1], l_in[:, slot, 1], ALU.mult).then_inc(parts_ready, 1)
                        dve.wait_ge(parts_ready, blk * (2 * KD) + (2 * m + 2))
                        dve.sem_inc(pair_free, 1)
                        dve.tensor_tensor(part_a[:], part_a[:], part_b[:], ALU.add).then_inc(m_ready, 1)
                        dve.wait_ge(m_hi, blk * KD + (m + 1))
                        dve.tensor_tensor(mT[:, m, 1], part_a[:], mT[:, m, 0].bitcast(F32), ALU.subtract).then_inc(m_lo, 1)
                        if more and m < TPB:
                            gate(blk + 1, m)
                    for t in range(TPB):
                        slot = (KD + t) % 2
                        dve.wait_ge(std_ready, blk * TPB + (t + 2))
                        dve.reciprocal(rstd[:], std[:]).then_inc(rstd_ready, 1)
                        dve.wait_ge(rstd_ready, blk * TPB + (t + 2))
                        dve.scalar_tensor_tensor(y[:, t % 2], bank[:, 2 * slot:2 * slot + 2].rearrange("p b n -> p (b n)"), rstd[:, 0:1],
                                                 gain[:], ALU.mult, ALU.mult).then_inc(y_scaled, 1)
                        dve.wait_ge(y_scaled, blk * TPB + (t + 1))
                        dve.sem_inc(pair_free, 1)
                        dve.wait_ge(x_arrived, blk * (16 * TPB) + (16 * t + 16))
                        dve.tensor_tensor(y[:, t % 2], y[:, t % 2], x_in[:], ALU.add).then_inc(y_ready, 1)
                        if more and t in TURN_AFTER:
                            split_uT(blk + 1, TURN_AFTER.index(t))
                        if more and t == 0:
                            for q in range(TPB, Q):
                                gate(blk + 1, q)

                dve.sem_inc(m_lo, 1)
                with dve.Fori(0, NB - 1) as blk:
                    block_work(blk, True)
                block_work(NB - 1, False)

            @block.tensor
            def _(pe):
                pe.wait_ge(const_in, 32)

                def turn_branch(blk, br):
                    pe.wait_ge(u_ready, blk * Q + (br * TPB + TPB + 2))
                    pe.wait_ge(uT_lo, blk * (2 * KW) + (br * KW + KW))
                    for k in range(KW):
                        for t in range(TPB):
                            last = pe.transpose(bank[:, B_TURN + k, t * P:(t + 1) * P], u[:, t, k * P:(k + 1) * P], ident[:])
                        last.then_inc(turned, 1)

                pe.sem_inc(turned, 4)
                pe.sem_inc(uT_lo, 4)
                pe.sem_inc(pair_done, 6)
                pe.sem_inc(pair_free, 2)
                turn_branch(0, 0)
                turn_branch(0, 1)

                def block_work(blk, more):
                    pe.wait_ge(uT_lo, blk * (2 * KW) + (2 * KW + 4))
                    for m in range(KD):
                        pe.wait_ge(wb_ready, blk * KD + (m + 1))
                        pe.wait_ge(pair_free, blk * PAIRS_PB + (m + 1))
                        slot = m % 2
                        for br in range(2):
                            for k in range(KW):
                                last = three_products(pe, bank[:, 2 * slot + br], (wb_hi[:, slot, br, k], wb_lo[:, slot, br, k]),
                                                      (uT[:, br, k, 0], uT[:, br, k, 1]), k == 0, k == KW - 1)
                        last.then_inc(pair_done, 1)
                    for t in range(TPB):
                        slot = (KD + t) % 2
                        rows = slice(t * P, (t + 1) * P)
                        pe.wait_ge(pair_free, blk * PAIRS_PB + (KD + t + 1))
                        for half in range(2):
                            cols = slice(half * BLK, (half + 1) * BLK)
                            for k in range(KD):
                                if t == 0 and half == 0:
                                    pe.wait_ge(m_lo, blk * KD + (k + 2))
                                    pe.wait_ge(wo_ready, k + 1)
                                last = three_products(pe, bank[:, 2 * slot + half], (mT[:, k, 0, rows], mT[:, k, 1, rows]),
                                                      (wo_hi[:, k, cols], wo_lo[:, k, cols]), k == 0, k == KD - 1)
                        last.then_inc(pair_done, 1)
                        if more and t in TURN_AFTER:
                            turn_branch(blk + 1, TURN_AFTER.index(t))

                with pe.Fori(0, NB - 1) as blk:
                    block_work(blk, True)
                block_work(NB - 1, False)
    clear_semaphores(nc, sems)


def hybrid_mla_hgrn2_gated_merge(nc, x, g_pre, w_in, b_gate, g_q, w_uq, g_kv, w_ukv, lb_logits, g_hgrn,
                                 w_branch_a, w_branch_b, w_out, g_post, ident, rope, causal, result):
    def scratch(name, *shape):
        return nc.dram_tensor(name, shape, F32).ap()

    projT = scratch("projT", N_FM, P, S)
    gateTok = scratch("gateTok", 2, TT, P, W)
    hgTok = scratch("hgTok", TT, P, 2 * W)
    qT = scratch("qT", HEADS, 2, QK, S)
    knT = scratch("knT", PAIRS, 2, P, S)
    kpT = scratch("kpT", 2, ROPE, S)
    vTok = scratch("vTok", HEADS, P, TT, P)
    oA = scratch("oA", TT, P, W)
    oB = scratch("oB", TT, P, W)

    with nc.sbuf_tensor("hT_hi", [P, KD, S], F32R) as hT_hi, nc.sbuf_tensor("hT_lo", [P, KD, S], F32R) as hT_lo:
        input_projection(nc, hT_hi, hT_lo, x, g_pre, w_in, ident, projT, gateTok, hgTok)
        merge_logits_and_recurrence(nc, hT_hi, hT_lo, w_in, b_gate, lb_logits, g_hgrn, ident, causal, projT, hgTok, oB)
    latent_projections(nc, projT, g_q, g_kv, w_uq, w_ukv, rope, ident, qT, knT, kpT, vTok)
    attention(nc, qT, knT, kpT, vTok, ident, oA)
    merge_and_output(nc, x, oA, oB, gateTok, projT, w_branch_a, w_branch_b, w_out, g_post, ident, result)


_INS = ['x', 'g_pre', 'w_in', 'b_gate', 'g_q', 'w_uq', 'g_kv', 'w_ukv', 'lb_logits', 'g_hgrn',
        'w_branch_a', 'w_branch_b', 'w_out', 'g_post']


def _rope_table():
    half = ROPE // 2
    inv = np.float32(ROPE_THETA) ** (-np.arange(0, ROPE, 2, dtype=np.float32) / np.float32(ROPE))
    angle = (np.arange(S, dtype=np.float32)[:, None] * inv[None, :]).T
    return np.concatenate([np.ones((NOPE, S)), np.cos(angle), np.cos(angle), -np.sin(angle), np.sin(angle)]).astype(np.float32)


def _causal_mask():
    t = np.arange(P)
    return ((t[:, None] // HG_BLOCK == t[None, :] // HG_BLOCK) & (t[None, :] >= t[:, None])).astype(np.int32)


def kernel(**inputs):
    import concourse.bacc as bacc
    from concourse.bass_utils import run_bass_kernel_spmd

    nc = bacc.Bacc("TRN2", target_bir_lowering=False, num_devices=1)
    data = {name: inputs[name] for name in _INS}
    data = {name: a.reshape(a.shape[-2:]) for name, a in data.items()}
    data["ident"] = np.eye(P, dtype=np.float32)
    data["rope"] = _rope_table()
    data["causal"] = _causal_mask()
    arrays, args = {}, []
    for name, a in data.items():
        arrays[f"in_{name}_dram"] = np.ascontiguousarray(a)
        args.append(nc.dram_tensor(f"in_{name}_dram", a.shape, mybir.dt.from_np(a.dtype), kind="ExternalInput").ap())
    args.append(nc.dram_tensor("out_0_dram", (S, D), F32, kind="ExternalOutput").ap())
    hybrid_mla_hgrn2_gated_merge(nc, *args)
    r = run_bass_kernel_spmd(nc, [arrays], core_ids=[0])
    return r.results[0]["out_0_dram"].reshape(1, S, D)
```
